# Optimizing a Trainium2 kernel written in Bass

```python
import math
import jax, jax.numpy as jnp
from jax import lax
import numpy as np

D_MODEL = 1024
BATCH = 1
SEQ = 512
DEPTH = 1
DEC_BATCH = 8
DEC_SEQ = 4
PAST_LEN = 4096
PAGE_SIZE = 128

CONF_DIM = D_MODEL // 2
CONF_KW = 31
SSM_DINNER = D_MODEL
SSM_HEADDIM = 64
SSM_HEADS = SSM_DINNER // SSM_HEADDIM
SSM_GROUPS = 2
SSM_DSTATE = 128
SSM_KW = 4
SSM_CHUNK = 128
SSM_CONV_DIM = SSM_DINNER + 2 * SSM_GROUPS * SSM_DSTATE
GMLP_DIM = D_MODEL // 2
GMLP_GROUPS = 4
GMLP_CHUNK = 128
D_FF = 2816
FFN_KW = 3
N_BRANCH = 3
EPS = 1e-6
IN_DIM = 2 * CONF_DIM + SSM_DINNER + SSM_CONV_DIM + SSM_HEADS + 2 * GMLP_DIM

kernel_name = "hybrid_conformer_ssd_gmlp_decoder_step"

def rmsnorm(x, g):
    xf = x.astype(jnp.float32)
    y = xf * lax.rsqrt(jnp.mean(xf * xf, axis=-1, keepdims=True) + EPS)
    return (y * g.astype(jnp.float32)).astype(x.dtype)

def layernorm(x, g, b):
    xf = x.astype(jnp.float32)
    mu = jnp.mean(xf, axis=-1, keepdims=True)
    var = jnp.mean(jnp.square(xf - mu), axis=-1, keepdims=True)
    y = (xf - mu) * lax.rsqrt(var + EPS)
    return (y * g.astype(jnp.float32) + b.astype(jnp.float32)).astype(x.dtype)

def causal_dwconv(hist, x, w, b):
    k = w.shape[0]
    xe = jnp.concatenate([hist.astype(x.dtype), x], axis=1)
    y = lax.conv_general_dilated(xe, w[:, None, :].astype(x.dtype), window_strides=(1,),
                                 padding='VALID', dimension_numbers=('NWC', 'WIO', 'NWC'),
                                 feature_group_count=x.shape[-1])
    return y + b.astype(x.dtype), xe[:, xe.shape[1] - (k - 1):]

def ssd(x, dt, a_neg, bm, cm, h0):
    f32 = jnp.float32
    n, t, h, p = x.shape
    g, s = bm.shape[2], bm.shape[3]
    r = h // g
    lc = min(SSM_CHUNK, t)
    tp = -(-t // lc) * lc
    pad = tp - t
    if pad:
        padf = lambda a: jnp.pad(a, [(0, 0), (0, pad)] + [(0, 0)] * (a.ndim - 2))
        x, dt, bm, cm = padf(x), padf(dt), padf(bm), padf(cm)
    nc = tp // lc
    xr = x.astype(f32).reshape(n, nc, lc, g, r, p)
    dtr = dt.astype(f32).reshape(n, nc, lc, g, r)
    br = bm.astype(f32).reshape(n, nc, lc, g, s)
    cr = cm.astype(f32).reshape(n, nc, lc, g, s)
    a_cs = jnp.cumsum(dtr * a_neg.astype(f32).reshape(g, r), axis=2)
    xdt = xr * dtr[..., None]
    a_t = jnp.moveaxis(a_cs, 2, -1)
    causal = jnp.tril(jnp.ones((lc, lc), dtype=bool))
    decay = jnp.exp(jnp.where(causal, a_t[..., :, None] - a_t[..., None, :], -jnp.inf))
    cb = jnp.einsum('bcign,bcjgn->bcgij', cr, br)
    mix = cb[:, :, :, None] * decay
    y_diag = jnp.einsum('bcgrij,bcjgrp->bcigrp', mix, xdt)
    to_end = jnp.exp(a_cs[:, :, -1:] - a_cs)
    chunk_states = jnp.einsum('bclgn,bclgr,bclgrp->bcgrpn', br, to_end, xdt)
    chunk_decay = jnp.exp(a_cs[:, :, -1])

    def step(hc, inp):
        dec, st = inp
        return dec[..., None, None] * hc + st, hc

    h_init = h0.astype(f32).reshape(n, g, r, p, s)
    h_last, h_in = lax.scan(step, h_init, (jnp.moveaxis(chunk_decay, 1, 0), jnp.moveaxis(chunk_states, 1, 0)))
    h_in = jnp.moveaxis(h_in, 0, 1)
    y_off = jnp.einsum('bclgn,bcgrpn,bclgr->bclgrp', cr, h_in, jnp.exp(a_cs))
    y = (y_diag + y_off).reshape(n, tp, h, p)[:, :t]
    return y, h_last.reshape(n, h, p, s)

def chunk_spatial(v, w_s, b_s):
    n, t, dv = v.shape
    cg = dv // GMLP_GROUPS
    tp = -(-t // GMLP_CHUNK) * GMLP_CHUNK
    vp = jnp.pad(v, ((0, 0), (0, tp - t), (0, 0))).reshape(n, tp // GMLP_CHUNK, GMLP_CHUNK, GMLP_GROUPS, cg)
    w = jnp.where(jnp.tril(jnp.ones((GMLP_CHUNK, GMLP_CHUNK), dtype=bool)), w_s, 0)
    sm = jnp.einsum('gts,bksgc->bktgc', w, vp) + b_s.T[:, :, None]
    return sm.reshape(n, tp, dv)[:, :t].astype(v.dtype)

def layer(x, hist_a, h_ssm, hist_ssm, hist_ffn, lp):
    (norm1_g, w_in, w_gate, b_gate, conf_conv_w, conf_conv_b, conf_ln_g, conf_ln_b, conf_w_out,
     ssm_conv_w, ssm_conv_b, ssm_dt_bias, ssm_a_log, ssm_d, ssm_norm_g, ssm_w_out,
     gmlp_ln_g, gmlp_ln_b, gmlp_w_s, gmlp_b_s, gmlp_w_out, w_o,
     norm2_g, ffn_w_up, ffn_conv_w, ffn_conv_b, ffn_w_down) = lp
    n, t, _ = x.shape
    f32 = jnp.float32
    h = rmsnorm(x, norm1_g)
    proj = h @ w_in
    o1 = CONF_DIM
    o2 = o1 + CONF_DIM
    o3 = o2 + SSM_DINNER
    o4 = o3 + SSM_CONV_DIM
    o5 = o4 + SSM_HEADS
    o6 = o5 + GMLP_DIM
    a1, a2, z, xbc, dt_raw, u, v = jnp.split(proj, [o1, o2, o3, o4, o5, o6], axis=-1)
    ga = a1 * jax.nn.sigmoid(a2)
    ca, new_hist_a = causal_dwconv(hist_a, ga, conf_conv_w, conf_conv_b)
    y_a = jax.nn.silu(layernorm(ca, conf_ln_g, conf_ln_b)) @ conf_w_out
    xbc_c, new_hist_ssm = causal_dwconv(hist_ssm, xbc, ssm_conv_w, ssm_conv_b)
    xbc_c = jax.nn.silu(xbc_c)
    xs_, b_, c_ = jnp.split(xbc_c, [SSM_DINNER, SSM_DINNER + SSM_GROUPS * SSM_DSTATE], axis=-1)
    dt = jax.nn.softplus(dt_raw.astype(f32) + ssm_dt_bias.astype(f32))
    a_neg = -jnp.exp(ssm_a_log.astype(f32))
    xh = xs_.reshape(n, t, SSM_HEADS, SSM_HEADDIM)
    y_ssd, new_h = ssd(xh, dt, a_neg,
                       b_.reshape(n, t, SSM_GROUPS, SSM_DSTATE),
                       c_.reshape(n, t, SSM_GROUPS, SSM_DSTATE), h_ssm)
    y_ssd = (y_ssd + ssm_d.astype(f32)[:, None] * xh.astype(f32)).reshape(n, t, SSM_DINNER).astype(x.dtype)
    y_b = rmsnorm(y_ssd * jax.nn.silu(z), ssm_norm_g) @ ssm_w_out
    u = jax.nn.gelu(u)
    vn = layernorm(jax.nn.gelu(v), gmlp_ln_g, gmlp_ln_b)
    y_c = (u * chunk_spatial(vn, gmlp_w_s, gmlp_b_s)) @ gmlp_w_out
    gates = jax.nn.sigmoid(h @ w_gate + b_gate).reshape(n, t, N_BRANCH, D_MODEL)
    mixed = gates[:, :, 0] * y_a + gates[:, :, 1] * y_b + gates[:, :, 2] * y_c
    x = x + mixed @ w_o
    h2 = rmsnorm(x, norm2_g)
    up = h2 @ ffn_w_up
    ag, av = up[..., :D_FF], up[..., D_FF:]
    agc, new_hist_ffn = causal_dwconv(hist_ffn, ag, ffn_conv_w, ffn_conv_b)
    x = x + (jax.nn.silu(agc) * av) @ ffn_w_down
    return x, new_hist_a, new_h, new_hist_ssm, new_hist_ffn, vn

def setup_inputs(seed: int = 0) -> dict:
    key = jax.random.key(seed)
    ks = iter(jax.random.split(key, 48))
    f32 = jnp.float32
    L = DEPTH

    def nrm(shape, scale):
        return jax.random.normal(next(ks), shape, f32) * scale

    def gain(shape):
        return 1.0 + 0.1 * jax.random.normal(next(ks), shape, f32)

    dt0 = jnp.exp(jax.random.uniform(next(ks), (L, SSM_HEADS), f32, math.log(1e-3), math.log(1e-1)))
    dt_bias = dt0 + jnp.log(-jnp.expm1(-dt0))
    a_log = jnp.log(jax.random.uniform(next(ks), (L, SSM_HEADS), f32, 1.0, 16.0))
    return {
        "x_prompt": nrm((BATCH, SEQ, D_MODEL), 1.0),
        "x_sample": nrm((DEC_BATCH, DEC_SEQ, D_MODEL), 1.0),
        "state_conv_a": nrm((L, DEC_BATCH, CONF_KW - 1, CONF_DIM), 0.5),
        "state_ssm": nrm((L, DEC_BATCH, SSM_HEADS, SSM_HEADDIM, SSM_DSTATE), 0.5),
        "state_conv_ssm": nrm((L, DEC_BATCH, SSM_KW - 1, SSM_CONV_DIM), 1.0),
        "state_conv_ffn": nrm((L, DEC_BATCH, FFN_KW - 1, D_FF), 1.0),
        "norm1_g": gain((L, D_MODEL)),
        "w_in": nrm((L, D_MODEL, IN_DIM), D_MODEL ** -0.5),
        "w_gate": nrm((L, D_MODEL, N_BRANCH * D_MODEL), D_MODEL ** -0.5),
        "b_gate": nrm((L, N_BRANCH * D_MODEL), 0.02),
        "conf_conv_w": nrm((L, CONF_KW, CONF_DIM), CONF_KW ** -0.5),
        "conf_conv_b": nrm((L, CONF_DIM), 0.02),
        "conf_ln_g": gain((L, CONF_DIM)),
        "conf_ln_b": nrm((L, CONF_DIM), 0.02),
        "conf_w_out": nrm((L, CONF_DIM, D_MODEL), CONF_DIM ** -0.5),
        "ssm_conv_w": nrm((L, SSM_KW, SSM_CONV_DIM), SSM_KW ** -0.5),
        "ssm_conv_b": nrm((L, SSM_CONV_DIM), 0.02),
        "ssm_dt_bias": dt_bias,
        "ssm_a_log": a_log,
        "ssm_d": gain((L, SSM_HEADS)),
        "ssm_norm_g": gain((L, SSM_DINNER)),
        "ssm_w_out": nrm((L, SSM_DINNER, D_MODEL), SSM_DINNER ** -0.5),
        "gmlp_ln_g": gain((L, GMLP_DIM)),
        "gmlp_ln_b": nrm((L, GMLP_DIM), 0.02),
        "gmlp_w_s": nrm((L, GMLP_GROUPS, GMLP_CHUNK, GMLP_CHUNK), GMLP_CHUNK ** -0.5),
        "gmlp_b_s": gain((L, GMLP_GROUPS, GMLP_CHUNK)),
        "gmlp_w_out": nrm((L, GMLP_DIM, D_MODEL), GMLP_DIM ** -0.5),
        "w_o": nrm((L, D_MODEL, D_MODEL), D_MODEL ** -0.5),
        "norm2_g": gain((L, D_MODEL)),
        "ffn_w_up": nrm((L, D_MODEL, 2 * D_FF), D_MODEL ** -0.5),
        "ffn_conv_w": nrm((L, FFN_KW, D_FF), FFN_KW ** -0.5),
        "ffn_conv_b": nrm((L, D_FF), 0.02),
        "ffn_w_down": nrm((L, D_FF, D_MODEL), D_FF ** -0.5),
        "final_norm_g": gain((D_MODEL,)),
    }

def reference(x_prompt, x_sample, state_conv_a, state_ssm, state_conv_ssm, state_conv_ffn,
              norm1_g, w_in, w_gate, b_gate, conf_conv_w, conf_conv_b, conf_ln_g, conf_ln_b, conf_w_out,
              ssm_conv_w, ssm_conv_b, ssm_dt_bias, ssm_a_log, ssm_d, ssm_norm_g, ssm_w_out,
              gmlp_ln_g, gmlp_ln_b, gmlp_w_s, gmlp_b_s, gmlp_w_out, w_o,
              norm2_g, ffn_w_up, ffn_conv_w, ffn_conv_b, ffn_w_down, final_norm_g):
    xp, xs = x_prompt, x_sample
    nb = xp.shape[0]
    stacked = (norm1_g, w_in, w_gate, b_gate, conf_conv_w, conf_conv_b, conf_ln_g, conf_ln_b, conf_w_out,
               ssm_conv_w, ssm_conv_b, ssm_dt_bias, ssm_a_log, ssm_d, ssm_norm_g, ssm_w_out,
               gmlp_ln_g, gmlp_ln_b, gmlp_w_s, gmlp_b_s, gmlp_w_out, w_o,
               norm2_g, ffn_w_up, ffn_conv_w, ffn_conv_b, ffn_w_down)
    pa, ph, pc, pf = [], [], [], []
    sa, sh, sc, sf, sv = [], [], [], [], []
    for l in range(DEPTH):
        lp = tuple(a[l] for a in stacked)
        xp, na, nh, nc, nf, _ = layer(
            xp,
            jnp.zeros((nb, CONF_KW - 1, CONF_DIM), xp.dtype),
            jnp.zeros((nb, SSM_HEADS, SSM_HEADDIM, SSM_DSTATE), jnp.float32),
            jnp.zeros((nb, SSM_KW - 1, SSM_CONV_DIM), xp.dtype),
            jnp.zeros((nb, FFN_KW - 1, D_FF), xp.dtype),
            lp)
        pa.append(na); ph.append(nh); pc.append(nc); pf.append(nf)
        xs, na, nh, nc, nf, nv = layer(xs, state_conv_a[l], state_ssm[l], state_conv_ssm[l], state_conv_ffn[l], lp)
        sa.append(na); sh.append(nh); sc.append(nc); sf.append(nf); sv.append(nv)
    y_prompt = rmsnorm(xp, final_norm_g)
    y_sample = rmsnorm(xs, final_norm_g)
    new_conv_a_p = jnp.stack(pa)
    new_ssm_p = jnp.stack(ph)
    new_conv_ssm_p = jnp.stack(pc)
    new_conv_ffn_p = jnp.stack(pf)
    new_conv_a_s = jnp.stack(sa)
    new_ssm_s = jnp.stack(sh)
    new_conv_ssm_s = jnp.stack(sc)
    new_conv_ffn_s = jnp.stack(sf)
    new_gmlp_v_s = jnp.stack(sv)
    return (y_prompt, y_sample, new_conv_a_p, new_ssm_p, new_conv_ssm_p, new_conv_ffn_p,
            new_conv_a_s, new_ssm_s, new_conv_ssm_s, new_conv_ffn_s, new_gmlp_v_s)


_drawn_inputs = setup_inputs


def setup_inputs(seed=0):
    import zlib

    import numpy as np

    out = dict(_drawn_inputs(seed))
    spreads = {}
    factors = {'b_gate': 8.0,
     'conf_conv_b': 5.092,
     'conf_ln_b': 8.0,
     'gmlp_ln_b': 2.865,
     'ffn_conv_b': 6.476}
    for name, (base, spread) in spreads.items():
        noise = np.random.default_rng([zlib.crc32(name.encode()), seed]).standard_normal(out[name].shape)
        drawn = base * np.exp(spread * noise) if base else spread * noise
        out[name] = __import__('jax').numpy.asarray(drawn.astype(out[name].dtype))
    for name, factor in factors.items():
        out[name] = (out[name] * factor).astype(out[name].dtype)
    return out
```

```python
from contextlib import ExitStack

import numpy as np
import concourse.bass as bass
from concourse import mybir

F32 = mybir.dt.float32
F32R = mybir.dt.float32r
ACT = mybir.ActivationFunctionType
ALU = mybir.AluOpType

P = 128
D, SEQ, NB, TS = 1024, 512, 8, 4
SMP = NB * TS
TOK = SEQ + SMP
HALF = TOK // 2
KD = D // P
CONF, CKW = 512, 31
HEADS, HD, STATE, SKW, XBC = 16, 64, 128, 4, 1536
FF, FKW = 2816, 3
NF = FF // P
FFA = 12
FFB = NF - FFA
CH = 128
NCH = SEQ // CH
EPS = 1e-6
SLOTS = 4
ELEM = KD * P

PHASES = [
    ("A", 2, (8, 8, 8, 8), 1),
    ("VU", 2, (8, 8, 8, 8), 1),
    ("X", 3, (8, 8, 8, 8), 1),
    ("G2", 4, (8, 4, 8, 4), 1),
    ("G0", 4, (8, 4, 8, 4), 1),
    ("Z", 2, (8, 8, 8, 8), 1),
    ("G1", 4, (8, 8, 8, 8), 1),
    ("WO", 2, (8, 8, 8, 8), 1),
    ("U1", 6, (8, 8, 8, 8), 1),
    ("D1", 4, (6, 6, 6, 6), 2),
    ("U2", 5, (8, 8, 8, 8), 1),
    ("D2", 4, (5, 5, 5, 5), 2),
]


class Phase:
    def __init__(self, name, quads, kb, per_block, quad0, pair0):
        self.name, self.quads, self.kb, self.per_block = name, quads, kb, per_block
        self.quad0, self.pair0 = quad0, pair0
        self.pairs_per_quad = 2 // per_block

    def pair(self, i, s):
        if self.per_block == 2:
            return i + self.pair0
        return i * 2 + (self.pair0 + s // 2)

    def acc(self, s):
        return s // 2 if self.per_block == 2 else s % 2


def phases():
    out, q, p = {}, 0, 0
    for name, quads, kb, per_block in PHASES:
        out[name] = Phase(name, quads, kb, per_block, q, p)
        q += quads
        p += quads * (2 // per_block)
    return out


PARAM_BLOCKS = [("norm1_g", KD), ("b_gate", 3 * KD), ("conf_w", 4 * CKW), ("conf_b", 4), ("conf_ln_g", 4),
                ("conf_ln_b", 4), ("ssm_w", 12 * SKW), ("ssm_b", 12), ("ssm_g", KD), ("ssm_d", KD),
                ("gmlp_ln_g", 4), ("gmlp_ln_b", 4), ("norm2_g", KD), ("ffn_w", NF * FKW), ("ffn_b", NF),
                ("final_g", KD)]
PARAM_AT, _n = {}, 0
for _name, _k in PARAM_BLOCKS:
    PARAM_AT[_name] = _n
    _n += _k
N_PARAM = _n


def line(k):
    return k - 1 + SEQ + NB * (k - 1 + TS)


def loop(e, lo, hi, body):
    if hi - lo == 1:
        body(lo)
    elif hi > lo:
        with e.Fori(lo, hi) as i:
            body(i)


def wait(e, sem, value):
    if isinstance(value, int) and value <= 0:
        return
    e.wait_ge(sem, value)


def pick(t, j):
    if isinstance(j, int):
        return t[:, j]
    v = t[:, bass.ds(j, 1)]
    names = "abcdef"[:len(v.shape) - 2]
    return v.rearrange(f"p o {' '.join(names)} -> p (o {names[0]}) {' '.join(names[1:])}")


def build(nc, ins, outs):
    ph = phases()
    order = [x[0] for x in PHASES]
    with ExitStack() as ctx:
        def sb(name, shape, dt=F32):
            return ctx.enter_context(nc.sbuf_tensor(name, shape, dt))

        sems = {}

        def sem(name):
            if name not in sems:
                sems[name] = ctx.enter_context(nc.semaphore(name))
            return sems[name]

        h_split = sb("h_split", [P, KD, 2, TOK], F32R)
        w_split = sb("w_split", [P, SLOTS, 2, ELEM], F32R)
        w_raw = sb("w_raw", [P, SLOTS, ELEM])
        params = sb("params", [P, N_PARAM])
        consts = sb("consts", [P, 3, P])
        mask_s = sb("mask_s", [SMP, 2, SMP])
        xbc = sb("xbc", [P, 12, TOK])
        u_sb = sb("u_sb", [P, 4, TOK])
        mixed = sb("mixed", [P, KD, TOK])
        ca = sb("ca", [P, 4, TOK])
        temps = sb("temps", [P, 6, 576])
        small = sb("small", [P, 12, 5 * HEADS])
        a_rows = sb("a_rows", [HEADS, TOK])
        bias_rows = sb("bias_rows", [P, 2, HEADS])
        w_dt = sb("w_dt", [P, KD, HEADS])
        w_dt_split = sb("w_dt_split", [P, 2, KD, HEADS], F32R)
        eps = sb("eps", [P, 1])
        hist_x = sb("hist_x", [P, 12, NB, SKW - 1])
        hist_f = sb("hist_f", [P, NF, NB, FKW - 1])
        tail_x = sb("tail_x", [P, 12, (NB + 1) * (SKW - 1)])
        tail_f = sb("tail_f", [P, NF, (NB + 1) * (FKW - 1)])
        with ExitStack() as early:
            part0, part1, part2 = (early.enter_context(nc.sbuf_tensor(f"part{n}", [P, 8 * TOK], F32))
                                   for n in range(3))
        branch = sb("branch", [P, 24, TOK], F32R)

        def carve(tensor, *shapes):
            out, o = [], 0
            for parts, *dims in shapes:
                n = int(np.prod(dims))
                v = tensor[0:parts, o:o + n]
                if len(dims) == 2:
                    v = v.rearrange("p (a b) -> p a b", a=dims[0])
                out.append(v)
                o += n
            assert o <= tensor.shape[1]
            return out

        u_flat = u_sb[:, :, :].rearrange("p j n -> p (j n)")
        ca_flat = ca[:, :, :].rearrange("p j n -> p (j n)")
        v_sb = mixed[:, 0:4]
        (line_a,) = carve(part1, (P, 4, line(CKW)))
        vnat, ws_t, bs, ws_s = carve(part2, (P, 5, CONF), (P, 4, CH), (P, 4, CH), (SMP, 4, SMP))
        (h_chunk,) = carve(part0, (P, NCH, D))
        (xdt,) = carve(part2, (P, NCH, D))
        bnat, cbm = carve(ca_flat, (P, NCH, 2 * STATE), (P, 2, SEQ))
        (xw,) = carve(u_flat, (P, 2, D))
        (h0,) = carve(u_flat, (P, 2, D))
        bnat_s, bm_s, xdt_s, xw_s, cbm_s = carve(part1, (SMP, 2 * STATE), (SMP, 2, 2 * STATE), (SMP, D), (SMP, D),
                                                 (SMP, 2, SMP))
        ident, tri, ones = consts[:, 0], consts[:, 1], consts[:, 2]
        X_DT, ABS, EXPN, RATIO, RATIO2, POLY, TO_END, DT, ADT, A_CUM, TOTAL, DECAY = range(12)

        def param(name, j):
            if isinstance(j, int):
                return params[:, PARAM_AT[name] + j:PARAM_AT[name] + j + 1]
            return params[:, bass.ds(j + PARAM_AT[name], 1)]

        def T(r, n=TOK):
            return temps[:, r, 0:n]

        accs = ctx.enter_context(nc.psum_tensor("accs", [P, 2, 2, 512], F32))
        misc = ctx.enter_context(nc.psum_tensor("misc", [P, 4, 512], F32))
        stat = misc[:, 0:2, 0:HALF]

        def acc(a):
            return accs[:, a, :, 0:HALF]

        def halves(ap):
            return ap.rearrange("p (h n) -> p h n", h=2)

        def acc_pieces(a):
            return [accs[:, a, 0, 0:HALF], accs[:, a, 1, 0:SEQ - HALF],
                    accs[:, a, 1, SEQ - HALF:HALF].rearrange("p (b t) -> p b t", b=NB)]

        def samples(ln, start, k):
            return ln[:, start:start + NB * (k - 1 + TS)].rearrange("p (b t) -> p b t", b=NB)

        def line_pieces(ln, k):
            return [ln[:, k - 1:k - 1 + HALF], ln[:, k - 1 + HALF:k - 1 + SEQ],
                    samples(ln, k - 1 + SEQ, k)[:, :, k - 1:]]

        def conv_pieces(cv, k):
            return [cv[:, 0:HALF], cv[:, HALF:SEQ], samples(cv, SEQ, k)[:, :, k - 1:]]

        w_landed = [sem(f"w_landed{s}") for s in range(SLOTS)]
        w_hi = [sem(f"w_hi{s}") for s in range(SLOTS)]
        w_lo = [sem(f"w_lo{s}") for s in range(SLOTS)]
        acc_full = [sem(f"acc_full{a}") for a in range(2)]
        acc_free = [sem(f"acc_free{a}") for a in range(2)]

        block = ctx.enter_context(nc.Block())

        def w_src(name, i, s):
            if name in ("A", "VU", "X"):
                return ins["w_in_main"], i * 4 + ({"A": 0, "VU": 8, "X": 16}[name] + s)
            if name == "Z":
                return ins["w_in_z"], i * 4 + s
            if name in ("G0", "G1", "G2"):
                g = int(name[1])
                if s % 2 == 0:
                    return ins["w_gate"], i * 2 + (g * KD + s // 2)
                return ins[("conf_w_out", "ssm_w_out", "gmlp_w_out")[g]], i * 2 + s // 2
            if name == "WO":
                return ins["w_o"], i * 4 + s
            if name in ("U1", "U2"):
                return ins["ffn_w_up"], i * 4 + ((0 if name == "U1" else 2 * FFA) + s)
            return ins["ffn_w_down1" if name == "D1" else "ffn_w_down2"], i * 4 + s

        def load_quad(sp, p, i):
            for s in range(SLOTS):
                src, j = w_src(p.name, i, s)
                n = p.kb[s] * P
                wait(sp, w_lo[s], i + p.quad0)
                ap = src[j] if isinstance(j, int) else src[bass.ds(j, 1)].rearrange("o p n -> (o p) n")
                sp.dma_start(w_raw[:, s, 0:n], ap).then_inc(w_landed[s], 16)

        def load_phase(sp, name, first=0):
            p = ph[name]
            loop(sp, first, p.quads, lambda i: load_quad(sp, p, i))

        def split_hi(act, p, i, s):
            n = p.kb[s] * P
            act.wait_ge(w_landed[s], i * 16 + (p.quad0 + 1) * 16)
            act.activation(w_split[:, s, 0, 0:n], w_raw[:, s, 0:n], ACT.Copy).then_inc(w_hi[s], 1)

        def split_lo(pool, p, i, s):
            n = p.kb[s] * P
            pool.wait_ge(w_hi[s], i + (p.quad0 + 1))
            pool.tensor_tensor(w_split[:, s, 1, 0:n], w_raw[:, s, 0:n], w_split[:, s, 0, 0:n].bitcast(F32),
                               ALU.subtract).then_inc(w_lo[s], 1)

        def act_quad(act, p, i, ahead, evac):
            for s in range(p.per_block - 1, SLOTS, p.per_block):
                a = p.acc(s)
                act.wait_ge(acc_full[a], p.pair(i, s) + 1)
                evac(i, s)
                if ahead is not None:
                    for r in range(s + 1 - p.per_block, s + 1):
                        split_hi(act, ahead[0], ahead[1], r)

        def after(p):
            at = order.index(p.name)
            return (ph[order[at + 1]], 0) if at + 1 < len(order) else None

        def act_phase(act, name, evac, unroll=False):
            p = ph[name]
            if unroll:
                for i in range(p.quads - 1):
                    act_quad(act, p, i, (p, i + 1), evac)
            else:
                loop(act, 0, p.quads - 1, lambda i: act_quad(act, p, i, (p, i + 1), evac))
            act_quad(act, p, p.quads - 1, after(p), evac)

        def pe_quad(pe, p, i, rhs):
            for s in range(SLOTS):
                a = p.acc(s)
                first, last = s % p.per_block == 0, s % p.per_block == p.per_block - 1
                pe.wait_ge(w_lo[s], i + (p.quad0 + 1))
                if first:
                    wait(pe, acc_free[a], p.pair(i, s))
                for k in range(p.kb[s]):
                    for n, (wp, xp) in enumerate(((0, 0), (0, 1), (1, 0))):
                        for half in range(2):
                            mm = pe.matmul(accs[:, a, half, 0:HALF], w_split[:, s, wp, k * P:(k + 1) * P],
                                           rhs(s, k, xp, half), start=(first and k == 0 and n == 0),
                                           stop=(last and k == p.kb[s] - 1 and n == 2))
                if last:
                    mm.then_inc(acc_full[a], 1)

        def pe_phase(pe, name, rhs, first=0):
            p = ph[name]
            loop(pe, first, p.quads, lambda i: pe_quad(pe, p, i, rhs))

        def tokens(half):
            return slice(half * HALF, (half + 1) * HALF)

        def h_rhs(s, k, part, half):
            return h_split[:, k, part, tokens(half)]

        def gmlp_at(k):
            return k, 4 + k

        def conf_at(k):
            return 8 + k, 12 + k

        def ssm_at(k):
            return 16 + k, k

        def mixed_at(k):
            return (8 + k, 12 + k) if k < 4 else (k - 4, k)

        def branch_rhs(at):
            return lambda s, k, part, half: branch[:, at(k)[part], tokens(half)]

        def merge_rhs(at):
            return lambda s, k, part, half: (h_rhs if s % 2 == 0 else branch_rhs(at))(s, k, part, half)

        def down_rhs(kb):
            return lambda s, k, part, half: branch[:, 12 * part + kb * (s % 2) + k, tokens(half)]

        @block.sync
        def _(sp):
            for j in range(KD):
                sp.dma_start(xbc[:, j], ins["x"][:, j]).then_inc(sem(f"x_landed{j}"), 16)
                if j == 3:
                    sp.dma_start(consts[:, :, :], ins["consts"]).then_inc(sem("consts_landed"), 16)
                    sp.dma_start(params[:, :], ins["params"]).then_inc(sem("params_landed"), 16)
            load_quad(sp, ph["A"], 0)
            for j in range(4):
                sp.dma_start(samples(line_a[:, j], CKW - 1 + SEQ, CKW)[:, :, 0:CKW - 1],
                             ins["state_conv_a"][:, j]).then_inc(sem("hist_a_landed"), 16)
            sp.dma_start(hist_x[:, :, :, :], ins["state_conv_ssm"]).then_inc(sem("hist_landed"), 16)
            sp.dma_start(hist_f[:, :, :, :], ins["state_conv_ffn"]).then_inc(sem("hist_landed"), 16)
            sp.dma_start(mask_s[:, :, :], ins["mask_s"]).then_inc(sem("small_landed"), 16)
            sp.dma_start(w_dt[:, :, :], ins["w_dt"]).then_inc(sem("small_landed"), 16)
            sp.dma_start(bias_rows[:, 0], ins["ssm_dt_bias"].partition_broadcast(P)).then_inc(sem("small_landed"), 16)
            sp.dma_start(bias_rows[:, 1], ins["ssm_a_log"].partition_broadcast(P)).then_inc(sem("small_landed"), 16)
            load_quad(sp, ph["A"], 1)
            sp.dma_start(ws_t, ins["gmlp_w_s"]).then_inc(sem("gmlp_landed"), 16)
            sp.dma_start(bs.rearrange("p g n -> p (g n)"), ins["gmlp_b_s"].partition_broadcast(P))\
                .then_inc(sem("gmlp_landed"), 16)
            for b in range(NB):
                for g in range(4):
                    sp.dma_start(ws_s[TS * b:TS * b + TS, g].rearrange("p (b t) -> p b t", b=NB),
                                 ins["gmlp_w_s"][0:TS, g, 0:TS].unsqueeze(1).to_broadcast([TS, NB, TS]))\
                        .then_inc(sem("gmlp_landed"), 16)
            load_phase(sp, "VU")
            load_phase(sp, "X")
            sp.wait_ge(acc_free[1], 4)
            for j in range(4):
                sp.dma_start(outs["conv_a_p"][:, j], line_a[:, j, SEQ:SEQ + CKW - 1]).then_inc(sem("stored_a"), 16)
                sp.dma_start(outs["conv_a_s"][:, j], samples(line_a[:, j], CKW - 1 + SEQ, CKW)[:, :, TS:])\
                    .then_inc(sem("stored_a"), 16)
            load_quad(sp, ph["G2"], 0)
            sp.wait_ge(sem("vn_done"), 4)
            sp.dma_start(outs["gmlp_v_s"], v_sb[:, :, SEQ:TOK]).then_inc(sem("stored_v"), 16)
            load_phase(sp, "G2", first=1)
            sp.wait_ge(sem("tail_x"), 24)
            sp.dma_start(outs["conv_ssm"], tail_x[:, :, :]).then_inc(sem("stored_tails"), 16)
            load_phase(sp, "G0")
            load_phase(sp, "Z")
            sp.wait_ge(sem("chunk_sum"), 2 * NCH)
            for b in range(NB):
                r = b % 2
                if b >= 2:
                    sp.wait_ge(sem(f"h0_stored{r}"), 16 * (b // 2))
                sp.dma_start(h0[:, r], ins["state_ssm"][b]).then_inc(sem(f"h0_landed{r}"), 16)
                if b >= 1:
                    sp.wait_ge(sem("h0_new"), 2 * b)
                    sp.dma_start(outs["ssm_s"][b - 1], h0[:, 1 - r]).then_inc(sem(f"h0_stored{1 - r}"), 16)
            sp.wait_ge(sem("h0_new"), 2 * NB)
            sp.dma_start(outs["ssm_s"][NB - 1], h0[:, 1]).then_inc(sem("h0_stored1"), 16)
            sp.wait_ge(sem("chunk_state"), 2 * NCH)
            sp.dma_start(outs["ssm_p"], h_chunk[:, NCH - 1]).then_inc(sem("stored_h"), 16)
            load_phase(sp, "G1")
            for j in range(KD):
                sp.wait_ge(sem("ssm_f32"), j + 1)
                sp.dma_start(xbc[:, j], ins["x"][:, j]).then_inc(sem(f"x_landed{j}"), 16)
            for name in ("WO", "U1", "D1", "U2", "D2"):
                load_phase(sp, name)
            sp.wait_ge(sem("tail_f"), 2 * NF)
            sp.dma_start(outs["conv_ffn"], tail_f[:, :, :]).then_inc(sem("stored_tails"), 16)
            for j in range(KD):
                sp.wait_ge(sem("y_done"), j + 1)
                sp.dma_start(outs["y"][:, j], xbc[:, j]).then_inc(sem("stored_y"), 16)
            sp.wait_ge(sem("stored_a"), 16 * 8)
            sp.wait_ge(sem("stored_v"), 16)
            sp.wait_ge(sem("stored_tails"), 32)
            sp.wait_ge(sem("stored_h"), 16)
            sp.wait_ge(sem("h0_stored0"), 16 * NB // 2)
            sp.wait_ge(sem("h0_stored1"), 16 * NB // 2)
            sp.wait_ge(sem("stored_y"), 16 * KD)

        @block.gpsimd
        def _(pool):
            def pool_phase(name, work):
                p = ph[name]

                def quad(i, ahead):
                    for r in range(2):
                        work(i, r)
                        if ahead is not None:
                            split_lo(pool, ahead[0], ahead[1], 2 * r)
                            split_lo(pool, ahead[0], ahead[1], 2 * r + 1)
                loop(pool, 0, p.quads - 1, lambda i: quad(i, (p, i + 1)))
                quad(p.quads - 1, after(p))

            def nothing(i, r):
                pass

            def history(hist, f, par, k, conv, done):
                wait(pool, conv, f * k - k)
                pool.tensor_copy(samples(temps[:, par], k - 1 + SEQ, k)[:, :, 0:k - 1], pick(hist, f)).then_inc(done, 1)

            def tails(tail, f, par, k, done):
                n = k - 1
                dst = pick(tail, f)
                pool.tensor_copy(dst[:, 0:n], temps[:, par, SEQ:SEQ + n]).then_inc(done, 1)
                pool.tensor_copy(dst[:, n:].rearrange("p (b t) -> p b t", b=NB),
                                 samples(temps[:, par], n + SEQ, k)[:, :, TS:]).then_inc(done, 1)

            pool.memset(eps[:, :], EPS).then_inc(sem("eps_set"), 1)
            pool.memset(line_a[:, :, 0:CKW - 1], 0.0).then_inc(sem("zeros_a"), 1)
            for s in range(SLOTS):
                split_lo(pool, ph["A"], 0, s)
            pool_phase("A", nothing)
            pool.wait_ge(acc_free[1], 4)
            pool.memset(temps[:, 0:2, 0:SKW - 1], 0.0).then_inc(sem("zeros_x"), 1)
            pool.wait_ge(sem("hist_landed"), 32)
            history(hist_x, 0, 0, SKW, sem("x_conv"), sem("x_hist"))
            history(hist_x, 1, 1, SKW, sem("x_conv"), sem("x_hist"))
            pool_phase("VU", nothing)

            def x_work(i, r):
                p = ph["X"]
                for par in range(2):
                    f = 4 * i + 2 * r + par
                    pool.wait_ge(acc_free[par], p.pair(i, 2 * r) + 1)
                    tails(tail_x, f, par, SKW, sem("tail_x"))
                    if f + 2 < 12:
                        history(hist_x, f + 2, par, SKW, sem("x_conv"), sem("x_hist"))
            p = ph["X"]
            for i in range(p.quads):
                for r in range(2):
                    x_work(i, r)
                    q, j = (p, i + 1) if i + 1 < p.quads else after(p)
                    split_lo(pool, q, j, 2 * r)
                    split_lo(pool, q, j, 2 * r + 1)

            def merge(name, n0):
                p = ph[name]

                def work(i, r):
                    j = i * 2 + r
                    pool.wait_ge(acc_free[0], p.pair(i, 2 * r) + 1)
                    pool.wait_ge(acc_free[1], p.pair(i, 2 * r) + 1)
                    if n0 == 0:
                        pool.tensor_tensor(pick(mixed, j), T(r), T(2), ALU.mult).then_inc(sem("merged"), 1)
                    else:
                        pool.tensor_tensor(T(2), T(r), T(2), ALU.mult).then_inc(sem("gated"), 1)
                        pool.wait_ge(sem("gated"), j + (n0 - 8 + 1))
                        pool.tensor_tensor(pick(mixed, j), pick(mixed, j), T(2), ALU.add).then_inc(sem("merged"), 1)
                pool_phase(name, work)

            pool.wait_ge(sem("v_turned"), 5)
            pool.wait_ge(sem("stored_v"), 16)
            merge("G2", 0)
            merge("G0", 8)

            pool.wait_ge(sem("dec_exp"), 1)
            for c in range(NCH):
                pool.wait_ge(sem("xdt"), 2 * (c + 1))
                if c >= 2:
                    pool.wait_ge(sem("chunk_sum"), 2 * (c - 1))
                pool.tensor_tensor(xw[:, c % 2].rearrange("p (h d) -> p h d", h=HEADS),
                                   xdt[:, c].rearrange("p (h d) -> p h d", h=HEADS),
                                   small[:, TO_END, c * HEADS:(c + 1) * HEADS].unsqueeze(2)
                                   .to_broadcast([P, HEADS, HD]), ALU.mult).then_inc(sem("xw"), 1)
            pool.wait_ge(sem("xdt"), 2 * NCH + 2)
            pool.tensor_tensor(xw_s.rearrange("p (h d) -> p h d", h=HEADS),
                               xdt_s.rearrange("p (h d) -> p h d", h=HEADS),
                               small[0:SMP, TO_END, NCH * HEADS:].unsqueeze(2).to_broadcast([SMP, HEADS, HD]),
                               ALU.mult).then_inc(sem("xw"), 1)
            pool.wait_ge(sem("s_exp"), 2)
            for b in range(NB):
                pool.wait_ge(sem("s_off"), b + 1)
                for g in range(2):
                    hv = h0[:, b % 2, g * 512:(g + 1) * 512].rearrange("p (h d) -> p h d", h=8)
                    last = T(5, 512).rearrange("p (h i) -> p h i", h=HEADS)[:, g * 8:(g + 1) * 8,
                                                                            TS * b + TS - 1:TS * b + TS]
                    pool.tensor_tensor(hv, hv, last.to_broadcast([P, 8, HD]), ALU.mult).then_inc(sem("h0_decayed"), 1)

            pool_phase("Z", nothing)
            merge("G1", 16)
            pool_phase("WO", nothing)
            pool.wait_ge(sem("n2_lo"), KD)
            pool.memset(temps[:, 0:2, 0:FKW - 1], 0.0).then_inc(sem("zeros_f"), 1)
            history(hist_f, 0, 0, FKW, sem("f_conv"), sem("f_hist"))
            history(hist_f, 1, 1, FKW, sem("f_conv"), sem("f_hist"))

            def up(name, f0):
                p = ph[name]

                def work(i, r):
                    f = i * 2 + (f0 + r)
                    pool.wait_ge(acc_free[0], p.pair(i, 2 * r) + 1)
                    tails(tail_f, f, r, FKW, sem("tail_f"))
                    if not (isinstance(f, int) and f + 2 >= NF):
                        history(hist_f, i * 2 + (f0 + r + 2), r, FKW, sem("f_conv"), sem("f_hist"))
                pool_phase(name, work)
            up("U1", 0)
            pool_phase("D1", nothing)
            up("U2", FFA)
            pool_phase("D2", nothing)

        @block.scalar
        def _(act):
            def hi_blocks(name, n, src, dst):
                for j in range(n):
                    act.wait_ge(sem(name + "_f32"), j + 1)
                    act.activation(dst(j), src(j), ACT.Copy).then_inc(sem(name + "_hi"), 1)

            def root(name, mm, width, dst):
                act.wait_ge(sem(name + "_" + mm[0]), mm[1])
                act.activation(halves(dst), stat, ACT.Sqrt, bias=eps[:, 0:1], scale=1.0 / width)\
                    .then_inc(sem(name + "_root"), 1)

            for j in range(KD):
                act.wait_ge(sem(f"x_landed{j}"), 16)
                if j >= 2:
                    act.wait_ge(sem("n1_sum"), j - 1)
                act.activation(T(j % 2), xbc[:, j], ACT.Square).then_inc(sem("n1_sq"), 1)
            act.wait_ge(sem("eps_set"), 1)
            root("n1", ("sum", KD), D, T(2))
            for s in range(SLOTS):
                split_hi(act, ph["A"], 0, s)
            hi_blocks("n1", KD, lambda j: T(4 + j % 2), lambda j: h_split[:, j, 0])

            def evac_a(i, s):
                if s % 2 == 0:
                    wait(act, acc_free[1], 2 * i + s // 2 - 1)
                    act.activation(halves(T(s // 2)), acc(0), ACT.Sigmoid).then_inc(acc_free[0], 1)
            act_phase(act, "A", evac_a, unroll=True)

            def evac_vu(i, s):
                a = s % 2
                act.activation(halves((v_sb if i == 0 else u_sb)[:, s]), acc(a), ACT.Gelu_apprx_tanh)\
                    .then_inc(acc_free[a], 1)
            act_phase(act, "VU", evac_vu, unroll=True)

            def to_line(a, r, k):
                for n, (src, dst) in enumerate(zip(acc_pieces(a), line_pieces(temps[:, r], k))):
                    ins_ = act.activation(dst, src, ACT.Copy)
                ins_.then_inc(acc_free[a], 1)

            def silu_x(j):
                cv = temps[:, 2 + j % 2]
                act.wait_ge(sem("x_conv"), SKW * (j + 1))
                act.activation(xbc[:, j, 0:SEQ], cv[:, 0:SEQ], ACT.Silu, bias=param("ssm_b", j))
                act.activation(xbc[:, j, SEQ:TOK].rearrange("p (b t) -> p b t", b=NB),
                               conv_pieces(cv, SKW)[2], ACT.Silu, bias=param("ssm_b", j)).then_inc(sem("xbc_done"), 1)

            def evac_x(i, s):
                b = 4 * i + s
                wait(act, sem("x_conv"), SKW * (b - 1))
                wait(act, sem("tail_x"), 2 * (b - 1))
                if b < 2:
                    act.wait_ge(acc_free[1], 4)
                to_line(s % 2, s % 2, SKW)
                if b >= 1:
                    silu_x(b - 1)
                if (i, s) == (2, 0):
                    root("gl", ("var", 1), CONF, T(5))
            act_phase(act, "X", evac_x, unroll=True)
            silu_x(11)

            act.wait_ge(sem("dt_abs"), 1)
            act.activation(small[:, EXPN], small[:, ABS], ACT.Exp, scale=-1.0).then_inc(sem("dt_exp"), 1)
            act.activation(bias_rows[:, 1], bias_rows[:, 1], ACT.Exp).then_inc(sem("dt_exp"), 1)
            for c in range(NCH + 1):
                act.wait_ge(sem("v_turned"), c + 1)
                if c < NCH:
                    act.activation(vnat[:, c], misc[:, c], ACT.Copy).then_inc(sem("vnat"), 1)
                else:
                    act.activation(vnat[0:SMP, c], misc[0:SMP, 0], ACT.Copy).then_inc(sem("vnat"), 1)
            hi_blocks("gm", 4, lambda j: u_sb[:, j], lambda j: branch[:, gmlp_at(j)[0]])

            def evac_branch(name, g, n0, extra=None):
                def evac(i, s):
                    j = i * 2 + s // 2
                    if s % 2 == 0:
                        wait(act, sem("merged"), j + (n0 - 1))
                        act.activation(halves(T(s // 2)), acc(0), ACT.Sigmoid,
                                       bias=param("b_gate", i * 2 + (8 * g + s // 2))).then_inc(acc_free[0], 1)
                    else:
                        wait(act, sem("merged"), j + n0)
                        act.activation(halves(T(2)), acc(1), ACT.Copy).then_inc(acc_free[1], 1)
                    if extra is not None:
                        extra(i, s)
                return evac

            def conf_norm(i, s):
                if (i, s) == (2, 1):
                    root("cf", ("var", 1), CONF, T(5))
            act.wait_ge(sem("xbc_done"), 12)
            act.wait_ge(sem("tail_x"), 24)
            p = ph["G2"]
            ev = evac_branch("G2", 2, 0, conf_norm)
            for i in range(p.quads):
                act_quad(act, p, i, (p, i + 1) if i + 1 < p.quads else after(p), ev)
            for j in range(4):
                act.wait_ge(sem("cf_scaled"), j + 1)
                act.activation(ca[:, j], ca[:, j], ACT.Silu, bias=param("conf_ln_b", j)).then_inc(sem("cf_f32"), 1)
            act.wait_ge(sem("stored_a"), 16 * 8)
            hi_blocks("cf", 4, lambda j: ca[:, j], lambda j: branch[:, conf_at(j)[0]])
            ev = evac_branch("G0", 0, 8)
            p = ph["G0"]
            act_quad(act, p, 0, (p, 1), ev)
            loop(act, 1, 3, lambda i: act_quad(act, p, i, (p, i + 1), ev))
            act_quad(act, p, 3, after(p), ev)

            act.wait_ge(sem("merged"), 16)
            act.wait_ge(sem("to_end_arg"), 2)
            act.activation(small[:, TO_END], small[:, TO_END], ACT.Exp).then_inc(sem("dec_exp"), 1)
            act.activation(small[:, DECAY, 0:NCH * HEADS], small[:, TOTAL, 0:NCH * HEADS], ACT.Exp)\
                .then_inc(sem("dec_exp"), 1)
            act.wait_ge(sem("a_turned"), 1)
            act.activation(a_rows[:, 0:SEQ], misc[0:HEADS, 2], ACT.Copy)
            act.activation(a_rows[:, SEQ:TOK], misc[0:HEADS, 3, 256:256 + SMP], ACT.Copy).then_inc(sem("a_rows"), 1)
            for c in range(NCH):
                act.wait_ge(sem("xb_turned"), c + 1)
                act.activation(bnat[:, c], misc[:, 2, 0:2 * STATE], ACT.Copy).then_inc(sem("bnat"), 1)
            act.wait_ge(sem("xb_turned"), NCH + 1)
            act.activation(bnat_s, misc[0:SMP, 2, 0:2 * STATE], ACT.Copy).then_inc(sem("bnat"), 1)
            for h in range(HEADS):
                act.wait_ge(sem("diff"), h + 1)
                act.activation(T(4 + h % 2, SEQ), T(4 + h % 2, SEQ), ACT.Exp).then_inc(sem("pair_decay"), 1)
                if h >= 2:
                    act.wait_ge(sem("y_head"), h - 1)
                act.activation(T(2 + h % 2, SEQ), misc[:, h % 2], ACT.Exp).then_inc(sem("a_exp"), 1)
            act.wait_ge(sem("s_diff"), 1)
            act.activation(temps[0:SMP, 4, 0:512], temps[0:SMP, 4, 0:512], ACT.Exp).then_inc(sem("s_exp"), 1)
            act.activation(T(5, 512), misc[:, 0], ACT.Exp).then_inc(sem("s_exp"), 1)

            def evac_z(i, s):
                b = 4 * i + s
                wait(act, sem("yz"), b - 1)
                act.activation(halves(T(s % 2)), acc(s % 2), ACT.Silu).then_inc(acc_free[s % 2], 1)
            act_phase(act, "Z", evac_z, unroll=True)
            root("ns", ("sum", 1), D, T(2))
            hi_blocks("ssm", KD, lambda j: T(4 + j % 2), lambda j: branch[:, ssm_at(j)[0]])
            ev = evac_branch("G1", 1, 16)
            p = ph["G1"]
            act_quad(act, p, 0, (p, 1), ev)
            loop(act, 1, 3, lambda i: act_quad(act, p, i, (p, i + 1), ev))
            act_quad(act, p, 3, after(p), ev)
            for j in range(KD):
                act.wait_ge(sem("merged"), 17 + j)
                act.activation(branch[:, mixed_at(j)[0]], mixed[:, j], ACT.Copy).then_inc(sem("mx_hi"), 1)
            act_phase(act, "WO", lambda i, s: None, unroll=True)
            root("n2", ("sum", 1), D, T(2))
            hi_blocks("n2", KD, lambda j: T(4 + j % 2), lambda j: h_split[:, j, 0])

            def up(name, f0):
                p = ph[name]


                def quad(i, ahead):
                    for r in range(2):
                        f = i * 2 + (f0 + r)
                        s = 2 * r
                        act.wait_ge(acc_full[0], p.pair(i, s) + 1)
                        wait(act, sem("f_conv"), i * (2 * FKW) + FKW * (f0 + r - 1))
                        wait(act, sem("tail_f"), i * 4 + 2 * (f0 + r - 1))
                        to_line(0, r, FKW)
                        split_hi(act, ahead[0], ahead[1], s)
                        act.wait_ge(sem("f_conv"), i * (2 * FKW) + FKW * (f0 + r + 1))
                        act.activation(T(2 + r, SEQ + NB * (FKW - 1 + TS)), T(2 + r, SEQ + NB * (FKW - 1 + TS)),
                                       ACT.Silu, bias=param("ffn_b", f)).then_inc(sem("f_silu"), 1)
                        act.wait_ge(acc_full[1], p.pair(i, s) + 1)
                        split_hi(act, ahead[0], ahead[1], s + 1)
                        act.wait_ge(acc_free[1], p.pair(i, s) + 1)
                        act.activation(pick(branch, i * 2 + r), T(4 + r), ACT.Copy).then_inc(sem("f_hi"), 1)
                if f0 == 0:
                    act.wait_ge(sem("zeros_f"), 1)
                    quad(0, (p, 1))
                    loop(act, 1, p.quads - 1, lambda i: quad(i, (p, i + 1)))
                else:
                    loop(act, 0, p.quads - 1, lambda i: quad(i, (p, i + 1)))
                quad(p.quads - 1, after(p))
            up("U1", 0)
            act_phase(act, "D1", lambda i, s: None)
            up("U2", FFA)
            act_phase(act, "D2", lambda i, s: None)
            root("nf", ("sum", 1), D, T(2))

        @block.tensor
        def _(pe):
            def channel_sum(src, done, start=True, stop=True):
                for half in range(2):
                    mm = pe.matmul(misc[:, half, 0:HALF], ones, src[:, tokens(half)], start=start, stop=stop)
                mm.then_inc(done, 1)

            pe.wait_ge(sem("consts_landed"), 16)
            for j in range(KD):
                pe.wait_ge(sem("n1_sq"), j + 1)
                channel_sum(T(j % 2), sem("n1_sum"), start=(j == 0), stop=(j == KD - 1))
            pe.wait_ge(sem("n1_lo"), KD)
            p = ph["A"]
            pe_quad(pe, p, 0, h_rhs)
            pe_quad(pe, p, 1, h_rhs)
            pe_phase(pe, "VU", h_rhs)
            p = ph["X"]
            pe_quad(pe, p, 0, h_rhs)
            pe.wait_ge(sem("gl_sum"), 1)
            channel_sum(T(4), sem("gl_mean"))
            pe_quad(pe, p, 1, h_rhs)
            pe.wait_ge(sem("gl_sq"), 1)
            channel_sum(T(4), sem("gl_var"))
            pe_quad(pe, p, 2, h_rhs)
            pe.wait_ge(sem("dt_w"), 1)
            for c in range(NCH):
                for k in range(KD):
                    for n, (wp, xp) in enumerate(((0, 0), (0, 1), (1, 0))):
                        pe.matmul(misc[:, 2, c * HEADS:(c + 1) * HEADS], h_split[:, k, xp, c * CH:(c + 1) * CH],
                                  w_dt_split[:, wp, k], start=(k == 0 and n == 0), stop=(k == KD - 1 and n == 2))
            for k in range(KD):
                for part in range(2):
                    mm = pe.matmul(misc[0:SMP, 2, NCH * HEADS:(NCH + 1) * HEADS],
                                   h_split[:, k, part, SEQ:TOK].bitcast(F32), w_dt[:, k],
                                   start=(k == 0 and part == 0), stop=(k == KD - 1 and part == 1))
            mm.then_inc(sem("dt_raw"), 1)
            pe.wait_ge(sem("vn_done"), 4)
            pe.wait_ge(sem("gl_root"), 1)
            for c in range(NCH):
                if c == 2:
                    pe.wait_ge(sem("dt_read"), 1)
                for j in range(4):
                    mm = pe.transpose(misc[:, c, j * P:(j + 1) * P], v_sb[:, j, c * CH:(c + 1) * CH], ident)
                mm.then_inc(sem("v_turned"), 1)
            pe.wait_ge(sem("vnat"), 1)
            for j in range(4):
                mm = pe.transpose(misc[0:SMP, 0, j * P:(j + 1) * P], v_sb[:, j, SEQ:TOK], ident)
            mm.then_inc(sem("v_turned"), 1)
            pe.wait_ge(sem("vnat"), NCH + 1)
            pe.wait_ge(sem("ws_masked"), 2)
            for g in range(4):
                b0 = 2 * (g % 2)
                if g >= 2:
                    pe.wait_ge(sem("mix_read"), g - 1)
                for c in range(NCH):
                    pe.matmul(misc[:, b0, c * CH:(c + 1) * CH], vnat[:, c, g * P:(g + 1) * P], ws_t[:, g],
                              start=True, stop=True)
                pe.matmul(misc[:, b0 + 1, 0:SMP], vnat[0:SMP, NCH, g * P:(g + 1) * P], ws_s[:, g],
                          start=True, stop=True).then_inc(sem("mix"), 1)
            p = ph["G2"]
            rhs = merge_rhs(gmlp_at)
            pe.wait_ge(sem("gm_lo"), 4)
            pe_quad(pe, p, 0, rhs)
            pe.wait_ge(sem("cf_sum"), 1)
            channel_sum(T(4), sem("cf_mean"))
            pe_quad(pe, p, 1, rhs)
            pe.wait_ge(sem("cf_sq"), 1)
            channel_sum(T(4), sem("cf_var"))
            pe_quad(pe, p, 2, rhs)
            pe_quad(pe, p, 3, rhs)
            pe.wait_ge(sem("cf_lo"), 4)
            pe_phase(pe, "G0", merge_rhs(conf_at))

            n4 = NCH * HEADS
            pe.wait_ge(sem("adt"), 1)
            pe.matmul(misc[:, 3, 0:n4], tri, small[:, ADT, 0:n4], start=True, stop=True)
            pe.matmul(misc[0:SMP, 3, n4:n4 + HEADS], mask_s[:, 0], small[0:SMP, ADT, n4:n4 + HEADS], start=True, stop=True)
            pe.matmul(misc[:, 3, 80:80 + n4], ones, small[:, ADT, 0:n4], start=True, stop=True)
            pe.matmul(misc[0:SMP, 3, 80 + n4:160], mask_s[:, 1], small[0:SMP, ADT, n4:n4 + HEADS],
                      start=True, stop=True).then_inc(sem("cum"), 1)
            pe.wait_ge(sem("to_end_arg"), 2)
            for c in range(NCH):
                pe.transpose(misc[0:HEADS, 2, c * CH:(c + 1) * CH], small[:, A_CUM, c * HEADS:(c + 1) * HEADS], ident)
            pe.transpose(misc[0:HEADS, 3, 256:256 + SMP], small[0:SMP, A_CUM, n4:n4 + HEADS],
                         ident[0:SMP, 0:SMP]).then_inc(sem("a_turned"), 1)
            pe.wait_ge(sem("a_rows"), 1)
            for c in range(NCH + 1):
                if c:
                    pe.wait_ge(sem("xdt"), 2 * c)
                    pe.wait_ge(sem("bnat"), c)
                rows, cols = (P, slice(c * CH, (c + 1) * CH)) if c < NCH else (SMP, slice(SEQ, TOK))
                for j in range(KD):
                    pe.transpose(misc[0:rows, j // 4, (j % 4) * P:(j % 4 + 1) * P], xbc[:, j, cols], ident)
                for g in range(2):
                    mm = pe.transpose(misc[0:rows, 2, g * P:(g + 1) * P], xbc[:, 8 + g, cols], ident)
                mm.then_inc(sem("xb_turned"), 1)
            pe.wait_ge(sem("xdt"), 2 * NCH + 2)
            pe.wait_ge(sem("bnat"), NCH + 1)
            for c in range(NCH):
                pe.wait_ge(sem("xw"), c + 1)
                for g in range(2):
                    b0 = 2 * (c % 2) + g
                    if c >= 2:
                        pe.wait_ge(sem("chunk_state"), 2 * (c - 2) + g + 1)
                    pe.matmul(misc[:, b0], bnat[:, c, g * STATE:(g + 1) * STATE], xw[:, c % 2, g * 512:(g + 1) * 512],
                              start=True, stop=True).then_inc(sem("chunk_sum"), 1)
            for g in range(2):
                pe.wait_ge(sem("chunk_state"), 4 + 1 + g)
                for c in range(NCH):
                    cols = slice(c * CH, (c + 1) * CH)
                    mm = pe.matmul(misc[:, g, cols], xbc[:, 8 + g, cols], xbc[:, 10 + g, cols], start=True, stop=True)
                mm.then_inc(sem("cb"), 1)
            pe.wait_ge(sem("chunk_state"), 2 * NCH)
            for g in range(2):
                mm = pe.matmul(misc[0:SMP, 2, g * SMP:(g + 1) * SMP], xbc[:, 8 + g, SEQ:TOK], xbc[:, 10 + g, SEQ:TOK],
                               start=True, stop=True)
            mm.then_inc(sem("cb"), 1)
            pe.wait_ge(sem("cbm"), 3)

            def spread(h):
                if h >= 2:
                    pe.wait_ge(sem("a_exp"), h - 1)
                pe.matmul(misc[:, h % 2], ident[0:HEADS, h:h + 1].to_broadcast([HEADS, P]), a_rows[:, 0:SEQ],
                          start=True, stop=True).then_inc(sem("a_spread"), 1)
            spread(0)
            for h in range(HEADS):
                if h + 1 < HEADS:
                    spread(h + 1)
                b0, rows = 2 + (h // 2) % 2, slice((h % 2) * HD, (h % 2 + 1) * HD)
                if h % 2 == 0 and h >= 4:
                    pe.wait_ge(sem("y_sum"), h // 2 - 1)
                pe.wait_ge(sem("mix_head"), h + 1)
                pe.wait_ge(sem("c_decayed"), h + 1)
                for c in range(NCH):
                    cols = slice(c * CH, (c + 1) * CH)
                    mm = pe.matmul(misc[rows, b0, cols], xdt[:, c, h * HD:(h + 1) * HD], T(4 + h % 2, SEQ)[:, cols],
                                   start=True, stop=(c == 0))
                    if c:
                        mm = pe.matmul(misc[rows, b0, cols], h_chunk[:, c - 1, h * HD:(h + 1) * HD],
                                       T(2 + h % 2, SEQ)[:, cols], start=False, stop=True)
                mm.then_inc(sem("y_head"), 1)
            pe.wait_ge(sem("a_exp"), HEADS)
            pe.wait_ge(sem("y_sum"), 8)
            for h in range(HEADS):
                mm = pe.matmul(misc[:, 0, h * SMP:(h + 1) * SMP], ident[0:HEADS, h:h + 1].to_broadcast([HEADS, P]),
                               a_rows[:, SEQ:TOK], start=True, stop=True)
            mm.then_inc(sem("s_spread"), 1)
            pe.wait_ge(sem("s_mix"), 1)
            for h in range(HEADS):
                rows = slice((h % 2) * HD, (h % 2 + 1) * HD)
                mm = pe.matmul(misc[rows, 1, (h // 2) * SMP:(h // 2 + 1) * SMP], xdt_s[:, h * HD:(h + 1) * HD],
                               temps[0:SMP, 4, h * SMP:(h + 1) * SMP], start=True, stop=True)
            mm.then_inc(sem("s_diag"), 1)
            pe.wait_ge(sem("xw"), NCH + 1)
            for b in range(NB):
                pe.wait_ge(sem(f"h0_landed{b % 2}"), 16 * (b // 2 + 1))
                for j in range(KD):
                    g = j // 4
                    mm = pe.matmul(misc[:, 2, j * SMP + TS * b:j * SMP + TS * b + TS], h0[:, b % 2, j * P:(j + 1) * P],
                                   xbc[:, 10 + g, SEQ + TS * b:SEQ + TS * b + TS], start=True, stop=True)
                mm.then_inc(sem("s_off"), 1)
                pe.wait_ge(sem("b_masked"), b + 1)
                for g in range(2):
                    pe.wait_ge(sem("s_exp"), 2)
                    bank = 0 if g == 0 else 3
                    if b:
                        pe.wait_ge(sem("h0_new"), 2 * (b - 1) + g + 1)
                    pe.matmul(misc[:, bank], bm_s[:, b % 2, g * STATE:(g + 1) * STATE], xw_s[:, g * 512:(g + 1) * 512],
                              start=True, stop=True).then_inc(sem("s_sum"), 1)

            pe_phase(pe, "Z", h_rhs)
            pe.wait_ge(sem("yz_sq"), 1)
            channel_sum(T(5), sem("ns_sum"))
            pe.wait_ge(sem("ssm_lo"), KD)
            pe_phase(pe, "G1", merge_rhs(ssm_at))
            pe.wait_ge(sem("mx_lo"), KD)
            pe_phase(pe, "WO", branch_rhs(mixed_at))
            pe.wait_ge(sem("x2_sq"), 1)
            channel_sum(T(5), sem("n2_sum"))
            pe.wait_ge(sem("n2_lo"), KD)
            pe_phase(pe, "U1", h_rhs)
            pe.wait_ge(sem("f_lo"), FFA)
            pe_phase(pe, "D1", down_rhs(FFA // 2))
            pe_phase(pe, "U2", h_rhs)
            pe.wait_ge(sem("f_lo"), NF)
            pe_phase(pe, "D2", down_rhs(FFB // 2))
            pe.wait_ge(sem("x3_sq"), 1)
            channel_sum(T(5), sem("nf_sum"))

        @block.vector
        def _(dve):
            chained = [0]

            def link(ins_):
                chained[0] += 1
                ins_.then_inc(sem("dve_chain"), 1)
                dve.wait_ge(sem("dve_chain"), chained[0])

            def operand(name, n, produce, tmp, lo):
                for j in range(n + 1):
                    if j < n:
                        if j >= 2:
                            dve.wait_ge(sem(name + "_lo"), j - 1)
                        produce(j).then_inc(sem(name + "_f32"), 1)
                    if j:
                        i = j - 1
                        dve.wait_ge(sem(name + "_hi"), i + 1)
                        hi, dst = lo(i)
                        dve.tensor_tensor(dst, tmp(i), hi.bitcast(F32), ALU.subtract).then_inc(sem(name + "_lo"), 1)

            def rstd(name):
                dve.wait_ge(sem(name + "_root"), 1)
                link(dve.reciprocal(T(3), T(2)))

            rstd("n1")
            dve.wait_ge(sem("params_landed"), 16)

            def h_parts(j):
                return h_split[:, j, 0], h_split[:, j, 1]

            def scaled(name):
                return lambda j: dve.scalar_tensor_tensor(out=T(4 + j % 2), in0=xbc[:, j], scalar=param(name, j),
                                                          in1=T(3), op0=ALU.mult, op1=ALU.mult)
            operand("n1", KD, scaled("norm1_g"), lambda j: T(4 + j % 2), h_parts)
            dve.wait_ge(sem("small_landed"), 16 * 4)
            link(dve.tensor_copy(w_dt_split[:, 0], w_dt[:, :, :]))
            dve.tensor_tensor(w_dt_split[:, 1], w_dt[:, :, :], w_dt_split[:, 0].bitcast(F32), ALU.subtract)\
                .then_inc(sem("dt_w"), 1)
            dve.wait_ge(sem("gmlp_landed"), 16 * (2 + 4 * NB))
            dve.tensor_tensor(ws_t, ws_t, tri.unsqueeze(1).to_broadcast([P, 4, CH]), ALU.mult)\
                .then_inc(sem("ws_masked"), 1)
            dve.tensor_tensor(ws_s, ws_s, mask_s[:, 0].unsqueeze(1).to_broadcast([SMP, 4, SMP]), ALU.mult)\
                .then_inc(sem("ws_masked"), 1)
            dve.wait_ge(sem("hist_a_landed"), 64)
            for b in range(4):
                dve.wait_ge(acc_full[1], b + 1)
                dve.wait_ge(acc_free[0], b + 1)
                for src, sig, dst in zip(acc_pieces(1), [T(b % 2)[:, 0:HALF], T(b % 2)[:, HALF:SEQ],
                                                         T(b % 2)[:, SEQ:].rearrange("p (b t) -> p b t", b=NB)],
                                         line_pieces(line_a[:, b], CKW)):
                    ins_ = dve.tensor_tensor(dst, src, sig, ALU.mult)
                ins_.then_inc(acc_free[1], 1)

            taps = [(b, t) for b in range(4) for t in range(CKW)]
            dve.wait_ge(acc_free[1], 4)
            dve.wait_ge(sem("zeros_a"), 1)

            def conf_taps(n):
                for _ in range(min(n, len(taps))):
                    b, t = taps.pop(0)
                    w = param("conf_w", b * CKW + t)
                    prompt = line_a[:, b, t:t + SEQ]
                    smp = samples(line_a[:, b], CKW - 1 + SEQ, CKW)[:, :, t:t + TS]
                    out_s = ca[:, b, SEQ:TOK].rearrange("p (b t) -> p b t", b=NB)
                    if t == 0:
                        dve.tensor_scalar(ca[:, b, 0:SEQ], prompt, w, param("conf_b", b), ALU.mult, ALU.add)
                        link(dve.tensor_scalar(out_s, smp, w, param("conf_b", b), ALU.mult, ALU.add))
                    else:
                        dve.scalar_tensor_tensor(out=ca[:, b, 0:SEQ], in0=prompt, scalar=w, in1=ca[:, b, 0:SEQ],
                                                 op0=ALU.mult, op1=ALU.add)
                        link(dve.scalar_tensor_tensor(out=out_s, in0=smp, scalar=w, in1=out_s, op0=ALU.mult,
                                                      op1=ALU.add))

            def x_conv(f):
                par, n = f % 2, line(SKW) - SKW + 1
                dve.wait_ge(acc_free[par], ph["X"].pair0 + f // 2 + 1)
                dve.wait_ge(sem("x_hist"), f + 1)
                if f >= 2:
                    dve.wait_ge(sem("xbc_done"), f - 1)
                if f == 0:
                    dve.wait_ge(sem("zeros_x"), 1)
                cv = T(2 + par, n)
                for t in range(SKW):
                    src, w = temps[:, par, t:t + n], param("ssm_w", f * SKW + t)
                    if t == 0:
                        dve.tensor_scalar(cv, src, w, None, ALU.mult).then_inc(sem("x_conv"), 1)
                    else:
                        dve.wait_ge(sem("x_conv"), f * SKW + t)
                        dve.scalar_tensor_tensor(out=cv, in0=src, scalar=w, in1=cv, op0=ALU.mult, op1=ALU.add)\
                            .then_inc(sem("x_conv"), 1)

            def four_sum(src, done):
                link(dve.tensor_tensor(T(4), src[:, 0], src[:, 1], ALU.add))
                link(dve.tensor_tensor(T(4), T(4), src[:, 2], ALU.add))
                dve.tensor_tensor(T(4), T(4), src[:, 3], ALU.add).then_inc(done, 1)

            def center(src, name):
                dve.wait_ge(sem(name + "_mean"), 1)
                for j in range(4):
                    ins_ = dve.scalar_tensor_tensor(out=halves(src[:, j]), in0=stat, scalar=-1.0 / CONF,
                                                    in1=halves(src[:, j]), op0=ALU.mult, op1=ALU.add)
                link(ins_)
                dve.tensor_tensor(T(4), src[:, 0], src[:, 0], ALU.mult)
                for j in range(1, 4):
                    link(dve.tensor_tensor(T(5), src[:, j], src[:, j], ALU.mult))
                    ins_ = dve.tensor_tensor(T(4), T(4), T(5), ALU.add)
                    if j < 3:
                        link(ins_)
                ins_.then_inc(sem(name + "_sq"), 1)

            def scale(src, name, gain, done):
                dve.wait_ge(sem(name + "_root"), 1)
                link(dve.reciprocal(T(4), T(5)))
                for j in range(4):
                    dve.scalar_tensor_tensor(out=src[:, j], in0=src[:, j], scalar=param(gain, j), in1=T(4),
                                             op0=ALU.mult, op1=ALU.mult).then_inc(done, 1)

            conf_taps(56)
            dve.wait_ge(acc_free[0], 6)
            dve.wait_ge(acc_free[1], 6)
            four_sum(v_sb, sem("gl_sum"))
            for f in range(12):
                x_conv(f)
                conf_taps(4)
                if f == 4:
                    center(v_sb, "gl")
                if f == 9:
                    scale(v_sb, "gl", "gmlp_ln_g", sem("vn_scaled"))
                    dve.wait_ge(sem("vn_scaled"), 4)
                    for j in range(4):
                        dve.tensor_scalar(v_sb[:, j], v_sb[:, j], param("gmlp_ln_b", j), None, ALU.add)\
                            .then_inc(sem("vn_done"), 1)

            def sm(q):
                return small[:, q]

            def by_head(ap):
                return ap.rearrange("p (c h) -> p c h", h=HEADS)
            dve.memset(small[:, X_DT], 0.0).then_inc(sem("dve_chain"), 1)
            chained[0] += 1
            dve.wait_ge(sem("dve_chain"), chained[0])
            dve.wait_ge(sem("dt_raw"), 1)
            n4 = NCH * HEADS
            dve.tensor_tensor(by_head(small[:, X_DT, 0:n4]), by_head(misc[:, 2, 0:n4]),
                              bias_rows[:, 0].unsqueeze(1).to_broadcast([P, NCH, HEADS]), ALU.add)
            dve.tensor_tensor(small[0:SMP, X_DT, n4:], misc[0:SMP, 2, n4:n4 + HEADS], bias_rows[0:SMP, 0], ALU.add)\
                .then_inc(sem("dt_read"), 1)
            dve.wait_ge(sem("dt_read"), 1)
            link(dve.tensor_scalar(sm(ABS), sm(X_DT), -1.0, None, ALU.mult))
            dve.tensor_tensor(sm(ABS), sm(ABS), sm(X_DT), ALU.max).then_inc(sem("dt_abs"), 1)
            dve.wait_ge(sem("dt_exp"), 1)
            link(dve.tensor_scalar(sm(RATIO), sm(EXPN), 2.0, None, ALU.add))
            link(dve.reciprocal(sm(RATIO2), sm(RATIO)))
            link(dve.tensor_tensor(sm(RATIO), sm(EXPN), sm(RATIO2), ALU.mult))
            link(dve.tensor_tensor(sm(RATIO2), sm(RATIO), sm(RATIO), ALU.mult))
            link(dve.tensor_scalar(sm(POLY), sm(RATIO2), 1.0 / 17, None, ALU.mult))
            for d in range(15, 1, -2):
                link(dve.scalar_tensor_tensor(out=sm(POLY), in0=sm(POLY), scalar=1.0 / d, in1=sm(RATIO2),
                                              op0=ALU.add, op1=ALU.mult))
            link(dve.scalar_tensor_tensor(out=sm(POLY), in0=sm(POLY), scalar=1.0, in1=sm(RATIO),
                                          op0=ALU.add, op1=ALU.mult))
            link(dve.tensor_scalar(sm(X_DT), sm(X_DT), 0.0, None, ALU.max))
            link(dve.scalar_tensor_tensor(out=sm(DT), in0=sm(POLY), scalar=2.0, in1=sm(X_DT), op0=ALU.mult,
                                          op1=ALU.add))
            dve.wait_ge(sem("dt_exp"), 2)
            dve.scalar_tensor_tensor(out=sm(ADT).rearrange("p (c h) -> p c h", h=HEADS),
                                     in0=sm(DT).rearrange("p (c h) -> p c h", h=HEADS), scalar=-1.0,
                                     in1=bias_rows[:, 1].unsqueeze(1).to_broadcast([P, NCH + 1, HEADS]),
                                     op0=ALU.mult, op1=ALU.mult).then_inc(sem("adt"), 1)

            for g in range(4):
                b0 = 2 * (g % 2)
                dve.wait_ge(sem("mix"), g + 1)
                wait(dve, sem("gm_f32"), g)
                dve.tensor_tensor(T(4, SEQ).rearrange("p (c t) -> p c t", c=NCH),
                                  misc[:, b0].rearrange("p (c t) -> p c t", c=NCH),
                                  bs[:, g].unsqueeze(1).to_broadcast([P, NCH, CH]), ALU.add)
                dve.tensor_tensor(temps[:, 4, SEQ:TOK].rearrange("p (b t) -> p b t", b=NB),
                                  misc[:, b0 + 1, 0:SMP].rearrange("p (b t) -> p b t", b=NB),
                                  bs[:, g, 0:TS].unsqueeze(1).to_broadcast([P, NB, TS]), ALU.add)\
                    .then_inc(sem("mix_read"), 1)
                dve.wait_ge(sem("mix_read"), g + 1)
                dve.tensor_tensor(u_sb[:, g], u_sb[:, g], T(4), ALU.mult).then_inc(sem("gm_f32"), 1)
            for g in range(4):
                dve.wait_ge(sem("gm_hi"), g + 1)
                dve.tensor_tensor(branch[:, gmlp_at(g)[1]], u_sb[:, g], branch[:, gmlp_at(g)[0]].bitcast(F32),
                                  ALU.subtract).then_inc(sem("gm_lo"), 1)

            conf_taps(len(taps))
            four_sum(ca, sem("cf_sum"))
            center(ca, "cf")
            scale(ca, "cf", "conf_ln_g", sem("cf_scaled"))
            dve.wait_ge(sem("stored_a"), 16 * 8)
            for j in range(4):
                dve.wait_ge(sem("cf_hi"), j + 1)
                dve.tensor_tensor(branch[:, conf_at(j)[1]], ca[:, j], branch[:, conf_at(j)[0]].bitcast(F32),
                                  ALU.subtract).then_inc(sem("cf_lo"), 1)

            dve.wait_ge(sem("cum"), 1)
            dve.tensor_copy(small[:, A_CUM, 0:n4], misc[:, 3, 0:n4])
            dve.tensor_copy(small[0:SMP, A_CUM, n4:], misc[0:SMP, 3, n4:n4 + HEADS])
            dve.tensor_copy(small[:, TOTAL, 0:n4], misc[:, 3, 80:80 + n4])
            link(dve.tensor_copy(small[0:SMP, TOTAL, n4:], misc[0:SMP, 3, 80 + n4:160]))
            dve.memset(small[:, TO_END, n4:], 0.0).then_inc(sem("dve_chain"), 1)
            chained[0] += 1
            dve.tensor_tensor(small[:, TO_END, 0:n4], small[:, TOTAL, 0:n4], small[:, A_CUM, 0:n4], ALU.subtract)\
                .then_inc(sem("to_end_arg"), 1)
            dve.wait_ge(sem("dve_chain"), chained[0])
            dve.tensor_tensor(small[0:SMP, TO_END, n4:], small[0:SMP, TOTAL, n4:], small[0:SMP, A_CUM, n4:],
                              ALU.subtract).then_inc(sem("to_end_arg"), 1)
            for c in range(NCH + 1):
                rows = P if c < NCH else SMP
                dve.wait_ge(sem("xb_turned"), c + 1)
                for r in range(2):
                    dst = (xdt[:, c] if c < NCH else xdt_s)[:, r * 512:(r + 1) * 512]
                    dve.tensor_tensor(dst.rearrange("p (h d) -> p h d", h=8),
                                      misc[0:rows, r].rearrange("p (h d) -> p h d", h=8),
                                      small[0:rows, DT, c * HEADS + 8 * r:c * HEADS + 8 * r + 8].unsqueeze(2)
                                      .to_broadcast([rows, 8, HD]), ALU.mult).then_inc(sem("xdt"), 1)
            dve.wait_ge(sem("dec_exp"), 2)
            for c in range(NCH):
                for g in range(2):
                    cols = slice(g * 512, (g + 1) * 512)
                    bank = misc[:, 2 * (c % 2) + g]
                    dve.wait_ge(sem("chunk_sum"), 2 * c + g + 1)
                    if c == 0:
                        dve.tensor_copy(h_chunk[:, 0, cols], bank).then_inc(sem("chunk_state"), 1)
                        continue
                    dve.wait_ge(sem("chunk_state"), 2 * c + g - 1)
                    dec = small[:, DECAY, c * HEADS + 8 * g:c * HEADS + 8 * g + 8]
                    link(dve.tensor_tensor(T(4 + g, 512).rearrange("p (h d) -> p h d", h=8),
                                           h_chunk[:, c - 1, cols].rearrange("p (h d) -> p h d", h=8),
                                           dec.unsqueeze(2).to_broadcast([P, 8, HD]), ALU.mult))
                    dve.tensor_tensor(h_chunk[:, c, cols], T(4 + g, 512), bank, ALU.add).then_inc(sem("chunk_state"), 1)
            for g in range(2):
                dve.wait_ge(sem("cb"), g + 1)
                dve.tensor_tensor(cbm[:, g].rearrange("p (c i) -> p c i", c=NCH),
                                  misc[:, g].rearrange("p (c i) -> p c i", c=NCH),
                                  tri.unsqueeze(1).to_broadcast([P, NCH, CH]), ALU.mult).then_inc(sem("cbm"), 1)
            dve.wait_ge(sem("cb"), 3)
            dve.tensor_tensor(cbm_s, misc[0:SMP, 2, 0:2 * SMP].rearrange("p (g i) -> p g i", g=2),
                              mask_s[:, 0].unsqueeze(1).to_broadcast([SMP, 2, SMP]), ALU.mult).then_inc(sem("cbm"), 1)
            dve.wait_ge(sem("cbm"), 3)

            def diffs(h):
                dve.wait_ge(sem("a_spread"), h + 1)
                if h >= 2:
                    dve.wait_ge(sem("y_head"), h - 1)
                for c in range(NCH):
                    cols = slice(c * CH, (c + 1) * CH)
                    ins_ = dve.tensor_scalar(T(4 + h % 2, SEQ)[:, cols], misc[:, h % 2, cols],
                                             small[:, A_CUM, c * HEADS + h:c * HEADS + h + 1], 0.0,
                                             ALU.subtract, ALU.min)
                ins_.then_inc(sem("diff"), 1)
            diffs(0)
            for h in range(HEADS):
                g = h // 8
                if h + 1 < HEADS:
                    diffs(h + 1)
                dve.wait_ge(sem("pair_decay"), h + 1)
                dve.tensor_tensor(T(4 + h % 2, SEQ), T(4 + h % 2, SEQ), cbm[:, g], ALU.mult)\
                    .then_inc(sem("mix_head"), 1)
                dve.wait_ge(sem("a_exp"), h + 1)
                dve.tensor_tensor(T(2 + h % 2, SEQ), T(2 + h % 2, SEQ), xbc[:, 10 + g, 0:SEQ], ALU.mult).then_inc(sem("c_decayed"), 1)
                if h % 2 == 1:
                    j = h // 2
                    dve.wait_ge(sem("y_head"), h + 1)
                    dve.scalar_tensor_tensor(out=xbc[:, j, 0:SEQ], in0=xbc[:, j, 0:SEQ], scalar=param("ssm_d", j),
                                             in1=misc[:, 2 + j % 2], op0=ALU.mult, op1=ALU.add)\
                        .then_inc(sem("y_sum"), 1)
            mixs = temps[0:SMP, 4, 0:512]
            dve.wait_ge(sem("s_spread"), 1)
            link(dve.tensor_tensor(mixs.rearrange("p (h i) -> p h i", h=HEADS),
                                   misc[0:SMP, 0].rearrange("p (h i) -> p h i", h=HEADS),
                                   small[0:SMP, A_CUM, n4:].unsqueeze(2).to_broadcast([SMP, HEADS, SMP]),
                                   ALU.subtract))
            dve.tensor_scalar(mixs, mixs, 0.0, None, ALU.min).then_inc(sem("s_diff"), 1)
            dve.wait_ge(sem("s_exp"), 1)
            for g in range(2):
                half = mixs[:, g * 256:(g + 1) * 256].rearrange("p (h i) -> p h i", h=8)
                ins_ = dve.tensor_tensor(half, half, cbm_s[:, g].unsqueeze(1).to_broadcast([SMP, 8, SMP]), ALU.mult)
            ins_.then_inc(sem("s_mix"), 1)
            dve.wait_ge(sem("bnat"), NCH + 1)

            def b_masked(b):
                dve.tensor_scalar(bm_s[:, b % 2], bnat_s, mask_s[:, 1, TS * b:TS * b + 1], None, ALU.mult)\
                    .then_inc(sem("b_masked"), 1)
            b_masked(0)
            for b in range(NB):
                if b + 1 < NB:
                    if b >= 1:
                        dve.wait_ge(sem("s_sum"), 2 * b)
                    b_masked(b + 1)
                for g in range(2):
                    dve.wait_ge(sem("s_sum"), 2 * b + g + 1)
                    dve.wait_ge(sem("h0_decayed"), 2 * b + g + 1)
                    hv = h0[:, b % 2, g * 512:(g + 1) * 512]
                    dve.tensor_tensor(hv, hv, misc[:, 0 if g == 0 else 3], ALU.add).then_inc(sem("h0_new"), 1)
            dve.wait_ge(sem("s_off"), NB)
            dve.wait_ge(sem("s_exp"), 2)
            dve.wait_ge(sem("s_diag"), 1)
            ys = T(4, KD * SMP)
            for r in range(2):
                rows = slice(r * HD, (r + 1) * HD)
                ins_ = dve.tensor_tensor(ys[rows].rearrange("p (j i) -> p j i", j=KD),
                                         misc[rows, 2, 0:KD * SMP].rearrange("p (j i) -> p j i", j=KD),
                                         temps[rows, 5, 0:512].rearrange("p (j r i) -> p j r i", j=KD, r=2)[:, :, r],
                                         ALU.mult)
            link(ins_)
            link(dve.tensor_tensor(ys, ys, misc[:, 1, 0:KD * SMP], ALU.add))
            for j in range(KD):
                ins_ = dve.scalar_tensor_tensor(out=xbc[:, j, SEQ:TOK], in0=xbc[:, j, SEQ:TOK],
                                                scalar=param("ssm_d", j), in1=ys[:, j * SMP:(j + 1) * SMP],
                                                op0=ALU.mult, op1=ALU.add)
            link(ins_)

            def sum_squares(j, last, done):
                dst = T(5) if j == 0 else T(4)
                link(dve.tensor_tensor(dst, xbc[:, j], xbc[:, j], ALU.mult))
                if j:
                    ins_ = dve.tensor_tensor(T(5), T(5), T(4), ALU.add)
                    if last:
                        ins_.then_inc(done, 1)
                    else:
                        link(ins_)

            for b in range(KD):
                dve.wait_ge(acc_free[b % 2], ph["Z"].pair0 + b // 2 + 1)
                dve.tensor_tensor(xbc[:, b], xbc[:, b], T(b % 2), ALU.mult).then_inc(sem("yz"), 1)
                dve.wait_ge(sem("yz"), b + 1)
                sum_squares(b, b == KD - 1, sem("yz_sq"))
            rstd("ns")

            def parts_of(at):
                return lambda j: (branch[:, at(j)[0]], branch[:, at(j)[1]])
            dve.wait_ge(sem("stored_h"), 16)
            operand("ssm", KD, scaled("ssm_g"), lambda j: T(4 + j % 2), parts_of(ssm_at))

            for j in range(KD):
                dve.wait_ge(sem("mx_hi"), j + 1)
                dve.tensor_tensor(branch[:, mixed_at(j)[1]], mixed[:, j], branch[:, mixed_at(j)[0]].bitcast(F32),
                                  ALU.subtract).then_inc(sem("mx_lo"), 1)
            p = ph["WO"]
            for j in range(KD):
                a = j % 2
                dve.wait_ge(sem(f"x_landed{j}"), 32)
                dve.wait_ge(acc_full[a], p.pair0 + j // 2 + 1)
                dve.tensor_tensor(halves(xbc[:, j]), acc(a), halves(xbc[:, j]), ALU.add).then_inc(acc_free[a], 1)
                dve.wait_ge(acc_free[a], p.pair0 + j // 2 + 1)
                sum_squares(j, j == KD - 1, sem("x2_sq"))
            rstd("n2")
            operand("n2", KD, scaled("norm2_g"), lambda j: T(4 + j % 2), h_parts)

            n_out = SEQ + NB * (FKW - 1 + TS)

            def up(name, f0):
                p = ph[name]

                def quad(i):
                    for r in range(2):
                        f = i * 2 + (f0 + r)
                        pair = p.pair(i, 2 * r)
                        dve.wait_ge(acc_free[0], pair + 1)
                        dve.wait_ge(sem("f_hist"), f + 1)
                        cv = T(2 + r, n_out)
                        for t in range(FKW):
                            src, w = temps[:, r, t:t + n_out], param("ffn_w", i * (2 * FKW) + ((f0 + r) * FKW + t))
                            if t == 0:
                                dve.tensor_scalar(cv, src, w, None, ALU.mult).then_inc(sem("f_conv"), 1)
                            else:
                                dve.wait_ge(sem("f_conv"), i * (2 * FKW) + ((f0 + r) * FKW + t))
                                dve.scalar_tensor_tensor(out=cv, in0=src, scalar=w, in1=cv, op0=ALU.mult, op1=ALU.add)\
                                    .then_inc(sem("f_conv"), 1)
                        dve.wait_ge(sem("f_silu"), f + 1)
                        dve.wait_ge(acc_full[1], pair + 1)
                        prod = T(4 + r)
                        for src, sil, dst in zip(acc_pieces(1), conv_pieces(temps[:, 2 + r], FKW),
                                                 [prod[:, 0:HALF], prod[:, HALF:SEQ],
                                                  prod[:, SEQ:TOK].rearrange("p (b t) -> p b t", b=NB)]):
                            ins_ = dve.tensor_tensor(dst, src, sil, ALU.mult)
                        ins_.then_inc(acc_free[1], 1)
                        dve.wait_ge(sem("f_hi"), f + 1)
                        dve.tensor_tensor(pick(branch, i * 2 + (12 + r)), prod, pick(branch, i * 2 + r).bitcast(F32),
                                          ALU.subtract).then_inc(sem("f_lo"), 1)
                loop(dve, 0, p.quads, quad)

            def down(name, squares):
                p = ph[name]
                for j in range(KD):
                    a = j % 2
                    dve.wait_ge(acc_full[a], p.pair0 + j // 2 + 1)
                    dve.tensor_tensor(halves(xbc[:, j]), acc(a), halves(xbc[:, j]), ALU.add).then_inc(acc_free[a], 1)
                    if squares:
                        dve.wait_ge(acc_free[a], p.pair0 + j // 2 + 1)
                        sum_squares(j, j == KD - 1, sem("x3_sq"))
            dve.wait_ge(sem("zeros_f"), 1)
            up("U1", 0)
            down("D1", False)
            up("U2", FFA)
            down("D2", True)
            rstd("nf")
            for j in range(KD):
                dve.scalar_tensor_tensor(out=xbc[:, j], in0=xbc[:, j], scalar=param("final_g", j), in1=T(3),
                                         op0=ALU.mult, op1=ALU.mult).then_inc(sem("y_done"), 1)
    return nc


def tiles(w, rows=None):
    k, n = w.shape
    return np.ascontiguousarray(w.reshape(k // P, P, n // P, P).transpose(2, 1, 0, 3).reshape(n // P, P, k))


def channels(a):
    lead = a.shape[:-1]
    v = a.reshape(*lead, a.shape[-1] // P, P)
    return np.ascontiguousarray(np.moveaxis(np.moveaxis(v, -1, 0), -1, 1))


def kernel(**inputs):
    import concourse.bacc as bacc
    from concourse.bass_utils import run_bass_kernel_spmd

    a = {k: np.asarray(v) for k, v in inputs.items()}
    o3, o4 = 2 * CONF + D, 2 * CONF + D + XBC
    o5 = o4 + HEADS
    win = a["w_in"][0]
    t_a1, t_a2 = tiles(win[:, 0:CONF]), tiles(win[:, CONF:2 * CONF])
    t_u, t_v = tiles(win[:, o5:o5 + CONF]), tiles(win[:, o5 + CONF:o5 + 2 * CONF])
    glu = np.stack([t_a2, t_a1], 1).reshape(8, P, D)
    up = tiles(a["ffn_w_up"][0])
    down = a["ffn_w_down"][0]

    def halves_of(w):
        t = tiles(w)
        return np.ascontiguousarray(t.reshape(KD, P, 2, w.shape[0] // 2).transpose(0, 2, 1, 3)
                                    .reshape(2 * KD, P, w.shape[0] // 2))
    cols = {
        "norm1_g": channels(a["norm1_g"][0]), "b_gate": channels(a["b_gate"][0]),
        "conf_w": channels(a["conf_conv_w"][0]), "conf_b": channels(a["conf_conv_b"][0]),
        "conf_ln_g": channels(a["conf_ln_g"][0]), "conf_ln_b": channels(a["conf_ln_b"][0]),
        "ssm_w": channels(a["ssm_conv_w"][0]), "ssm_b": channels(a["ssm_conv_b"][0]),
        "ssm_g": channels(a["ssm_norm_g"][0]), "ssm_d": channels(np.repeat(a["ssm_d"][0], HD)),
        "gmlp_ln_g": channels(a["gmlp_ln_g"][0]), "gmlp_ln_b": channels(a["gmlp_ln_b"][0]),
        "norm2_g": channels(a["norm2_g"][0]), "ffn_w": channels(a["ffn_conv_w"][0]),
        "ffn_b": channels(a["ffn_conv_b"][0]), "final_g": channels(a["final_norm_g"]),
    }
    i = np.arange(P)
    j = np.arange(SMP)
    same = (j[:, None] // TS) == (j[None, :] // TS)
    f32 = np.float32
    arrays = {
        "x": channels(np.concatenate([a["x_prompt"][0], a["x_sample"].reshape(SMP, D)], 0)),
        "consts": np.stack([np.eye(P), i[:, None] <= i[None, :], np.ones((P, P))], 1).astype(f32),
        "mask_s": np.stack([same & (j[:, None] <= j[None, :]), same], 1).astype(f32),
        "params": np.concatenate([cols[n].reshape(P, -1) for n, _ in PARAM_BLOCKS], 1),
        "w_in_main": np.concatenate([glu, t_v, t_u, tiles(win[:, o3:o4])], 0),
        "w_in_z": tiles(win[:, 2 * CONF:o3]),
        "w_dt": np.ascontiguousarray(win[:, o4:o5].reshape(KD, P, HEADS).transpose(1, 0, 2)),
        "ssm_dt_bias": a["ssm_dt_bias"][0], "ssm_a_log": a["ssm_a_log"][0],
        "w_gate": tiles(a["w_gate"][0]),
        "conf_w_out": tiles(a["conf_w_out"][0]), "ssm_w_out": tiles(a["ssm_w_out"][0]),
        "gmlp_w_out": tiles(a["gmlp_w_out"][0]), "w_o": tiles(a["w_o"][0]),
        "ffn_w_up": np.stack([up[0:NF], up[NF:]], 1).reshape(2 * NF, P, D),
        "ffn_w_down1": halves_of(down[0:FFA * P]), "ffn_w_down2": halves_of(down[FFA * P:]),
        "gmlp_w_s": np.ascontiguousarray(a["gmlp_w_s"][0].transpose(2, 0, 1)),
        "gmlp_b_s": a["gmlp_b_s"][0].reshape(-1),
        "state_conv_a": channels(a["state_conv_a"][0]),
        "state_conv_ssm": channels(a["state_conv_ssm"][0]),
        "state_conv_ffn": channels(a["state_conv_ffn"][0]),
        "state_ssm": np.ascontiguousarray(a["state_ssm"][0].transpose(0, 3, 1, 2).reshape(NB, STATE, D)),
    }
    arrays = {k: np.ascontiguousarray(v) for k, v in arrays.items()}
    shapes = {
        "y": (P, KD, TOK), "conv_a_p": (P, 4, CKW - 1), "conv_a_s": (P, 4, NB, CKW - 1),
        "conv_ssm": (P, 12, (NB + 1) * (SKW - 1)), "conv_ffn": (P, NF, (NB + 1) * (FKW - 1)),
        "ssm_p": (STATE, D), "ssm_s": (NB, STATE, D), "gmlp_v_s": (P, 4, SMP),
    }
    nc = bacc.Bacc("TRN2", target_bir_lowering=False, num_devices=1, dynamic_dma_scratch_size=1024)
    ins = {k: nc.dram_tensor(f"in_{k}", v.shape, F32, kind="ExternalInput").ap() for k, v in arrays.items()}
    outs = {k: nc.dram_tensor(f"out_{k}", v, F32, kind="ExternalOutput").ap() for k, v in shapes.items()}
    build(nc, ins, outs)
    r = run_bass_kernel_spmd(nc, [{f"in_{k}": v for k, v in arrays.items()}], core_ids=[0])
    got = {k: np.asarray(r.results[0][f"out_{k}"]) for k in shapes}

    def rows(t):
        v = np.moveaxis(np.moveaxis(t, 0, -1), 0, -2)
        return v.reshape(*v.shape[:-2], -1)

    y = rows(got["y"])
    n, m = SKW - 1, FKW - 1
    conv_ssm, conv_ffn = rows(got["conv_ssm"]), rows(got["conv_ffn"])

    def state(t):
        return t.reshape(*t.shape[:-2], STATE, HEADS, HD).transpose(0, 2, 3, 1)
    out = (
        y[0:SEQ][None], y[SEQ:].reshape(NB, TS, D), rows(got["conv_a_p"])[None, None],
        state(got["ssm_p"][None])[None], conv_ssm[0:n][None, None], conv_ffn[0:m][None, None],
        rows(got["conv_a_s"])[None], state(got["ssm_s"])[None],
        conv_ssm[n:].reshape(NB, n, XBC)[None], conv_ffn[m:].reshape(NB, m, FF)[None],
        rows(got["gmlp_v_s"]).reshape(NB, TS, CONF)[None],
    )
    return tuple(np.ascontiguousarray(o) for o in out)
```

```python
from contextlib import ExitStack

import numpy as np
import concourse.bass as bass
from concourse import mybir

F32 = mybir.dt.float32
F32R = mybir.dt.float32r
ACT = mybir.ActivationFunctionType
ALU = mybir.AluOpType

P = 128
D, SEQ, NB, TS = 1024, 512, 8, 4
SMP = NB * TS
TOK = SEQ + SMP
HALF = TOK // 2
KD = D // P
CONF, CKW = 512, 31
HEADS, HD, STATE, SKW, XBC = 16, 64, 128, 4, 1536
FF, FKW = 2816, 3
NF = FF // P
FFA = 12
FFB = NF - FFA
CH = 128
NCH = SEQ // CH
EPS = 1e-6
SLOTS = 4
CONF_SHARED = 3
ACT_TAPS = (2, 2)
POOL_TAPS = (3, 4)
RING = 8
GMLP_LOADS = 2 + NB
HEADS_AFTER = (0, 0, 0, 0, 0, 1, 1, 1, 1, 2, 1, 2, 1, 2, 2, 2)
ELEM = KD * P

PHASES = [
    ("A", 2, (8, 8, 8, 8), 1),
    ("VU", 2, (8, 8, 8, 8), 1),
    ("X", 3, (8, 8, 8, 8), 1),
    ("G2", 4, (8, 4, 8, 4), 1),
    ("G0", 4, (8, 4, 8, 4), 1),
    ("Z", 2, (8, 8, 8, 8), 1),
    ("G1", 4, (8, 8, 8, 8), 1),
    ("WO", 2, (8, 8, 8, 8), 1),
    ("U1", 6, (8, 8, 8, 8), 1),
    ("D1", 4, (6, 6, 6, 6), 2),
    ("U2", 5, (8, 8, 8, 8), 1),
    ("D2", 4, (5, 5, 5, 5), 2),
]


class Phase:
    def __init__(self, name, quads, kb, per_block, quad0, pair0):
        self.name, self.quads, self.kb, self.per_block = name, quads, kb, per_block
        self.quad0, self.pair0 = quad0, pair0
        self.pairs_per_quad = 2 // per_block

    def pair(self, i, s):
        if self.per_block == 2:
            return i + self.pair0
        return i * 2 + (self.pair0 + s // 2)

    def acc(self, s):
        return s // 2 if self.per_block == 2 else s % 2


def phases():
    out, q, p = {}, 0, 0
    for name, quads, kb, per_block in PHASES:
        out[name] = Phase(name, quads, kb, per_block, q, p)
        q += quads
        p += quads * (2 // per_block)
    return out


PARAM_BLOCKS = [("norm1_g", KD), ("b_gate", 3 * KD), ("conf_w", 4 * CKW), ("conf_b", 4), ("conf_ln_g", 4),
                ("conf_ln_b", 4), ("ssm_w", 12 * SKW), ("ssm_b", 12), ("ssm_g", KD), ("ssm_d", KD),
                ("gmlp_ln_g", 4), ("gmlp_ln_b", 4), ("norm2_g", KD), ("ffn_w", NF * FKW), ("ffn_b", NF),
                ("final_g", KD)]
PARAM_AT, _n = {}, 0
for _name, _k in PARAM_BLOCKS:
    PARAM_AT[_name] = _n
    _n += _k
N_PARAM = _n


def line(k):
    return k - 1 + SEQ + NB * (k - 1 + TS)


def loop(e, lo, hi, body):
    if hi - lo == 1:
        body(lo)
    elif hi > lo:
        with e.Fori(lo, hi) as i:
            body(i)


def wait(e, sem, value):
    if isinstance(value, int) and value <= 0:
        return
    e.wait_ge(sem, value)


def pick(t, j):
    if isinstance(j, int):
        return t[:, j]
    v = t[:, bass.ds(j, 1)]
    names = "abcdef"[:len(v.shape) - 2]
    return v.rearrange(f"p o {' '.join(names)} -> p (o {names[0]}) {' '.join(names[1:])}")


def build(nc, ins, outs):
    ph = phases()
    order = [x[0] for x in PHASES]
    with ExitStack() as ctx:
        def sb(name, shape, dt=F32):
            return ctx.enter_context(nc.sbuf_tensor(name, shape, dt))

        sems = {}

        def sem(name):
            if name not in sems:
                sems[name] = ctx.enter_context(nc.semaphore(name))
            return sems[name]

        h_split = sb("h_split", [P, KD, 2, TOK], F32R)
        w_split = sb("w_split", [P, SLOTS, 2, ELEM], F32R)
        w_raw = sb("w_raw", [P, SLOTS, ELEM])
        params = sb("params", [P, N_PARAM])
        consts = sb("consts", [P, 3, P])
        mask_s = sb("mask_s", [SMP, 2, SMP])
        xbc = sb("xbc", [P, 12, TOK])
        u_sb = sb("u_sb", [P, 4, TOK])
        mixed = sb("mixed", [P, KD, TOK])
        ca = sb("ca", [P, 4, TOK])
        temps = sb("temps", [P, 6, 576])
        small = sb("small", [P, 12, 5 * HEADS])
        a_rows = sb("a_rows", [HEADS, TOK])
        bias_rows = sb("bias_rows", [P, 2, HEADS])
        w_dt = sb("w_dt", [P, KD, HEADS])
        w_dt_split = sb("w_dt_split", [P, 2, KD, HEADS], F32R)
        eps = sb("eps", [P, 1])
        rms = sb("rms", [P, 2, 6])
        hist_x = sb("hist_x", [P, 12, NB, SKW - 1])
        hist_f = sb("hist_f", [P, NF, NB, FKW - 1])
        tail_x = sb("tail_x", [P, 12, (NB + 1) * (SKW - 1)])
        tail_f = sb("tail_f", [P, NF, (NB + 1) * (FKW - 1)])
        with ExitStack() as early:
            part0, part1, part2 = (early.enter_context(nc.sbuf_tensor(f"part{n}", [P, 8 * TOK], F32))
                                   for n in range(3))
        branch = sb("branch", [P, 24, TOK], F32R)

        def carve(tensor, *shapes):
            out, o = [], 0
            for parts, *dims in shapes:
                n = int(np.prod(dims))
                v = tensor[0:parts, o:o + n]
                if len(dims) == 2:
                    v = v.rearrange("p (a b) -> p a b", a=dims[0])
                out.append(v)
                o += n
            assert o <= tensor.shape[1]
            return out

        u_flat = u_sb[:, :, :].rearrange("p j n -> p (j n)")
        ca_flat = ca[:, :, :].rearrange("p j n -> p (j n)")
        v_sb = mixed[:, 0:4]
        (tap_ring,) = carve(part0, (P, RING, SEQ))
        (line_a,) = carve(part1, (P, 4, line(CKW)))
        vnat, ws_t, bs, ws_s = carve(part2, (P, 5, CONF), (P, 4, CH), (P, 4, CH), (SMP, 4, SMP))
        (h_chunk,) = carve(part0, (P, NCH, D))
        (xdt,) = carve(part2, (P, NCH, D))
        bnat, cbm = carve(ca_flat, (P, NCH, 2 * STATE), (P, 2, SEQ))
        (c_dec,) = carve(ca_flat, (P, 2, SEQ))
        (xw,) = carve(u_flat, (P, 2, D))
        (h0,) = carve(u_flat, (P, 2, D))
        bnat_s, bm_s, xdt_s, xw_s, cbm_s = carve(part1, (SMP, 2 * STATE), (SMP, 2, 2 * STATE), (SMP, D), (SMP, D),
                                                 (SMP, 2, SMP))
        ident, tri, ones = consts[:, 0], consts[:, 1], consts[:, 2]
        X_DT, ABS, EXPN, RATIO, RATIO2, POLY, TO_END, DT, ADT, A_CUM, TOTAL, DECAY = range(12)

        def param(name, j):
            if isinstance(j, int):
                return params[:, PARAM_AT[name] + j:PARAM_AT[name] + j + 1]
            return params[:, bass.ds(j + PARAM_AT[name], 1)]

        def T(r, n=TOK):
            return temps[:, r, 0:n]

        accs = ctx.enter_context(nc.psum_tensor("accs", [P, 2, 2, 512], F32))
        misc = ctx.enter_context(nc.psum_tensor("misc", [P, 4, 512], F32))
        stat = misc[:, 0:2, 0:HALF]

        def acc(a):
            return accs[:, a, :, 0:HALF]

        def halves(ap):
            return ap.rearrange("p (h n) -> p h n", h=2)

        def acc_pieces(a):
            return [accs[:, a, 0, 0:HALF], accs[:, a, 1, 0:SEQ - HALF],
                    accs[:, a, 1, SEQ - HALF:HALF].rearrange("p (b t) -> p b t", b=NB)]

        def samples(ln, start, k):
            return ln[:, start:start + NB * (k - 1 + TS)].rearrange("p (b t) -> p b t", b=NB)

        def line_pieces(ln, k):
            return [ln[:, k - 1:k - 1 + HALF], ln[:, k - 1 + HALF:k - 1 + SEQ],
                    samples(ln, k - 1 + SEQ, k)[:, :, k - 1:]]

        def conv_pieces(cv, k):
            return [cv[:, 0:HALF], cv[:, HALF:SEQ], samples(cv, SEQ, k)[:, :, k - 1:]]

        w_landed = [sem(f"w_landed{s}") for s in range(SLOTS)]
        w_hi = [sem(f"w_hi{s}") for s in range(SLOTS)]
        w_lo = [sem(f"w_lo{s}") for s in range(SLOTS)]
        acc_full = [sem(f"acc_full{a}") for a in range(2)]
        acc_free = [sem(f"acc_free{a}") for a in range(2)]

        block = ctx.enter_context(nc.Block())

        def w_src(name, i, s):
            if name in ("A", "VU", "X"):
                return ins["w_in_main"], i * 4 + ({"A": 0, "VU": 8, "X": 16}[name] + s)
            if name == "Z":
                return ins["w_in_z"], i * 4 + s
            if name in ("G0", "G1", "G2"):
                g = int(name[1])
                if s % 2 == 0:
                    return ins["w_gate"], i * 2 + (g * KD + s // 2)
                return ins[("conf_w_out", "ssm_w_out", "gmlp_w_out")[g]], i * 2 + s // 2
            if name == "WO":
                return ins["w_o"], i * 4 + s
            if name in ("U1", "U2"):
                return ins["ffn_w_up"], i * 4 + ((0 if name == "U1" else 2 * FFA) + s)
            return ins["ffn_w_down1" if name == "D1" else "ffn_w_down2"], i * 4 + s

        def load_quad(sp, p, i):
            for s in range(SLOTS):
                src, j = w_src(p.name, i, s)
                n = p.kb[s] * P
                wait(sp, w_lo[s], i + p.quad0)
                ap = src[j] if isinstance(j, int) else src[bass.ds(j, 1)].rearrange("o p n -> (o p) n")
                sp.dma_start(w_raw[:, s, 0:n], ap).then_inc(w_landed[s], 16)

        def load_phase(sp, name, first=0):
            p = ph[name]
            loop(sp, first, p.quads, lambda i: load_quad(sp, p, i))

        def split_hi(act, p, i, s):
            n = p.kb[s] * P
            act.wait_ge(w_landed[s], i * 16 + (p.quad0 + 1) * 16)
            act.activation(w_split[:, s, 0, 0:n], w_raw[:, s, 0:n], ACT.Copy).then_inc(w_hi[s], 1)

        def split_lo(pool, p, i, s):
            n = p.kb[s] * P
            pool.wait_ge(w_hi[s], i + (p.quad0 + 1))
            pool.tensor_tensor(w_split[:, s, 1, 0:n], w_raw[:, s, 0:n], w_split[:, s, 0, 0:n].bitcast(F32),
                               ALU.subtract).then_inc(w_lo[s], 1)

        def head_groups():
            out, h = [], 0
            for n in HEADS_AFTER:
                out.append(range(h, h + n))
                h += n
            assert h == HEADS
            return out

        def act_quad(act, p, i, ahead, evac, between=None):
            for s in range(p.per_block - 1, SLOTS, p.per_block):
                a = p.acc(s)
                act.wait_ge(acc_full[a], p.pair(i, s) + 1)
                evac(i, s)
                if ahead is not None:
                    for r in range(s + 1 - p.per_block, s + 1):
                        split_hi(act, ahead[0], ahead[1], r)
                if between is not None:
                    between(i, s)

        def after(p):
            at = order.index(p.name)
            return (ph[order[at + 1]], 0) if at + 1 < len(order) else None

        def act_phase(act, name, evac, unroll=False, between=None):
            p = ph[name]
            if unroll:
                for i in range(p.quads - 1):
                    act_quad(act, p, i, (p, i + 1), evac, between)
            else:
                loop(act, 0, p.quads - 1, lambda i: act_quad(act, p, i, (p, i + 1), evac, between))
            act_quad(act, p, p.quads - 1, after(p), evac, between)

        def pe_quad(pe, p, i, rhs, ready=None, between=None):
            for s in range(SLOTS):
                a = p.acc(s)
                first, last = s % p.per_block == 0, s % p.per_block == p.per_block - 1
                pe.wait_ge(w_lo[s], i + (p.quad0 + 1))
                if first:
                    wait(pe, acc_free[a], p.pair(i, s))
                for k in range(p.kb[s]):
                    if ready is not None:
                        ready(s, k)
                    for n, (wp, xp) in enumerate(((0, 0), (0, 1), (1, 0))):
                        for half in range(2):
                            mm = pe.matmul(accs[:, a, half, 0:HALF], w_split[:, s, wp, k * P:(k + 1) * P],
                                           rhs(s, k, xp, half), start=(first and k == 0 and n == 0),
                                           stop=(last and k == p.kb[s] - 1 and n == 2))
                if last:
                    mm.then_inc(acc_full[a], 1)
                if between is not None:
                    between(s)

        def pe_phase(pe, name, rhs, ready=None):
            p = ph[name]
            if ready is not None:
                pe_quad(pe, p, 0, rhs, ready)
            loop(pe, 0 if ready is None else 1, p.quads, lambda i: pe_quad(pe, p, i, rhs))

        def tokens(half):
            return slice(half * HALF, (half + 1) * HALF)

        def h_rhs(s, k, part, half):
            return h_split[:, k, part, tokens(half)]

        def gmlp_at(k):
            return k, 4 + k

        def conf_at(k):
            return 8 + k, 12 + k

        def ssm_at(k):
            return 16 + k, k

        def mixed_at(k):
            return (8 + k, 12 + k) if k < 4 else (k - 4, k)

        def parts_of(at):
            return lambda j: (branch[:, at(j)[0]], branch[:, at(j)[1]])

        def h_parts(j):
            return h_split[:, j, 0], h_split[:, j, 1]

        def nth(name):
            return ("n1", "gl", "cf", "ns", "n2", "nf").index(name) + 1

        def branch_rhs(at):
            return lambda s, k, part, half: branch[:, at(k)[part], tokens(half)]

        def merge_rhs(at):
            return lambda s, k, part, half: (h_rhs if s % 2 == 0 else branch_rhs(at))(s, k, part, half)

        def down_rhs(kb):
            return lambda s, k, part, half: branch[:, 12 * part + kb * (s % 2) + k, tokens(half)]

        @block.sync
        def _(sp):
            for j in range(KD):
                sp.dma_start(xbc[:, j], ins["x"][:, j]).then_inc(sem(f"x_landed{j}"), 16)
                if j == 3:
                    sp.dma_start(consts[:, :, :], ins["consts"]).then_inc(sem("consts_landed"), 16)
                    sp.dma_start(params[:, :], ins["params"]).then_inc(sem("params_landed"), 16)
            load_quad(sp, ph["A"], 0)
            for j in range(4):
                sp.dma_start(samples(line_a[:, j], CKW - 1 + SEQ, CKW)[:, :, 0:CKW - 1],
                             ins["state_conv_a"][:, j]).then_inc(sem("hist_a_landed"), 16)
            sp.dma_start(hist_x[:, :, :, :], ins["state_conv_ssm"]).then_inc(sem("hist_landed"), 16)
            sp.dma_start(hist_f[:, :, :, :], ins["state_conv_ffn"]).then_inc(sem("hist_landed"), 16)
            sp.dma_start(mask_s[:, :, :], ins["mask_s"]).then_inc(sem("small_landed"), 16)
            sp.dma_start(w_dt[:, :, :], ins["w_dt"]).then_inc(sem("small_landed"), 16)
            sp.dma_start(bias_rows[:, 0], ins["ssm_dt_bias"].partition_broadcast(P)).then_inc(sem("small_landed"), 16)
            sp.dma_start(bias_rows[:, 1], ins["ssm_a_log"].partition_broadcast(P)).then_inc(sem("small_landed"), 16)
            load_quad(sp, ph["A"], 1)
            sp.dma_start(ws_t, ins["gmlp_w_s"]).then_inc(sem("gmlp_landed"), 16)
            sp.dma_start(bs.rearrange("p g n -> p (g n)"), ins["gmlp_b_s"].partition_broadcast(P))\
                .then_inc(sem("gmlp_landed"), 16)
            for b in range(NB):
                sp.dma_start(ws_s[TS * b:TS * b + TS].rearrange("p g (b t) -> p g b t", b=NB),
                             ins["gmlp_w_s"][0:TS, :, 0:TS].unsqueeze(2).to_broadcast([TS, 4, NB, TS]))\
                    .then_inc(sem("gmlp_landed"), 16)
            load_phase(sp, "VU")
            load_phase(sp, "X")
            sp.wait_ge(acc_free[1], 4)
            for j in range(4):
                sp.dma_start(outs["conv_a_p"][:, j], line_a[:, j, SEQ:SEQ + CKW - 1]).then_inc(sem("stored_a"), 16)
                sp.dma_start(outs["conv_a_s"][:, j], samples(line_a[:, j], CKW - 1 + SEQ, CKW)[:, :, TS:])\
                    .then_inc(sem("stored_a"), 16)
            load_quad(sp, ph["G2"], 0)
            sp.wait_ge(sem("vn_done"), 4)
            sp.dma_start(outs["gmlp_v_s"], v_sb[:, :, SEQ:TOK]).then_inc(sem("stored_v"), 16)
            load_phase(sp, "G2", first=1)
            sp.wait_ge(sem("tail_x"), 24)
            sp.dma_start(outs["conv_ssm"], tail_x[:, :, :]).then_inc(sem("stored_tails"), 16)
            load_phase(sp, "G0")
            load_phase(sp, "Z")
            sp.wait_ge(sem("chunk_sum"), 2 * NCH)
            for b in range(NB):
                r = b % 2
                if b >= 2:
                    sp.wait_ge(sem(f"h0_stored{r}"), 16 * (b // 2))
                sp.dma_start(h0[:, r], ins["state_ssm"][b]).then_inc(sem(f"h0_landed{r}"), 16)
                if b >= 1:
                    sp.wait_ge(sem("h0_new"), 2 * b)
                    sp.dma_start(outs["ssm_s"][b - 1], h0[:, 1 - r]).then_inc(sem(f"h0_stored{1 - r}"), 16)
            sp.wait_ge(sem("h0_new"), 2 * NB)
            sp.dma_start(outs["ssm_s"][NB - 1], h0[:, 1]).then_inc(sem("h0_stored1"), 16)
            sp.wait_ge(sem("chunk_state"), 2 * NCH)
            sp.dma_start(outs["ssm_p"], h_chunk[:, NCH - 1]).then_inc(sem("stored_h"), 16)
            load_phase(sp, "G1")
            for j in range(KD):
                sp.wait_ge(sem("ssm_f32"), j + 1)
                sp.dma_start(xbc[:, j], ins["x"][:, j]).then_inc(sem(f"x_landed{j}"), 16)
            for name in ("WO", "U1", "D1", "U2", "D2"):
                load_phase(sp, name)
            sp.wait_ge(sem("tail_f"), 2 * NF)
            sp.dma_start(outs["conv_ffn"], tail_f[:, :, :]).then_inc(sem("stored_tails"), 16)
            for j in range(KD):
                sp.wait_ge(sem("y_done"), j + 1)
                sp.dma_start(outs["y"][:, j], xbc[:, j]).then_inc(sem("stored_y"), 16)
            sp.wait_ge(sem("stored_a"), 16 * 8)
            sp.wait_ge(sem("stored_v"), 16)
            sp.wait_ge(sem("stored_tails"), 32)
            sp.wait_ge(sem("stored_h"), 16)
            sp.wait_ge(sem("h0_stored0"), 16 * NB // 2)
            sp.wait_ge(sem("h0_stored1"), 16 * NB // 2)
            sp.wait_ge(sem("stored_y"), 16 * KD)

        @block.gpsimd
        def _(pool):
            def pool_phase(name, work):
                p = ph[name]

                def quad(i, ahead):
                    for r in range(2):
                        work(i, r)
                        if ahead is not None:
                            split_lo(pool, ahead[0], ahead[1], 2 * r)
                            split_lo(pool, ahead[0], ahead[1], 2 * r + 1)
                loop(pool, 0, p.quads - 1, lambda i: quad(i, (p, i + 1)))
                quad(p.quads - 1, after(p))

            def nothing(i, r):
                pass

            def history(hist, f, par, k, conv, taps, done):
                wait(pool, conv, f * taps - taps)
                pool.tensor_copy(samples(temps[:, par], k - 1 + SEQ, k)[:, :, 0:k - 1], pick(hist, f)).then_inc(done, 1)

            def tails(tail, f, par, k, done):
                n = k - 1
                dst = pick(tail, f)
                pool.tensor_copy(dst[:, 0:n], temps[:, par, SEQ:SEQ + n]).then_inc(done, 1)
                pool.tensor_copy(dst[:, n:].rearrange("p (b t) -> p b t", b=NB),
                                 samples(temps[:, par], n + SEQ, k)[:, :, TS:]).then_inc(done, 1)

            pool.memset(eps[:, :], EPS).then_inc(sem("eps_set"), 1)
            pool.memset(line_a[:, :, 0:CKW - 1], 0.0).then_inc(sem("zeros_a"), 1)
            def lo_odd(name, dst):
                for j in range(1, KD, 2):
                    pool.wait_ge(sem(name + "_hi"), j + 1)
                    hi, lo = dst(j)
                    pool.tensor_tensor(lo, T(5), hi.bitcast(F32), ALU.subtract).then_inc(sem(name + "_lo_odd"), 1)

            split_lo(pool, ph["A"], 0, 0)
            split_lo(pool, ph["A"], 0, 1)
            lo_odd("n1", h_parts)
            split_lo(pool, ph["A"], 0, 2)
            split_lo(pool, ph["A"], 0, 3)
            pool_phase("A", nothing)
            pool.wait_ge(acc_free[1], 4)
            pool.memset(temps[:, 0:2, 0:SKW - 1], 0.0).then_inc(sem("zeros_x"), 1)
            pool.wait_ge(sem("hist_landed"), 32)
            history(hist_x, 0, 0, SKW, sem("x_conv"), SKW - 1, sem("x_hist"))
            history(hist_x, 1, 1, SKW, sem("x_conv"), SKW - 1, sem("x_hist"))
            shared = iter(range(1, CKW))

            def add_taps(n):
                for _, t in zip(range(n), shared):
                    pool.wait_ge(sem("tap_product"), t + 1)
                    if t > 1:
                        pool.wait_ge(sem("tap_added"), t - 1)
                    pool.tensor_tensor(ca[:, CONF_SHARED, 0:SEQ], ca[:, CONF_SHARED, 0:SEQ], tap_ring[:, t % RING],
                                       ALU.add).then_inc(sem("tap_added"), 1)
            pool_phase("VU", lambda i, r: add_taps(POOL_TAPS[0]))

            def x_work(i, r):
                p = ph["X"]
                for par in range(2):
                    f = 4 * i + 2 * r + par
                    pool.wait_ge(acc_free[par], p.pair(i, 2 * r) + 1)
                    tails(tail_x, f, par, SKW, sem("tail_x"))
                    if f + 2 < 12:
                        history(hist_x, f + 2, par, SKW, sem("x_conv"), SKW - 1, sem("x_hist"))
            p = ph["X"]
            for i in range(p.quads):
                for r in range(2):
                    x_work(i, r)
                    add_taps(POOL_TAPS[1])
                    q, j = (p, i + 1) if i + 1 < p.quads else after(p)
                    split_lo(pool, q, j, 2 * r)
                    split_lo(pool, q, j, 2 * r + 1)

            def merge(name, n0):
                p = ph[name]

                def work(i, r):
                    j = i * 2 + r
                    pool.wait_ge(acc_free[0], p.pair(i, 2 * r) + 1)
                    pool.wait_ge(acc_free[1], p.pair(i, 2 * r) + 1)
                    if n0 == 0:
                        pool.tensor_tensor(pick(mixed, j), T(r), T(2), ALU.mult).then_inc(sem("merged"), 1)
                    else:
                        pool.tensor_tensor(T(2), T(r), T(2), ALU.mult).then_inc(sem("gated"), 1)
                        pool.wait_ge(sem("gated"), j + (n0 - 8 + 1))
                        pool.tensor_tensor(pick(mixed, j), pick(mixed, j), T(2), ALU.add).then_inc(sem("merged"), 1)
                pool_phase(name, work)

            pool.wait_ge(sem("v_turned"), 5)
            pool.wait_ge(sem("stored_v"), 16)
            add_taps(CKW)
            merge("G2", 0)
            merge("G0", 8)

            pool.wait_ge(sem("s_exp"), 2)
            for b in range(NB):
                pool.wait_ge(sem("s_off"), b + 1)
                for g in range(2):
                    hv = h0[:, b % 2, g * 512:(g + 1) * 512].rearrange("p (h d) -> p h d", h=8)
                    last = T(5, 512).rearrange("p (h i) -> p h i", h=HEADS)[:, g * 8:(g + 1) * 8,
                                                                            TS * b + TS - 1:TS * b + TS]
                    pool.tensor_tensor(hv, hv, last.to_broadcast([P, 8, HD]), ALU.mult).then_inc(sem("h0_decayed"), 1)

            pool_phase("Z", nothing)
            pool.wait_ge(sem("stored_h"), 16)
            lo_odd("ssm", parts_of(ssm_at))
            merge("G1", 16)
            pool_phase("WO", nothing)
            lo_odd("n2", h_parts)
            pool.memset(temps[:, 0:2, 0:FKW - 1], 0.0).then_inc(sem("zeros_f"), 1)
            history(hist_f, 0, 0, FKW, sem("f_conv"), FKW, sem("f_hist"))
            history(hist_f, 1, 1, FKW, sem("f_conv"), FKW, sem("f_hist"))

            def up(name, f0):
                p = ph[name]

                def work(i, r):
                    f = i * 2 + (f0 + r)
                    pool.wait_ge(acc_free[0], p.pair(i, 2 * r) + 1)
                    tails(tail_f, f, r, FKW, sem("tail_f"))
                    if not (isinstance(f, int) and f + 2 >= NF):
                        history(hist_f, i * 2 + (f0 + r + 2), r, FKW, sem("f_conv"), FKW, sem("f_hist"))
                pool_phase(name, work)
            up("U1", 0)
            pool_phase("D1", nothing)
            up("U2", FFA)
            pool_phase("D2", nothing)

        @block.scalar
        def _(act):
            def hi_blocks(name, n, src, dst):
                for j in range(n):
                    act.wait_ge(sem(name + "_f32"), j + 1)
                    act.activation(dst(j), src(j), ACT.Copy).then_inc(sem(name + "_hi"), 1)

            def root(name, width):
                act.wait_ge(sem("rms_sum"), nth(name))
                act.activation(rms[:, 0], misc[:, 3, 0:6], ACT.Sqrt, bias=eps[:, 0:1], scale=1.0 / width)\
                    .then_inc(sem("rms_root"), 1)

            for j in range(KD):
                act.wait_ge(sem(f"x_landed{j}"), 16)
                if j >= 2:
                    act.wait_ge(sem("n1_added"), max(j - 2, 1))
                act.activation(T(j % 2), xbc[:, j], ACT.Square).then_inc(sem("n1_sq"), 1)
            act.wait_ge(sem("eps_set"), 1)
            root("n1", D)
            split_hi(act, ph["A"], 0, 0)
            split_hi(act, ph["A"], 0, 1)
            hi_blocks("n1", KD, lambda j: T(4 + j % 2), lambda j: h_split[:, j, 0])
            split_hi(act, ph["A"], 0, 2)
            split_hi(act, ph["A"], 0, 3)

            def evac_a(i, s):
                if s % 2 == 0:
                    wait(act, acc_free[1], 2 * i + s // 2 - 1)
                    act.activation(halves(T(s // 2)), acc(0), ACT.Sigmoid).then_inc(acc_free[0], 1)
            act_phase(act, "A", evac_a, unroll=True)

            def evac_vu(i, s):
                a = s % 2
                act.activation(halves((v_sb if i == 0 else u_sb)[:, s]), acc(a), ACT.Gelu_apprx_tanh)\
                    .then_inc(acc_free[a], 1)
            shared = iter(range(CKW))

            def tap_products(n):
                for _, t in zip(range(n), shared):
                    src, w = line_a[:, CONF_SHARED, t:t + SEQ], param("conf_w", CONF_SHARED * CKW + t)
                    if t == 0:
                        act.wait_ge(acc_free[1], 4)
                        act.wait_ge(sem("zeros_a"), 1)
                        act.activation(ca[:, CONF_SHARED, 0:SEQ], src, ACT.Identity, bias=param("conf_b", CONF_SHARED),
                                       scale=w).then_inc(sem("tap_product"), 1)
                        continue
                    if t > RING:
                        act.wait_ge(sem("tap_added"), t - RING)
                    act.activation(tap_ring[:, t % RING], src, ACT.Copy, scale=w).then_inc(sem("tap_product"), 1)
            act_phase(act, "VU", evac_vu, unroll=True, between=lambda i, s: tap_products(ACT_TAPS[0]))

            def to_line(a, r, k):
                for n, (src, dst) in enumerate(zip(acc_pieces(a), line_pieces(temps[:, r], k))):
                    ins_ = act.activation(dst, src, ACT.Copy)
                ins_.then_inc(acc_free[a], 1)

            def silu_x(j):
                cv = temps[:, 2 + j % 2]
                act.wait_ge(sem("x_conv"), (SKW - 1) * (j + 1))
                act.activation(xbc[:, j, 0:SEQ], cv[:, 0:SEQ], ACT.Silu, bias=param("ssm_b", j))
                act.activation(xbc[:, j, SEQ:TOK].rearrange("p (b t) -> p b t", b=NB),
                               conv_pieces(cv, SKW)[2], ACT.Silu, bias=param("ssm_b", j)).then_inc(sem("xbc_done"), 1)

            def evac_x(i, s):
                b = 4 * i + s
                wait(act, sem("x_conv"), (SKW - 1) * (b - 1))
                wait(act, sem("tail_x"), 2 * (b - 1))
                if b < 2:
                    act.wait_ge(acc_free[1], 4)
                to_line(s % 2, s % 2, SKW)
                act.wait_ge(acc_free[s % 2], ph["X"].pair(i, s) + 1)
                act.wait_ge(sem("x_hist"), b + 1)
                if b < 2:
                    act.wait_ge(sem("zeros_x"), 1)
                n = line(SKW) - SKW + 1
                act.activation(T(2 + s % 2, n), temps[:, s % 2, 0:n], ACT.Copy, scale=param("ssm_w", b * SKW))\
                    .then_inc(sem("x_first"), 1)
                if b >= 1:
                    silu_x(b - 1)
                if (i, s) == (2, 0):
                    root("gl", CONF)
            act_phase(act, "X", evac_x, unroll=True, between=lambda i, s: tap_products(ACT_TAPS[1]))
            tap_products(CKW)
            silu_x(11)

            act.wait_ge(sem("dt_abs"), 1)
            act.activation(small[:, EXPN], small[:, ABS], ACT.Exp, scale=-1.0).then_inc(sem("dt_exp"), 1)
            act.activation(bias_rows[:, 1], bias_rows[:, 1], ACT.Exp).then_inc(sem("dt_exp"), 1)
            for c in range(NCH + 1):
                act.wait_ge(sem("v_turned"), c + 1)
                if c < NCH:
                    act.activation(vnat[:, c], misc[:, c], ACT.Copy).then_inc(sem("vnat"), 1)
                else:
                    act.activation(vnat[0:SMP, c], misc[0:SMP, 0], ACT.Copy).then_inc(sem("vnat"), 1)
            act.wait_ge(sem("tap_added"), CKW - 1)
            hi_blocks("gm", 4, lambda j: u_sb[:, j], lambda j: branch[:, gmlp_at(j)[0]])

            def evac_branch(name, g, n0):
                def evac(i, s):
                    j = i * 2 + s // 2
                    if s % 2 == 0:
                        wait(act, sem("merged"), j + (n0 - 1))
                        act.activation(halves(T(s // 2)), acc(0), ACT.Sigmoid,
                                       bias=param("b_gate", i * 2 + (8 * g + s // 2))).then_inc(acc_free[0], 1)
                    else:
                        wait(act, sem("merged"), j + n0)
                        act.activation(halves(T(2)), acc(1), ACT.Copy).then_inc(acc_free[1], 1)
                return evac

            def beside_g2(i, s):
                if (i, s) == (0, 2):
                    act.wait_ge(sem("to_end_arg"), 2)
                    act.activation(small[:, TO_END], small[:, TO_END], ACT.Exp).then_inc(sem("dec_exp"), 1)
                    act.activation(small[:, DECAY, 0:NCH * HEADS], small[:, TOTAL, 0:NCH * HEADS], ACT.Exp)\
                        .then_inc(sem("dec_exp"), 1)
                if (i, s) == (0, 3):
                    act.wait_ge(sem("a_turned"), 1)
                    act.activation(a_rows[:, 0:SEQ], misc[0:HEADS, 2], ACT.Copy)
                    act.activation(a_rows[:, SEQ:TOK], misc[0:HEADS, 3, 256:256 + SMP], ACT.Copy)\
                        .then_inc(sem("a_rows"), 1)
                if (i, s) == (1, 2):
                    root("cf", CONF)
                if i == 2:
                    act.wait_ge(sem("cf_scaled"), s + 1)
                    act.wait_ge(sem("stored_a"), 16 * 8)
                    act.activation(ca[:, s], ca[:, s], ACT.Silu, bias=param("conf_ln_b", s))\
                        .then_inc(sem("cf_f32"), 1)
                    act.wait_ge(sem("cf_f32"), s + 1)
                    act.activation(branch[:, conf_at(s)[0]], ca[:, s], ACT.Copy).then_inc(sem("cf_hi"), 1)
                if i == 3:
                    act.wait_ge(sem("cf_lo"), 4)
                    act.wait_ge(sem("xb_turned"), s + 1)
                    act.activation(bnat[:, s], misc[:, 2, 0:2 * STATE], ACT.Copy).then_inc(sem("bnat"), 1)
            act.wait_ge(sem("xbc_done"), 12)
            act.wait_ge(sem("tail_x"), 24)
            p = ph["G2"]
            ev = evac_branch("G2", 2, 0)
            for i in range(p.quads):
                act_quad(act, p, i, (p, i + 1) if i + 1 < p.quads else after(p), ev, beside_g2)

            groups = head_groups()

            def beside_g0(i, s):
                for h in groups[4 * i + s]:
                    act.wait_ge(sem("diff"), h + 1)
                    act.activation(T(4 + h % 2, SEQ), T(4 + h % 2, SEQ), ACT.Exp).then_inc(sem("pair_decay"), 1)
                    if h >= 2:
                        act.wait_ge(sem("y_head"), h - 1)
                    act.activation(c_dec[:, h % 2], misc[:, h % 2], ACT.Exp).then_inc(sem("a_exp"), 1)
            ev = evac_branch("G0", 0, 8)
            p = ph["G0"]
            for i in range(p.quads):
                act_quad(act, p, i, (p, i + 1) if i + 1 < p.quads else after(p), ev, beside_g0)
            act.wait_ge(sem("xb_turned"), NCH + 1)
            act.activation(bnat_s, misc[0:SMP, 2, 0:2 * STATE], ACT.Copy).then_inc(sem("bnat"), 1)
            act.wait_ge(sem("merged"), 16)
            act.wait_ge(sem("s_diff"), 1)
            act.activation(temps[0:SMP, 4, 0:512], temps[0:SMP, 4, 0:512], ACT.Exp).then_inc(sem("s_exp"), 1)
            act.activation(T(5, 512), misc[:, 0], ACT.Exp).then_inc(sem("s_exp"), 1)

            def evac_z(i, s):
                b = 4 * i + s
                wait(act, sem("yz"), b - 1)
                act.activation(halves(T(s % 2)), acc(s % 2), ACT.Silu).then_inc(acc_free[s % 2], 1)
            act_phase(act, "Z", evac_z, unroll=True)
            root("ns", D)
            hi_blocks("ssm", KD, lambda j: T(4 + j % 2), lambda j: branch[:, ssm_at(j)[0]])
            ev = evac_branch("G1", 1, 16)
            p = ph["G1"]
            act_quad(act, p, 0, (p, 1), ev)
            loop(act, 1, 3, lambda i: act_quad(act, p, i, (p, i + 1), ev))
            act_quad(act, p, 3, after(p), ev)
            for j in range(KD):
                act.wait_ge(sem("merged"), 17 + j)
                act.activation(branch[:, mixed_at(j)[0]], mixed[:, j], ACT.Copy).then_inc(sem("mx_hi"), 1)
            act_phase(act, "WO", lambda i, s: None, unroll=True)
            root("n2", D)
            hi_blocks("n2", KD, lambda j: T(4 + j % 2), lambda j: h_split[:, j, 0])

            def up(name, f0):
                p = ph[name]


                def quad(i, ahead):
                    for r in range(2):
                        f = i * 2 + (f0 + r)
                        s = 2 * r
                        act.wait_ge(acc_full[0], p.pair(i, s) + 1)
                        wait(act, sem("f_conv"), i * (2 * FKW) + FKW * (f0 + r - 1))
                        wait(act, sem("tail_f"), i * 4 + 2 * (f0 + r - 1))
                        to_line(0, r, FKW)
                        split_hi(act, ahead[0], ahead[1], s)
                        act.wait_ge(sem("f_conv"), i * (2 * FKW) + FKW * (f0 + r + 1))
                        act.activation(T(2 + r, SEQ + NB * (FKW - 1 + TS)), T(2 + r, SEQ + NB * (FKW - 1 + TS)),
                                       ACT.Silu, bias=param("ffn_b", f)).then_inc(sem("f_silu"), 1)
                        act.wait_ge(acc_full[1], p.pair(i, s) + 1)
                        split_hi(act, ahead[0], ahead[1], s + 1)
                        act.wait_ge(acc_free[1], p.pair(i, s) + 1)
                        act.activation(pick(branch, i * 2 + r), T(4 + r), ACT.Copy).then_inc(sem("f_hi"), 1)
                if f0 == 0:
                    act.wait_ge(sem("zeros_f"), 1)
                    quad(0, (p, 1))
                    loop(act, 1, p.quads - 1, lambda i: quad(i, (p, i + 1)))
                else:
                    loop(act, 0, p.quads - 1, lambda i: quad(i, (p, i + 1)))
                quad(p.quads - 1, after(p))
            up("U1", 0)
            act_phase(act, "D1", lambda i, s: None)
            up("U2", FFA)
            act_phase(act, "D2", lambda i, s: None)
            root("nf", D)

        @block.tensor
        def _(pe):
            def channel_sum(src, done):
                for half in range(2):
                    mm = pe.matmul(misc[:, half, 0:HALF], ones, src[:, tokens(half)], start=True, stop=True)
                mm.then_inc(done, 1)

            groups = [(h * HALF + o, n) for h in range(2) for o, n in ((0, P), (P, P), (HALF - P, HALF - 2 * P))]

            def token_sum(src):
                for c, (t0, _) in enumerate(groups):
                    mm = pe.matmul(misc[:, 3, c:c + 1], src[:, t0:t0 + P], ones[:, 0:1], start=True, stop=True)
                mm.then_inc(sem("rms_sum"), 1)

            def spread_rms(name):
                pe.wait_ge(sem("rms_inverse"), nth(name))
                for c, (t0, n) in enumerate(groups):
                    at = t0 % HALF + P - n
                    mm = pe.matmul(misc[:, c // 3, at:at + n], rms[:, 1, c:c + 1].to_broadcast([P, P]),
                                   ident[:, P - n:P], start=True, stop=True)
                mm.then_inc(sem("rms_spread"), 1)

            def lo_ready(name, slots=(0,)):
                def ready(s, k):
                    if s == slots[0]:
                        pe.wait_ge(sem(name + ("_lo", "_lo_odd")[k % 2]), k // 2 + 1)
                return ready

            def in_order(name, slots):
                def ready(s, k):
                    if s in slots:
                        pe.wait_ge(sem(name), k + 1 + slots[s])
                return ready

            pe.wait_ge(sem("consts_landed"), 16)
            pe.wait_ge(sem("n1_added"), KD - 1)
            token_sum(T(2))
            spread_rms("n1")
            p = ph["A"]
            pe_quad(pe, p, 0, h_rhs, lo_ready("n1"))
            pe_quad(pe, p, 1, h_rhs)
            pe_phase(pe, "VU", h_rhs)
            p = ph["X"]
            pe_quad(pe, p, 0, h_rhs)
            pe.wait_ge(sem("gl_sum"), 1)
            channel_sum(T(4), sem("gl_mean"))
            pe_quad(pe, p, 1, h_rhs)
            pe.wait_ge(sem("gl_sq"), 1)
            token_sum(T(4))
            pe_quad(pe, p, 2, h_rhs)
            spread_rms("gl")
            pe.wait_ge(sem("dt_w"), 1)
            for c in range(NCH):
                for k in range(KD):
                    for n, (wp, xp) in enumerate(((0, 0), (0, 1), (1, 0))):
                        pe.matmul(misc[:, 2, c * HEADS:(c + 1) * HEADS], h_split[:, k, xp, c * CH:(c + 1) * CH],
                                  w_dt_split[:, wp, k], start=(k == 0 and n == 0), stop=(k == KD - 1 and n == 2))
            for k in range(KD):
                for part in range(2):
                    mm = pe.matmul(misc[0:SMP, 2, NCH * HEADS:(NCH + 1) * HEADS],
                                   h_split[:, k, part, SEQ:TOK].bitcast(F32), w_dt[:, k],
                                   start=(k == 0 and part == 0), stop=(k == KD - 1 and part == 1))
            mm.then_inc(sem("dt_raw"), 1)
            pe.wait_ge(sem("vn_done"), 4)
            for c in range(NCH):
                if c == 2:
                    pe.wait_ge(sem("dt_read"), 1)
                for j in range(4):
                    mm = pe.transpose(misc[:, c, j * P:(j + 1) * P], v_sb[:, j, c * CH:(c + 1) * CH], ident)
                mm.then_inc(sem("v_turned"), 1)
            pe.wait_ge(sem("vnat"), 1)
            for j in range(4):
                mm = pe.transpose(misc[0:SMP, 0, j * P:(j + 1) * P], v_sb[:, j, SEQ:TOK], ident)
            mm.then_inc(sem("v_turned"), 1)
            pe.wait_ge(sem("vnat"), NCH + 1)
            pe.wait_ge(sem("ws_masked"), 2)
            for g in range(4):
                b0 = 2 * (g % 2)
                if g >= 2:
                    pe.wait_ge(sem("mix_read"), g - 1)
                for c in range(NCH):
                    pe.matmul(misc[:, b0, c * CH:(c + 1) * CH], vnat[:, c, g * P:(g + 1) * P], ws_t[:, g],
                              start=True, stop=True)
                pe.matmul(misc[:, b0 + 1, 0:SMP], vnat[0:SMP, NCH, g * P:(g + 1) * P], ws_s[:, g],
                          start=True, stop=True).then_inc(sem("mix"), 1)
            n4 = NCH * HEADS

            def cumulate():
                pe.wait_ge(sem("adt"), 1)
                pe.matmul(misc[:, 3, 0:n4], tri, small[:, ADT, 0:n4], start=True, stop=True)
                pe.matmul(misc[0:SMP, 3, n4:n4 + HEADS], mask_s[:, 0], small[0:SMP, ADT, n4:n4 + HEADS],
                          start=True, stop=True)
                pe.matmul(misc[:, 3, 80:80 + n4], ones, small[:, ADT, 0:n4], start=True, stop=True)
                pe.matmul(misc[0:SMP, 3, 80 + n4:160], mask_s[:, 1], small[0:SMP, ADT, n4:n4 + HEADS],
                          start=True, stop=True).then_inc(sem("cum"), 1)

            def turn_rows():
                pe.wait_ge(sem("to_end_arg"), 2)
                for c in range(NCH):
                    pe.transpose(misc[0:HEADS, 2, c * CH:(c + 1) * CH], small[:, A_CUM, c * HEADS:(c + 1) * HEADS],
                                 ident)
                pe.transpose(misc[0:HEADS, 3, 256:256 + SMP], small[0:SMP, A_CUM, n4:n4 + HEADS],
                             ident[0:SMP, 0:SMP]).then_inc(sem("a_turned"), 1)

            def turn_xb(c):
                if c == 0:
                    pe.wait_ge(sem("cf_scaled"), 4)
                    pe.wait_ge(sem("a_rows"), 1)
                elif c < NCH:
                    pe.wait_ge(sem("xdt"), 2 * c)
                    pe.wait_ge(sem("bnat"), c)
                rows, cols = (P, slice(c * CH, (c + 1) * CH)) if c < NCH else (SMP, slice(SEQ, TOK))
                for j in range(KD):
                    pe.transpose(misc[0:rows, j // 4, (j % 4) * P:(j % 4 + 1) * P], xbc[:, j, cols], ident)
                for g in range(2):
                    mm = pe.transpose(misc[0:rows, 2, g * P:(g + 1) * P], xbc[:, 8 + g, cols], ident)
                mm.then_inc(sem("xb_turned"), 1)

            def chunk_sum(c):
                if c == 0:
                    pe.wait_ge(sem("xdt"), 2 * NCH)
                    pe.wait_ge(sem("bnat"), NCH)
                pe.wait_ge(sem("xw"), c + 1)
                for g in range(2):
                    b0 = 2 * (c % 2) + g
                    if c >= 2:
                        pe.wait_ge(sem("chunk_state"), 2 * (c - 2) + g + 1)
                    pe.matmul(misc[:, b0], bnat[:, c, g * STATE:(g + 1) * STATE], xw[:, c % 2, g * 512:(g + 1) * 512],
                              start=True, stop=True).then_inc(sem("chunk_sum"), 1)

            def cb_products():
                for g in range(2):
                    pe.wait_ge(sem("chunk_state"), 4 + 1 + g)
                    for c in range(NCH):
                        cols = slice(c * CH, (c + 1) * CH)
                        mm = pe.matmul(misc[:, g, cols], xbc[:, 8 + g, cols], xbc[:, 10 + g, cols],
                                       start=True, stop=True)
                    mm.then_inc(sem("cb"), 1)

            def spread(h):
                if h == 0:
                    pe.wait_ge(sem("cbm"), 2)
                if h >= 2:
                    pe.wait_ge(sem("a_exp"), h - 1)
                pe.matmul(misc[:, h % 2], ident[0:HEADS, h:h + 1].to_broadcast([HEADS, P]), a_rows[:, 0:SEQ],
                          start=True, stop=True).then_inc(sem("a_spread"), 1)

            def y_head(h):
                b0, rows = 2 + (h // 2) % 2, slice((h % 2) * HD, (h % 2 + 1) * HD)
                if h == 0:
                    pe.wait_ge(sem("chunk_state"), 2 * NCH)
                if h % 2 == 0 and h >= 4:
                    pe.wait_ge(sem("y_sum"), h // 2 - 1)
                pe.wait_ge(sem("mix_head"), h + 1)
                pe.wait_ge(sem("c_decayed"), h + 1)
                for c in range(NCH):
                    cols = slice(c * CH, (c + 1) * CH)
                    mm = pe.matmul(misc[rows, b0, cols], xdt[:, c, h * HD:(h + 1) * HD], T(4 + h % 2, SEQ)[:, cols],
                                   start=True, stop=(c == 0))
                    if c:
                        mm = pe.matmul(misc[rows, b0, cols], h_chunk[:, c - 1, h * HD:(h + 1) * HD],
                                       c_dec[:, h % 2, cols], start=False, stop=True)
                mm.then_inc(sem("y_head"), 1)

            def beside_g2(i):
                def between(s):
                    if (i, s) == (0, 1):
                        cumulate()
                    if (i, s) == (0, 2):
                        turn_rows()
                    if (i, s) == (0, 3):
                        pe.wait_ge(sem("cf_sum"), 1)
                        channel_sum(T(4), sem("cf_mean"))
                    if (i, s) == (1, 1):
                        pe.wait_ge(sem("a_rows"), 1)
                        pe.wait_ge(sem("cf_sq"), 1)
                        token_sum(T(4))
                    if (i, s) == (1, 3):
                        spread_rms("cf")
                    if i == 3:
                        turn_xb(s)
                return between
            p = ph["G2"]
            rhs = merge_rhs(gmlp_at)
            for i in range(p.quads):
                pe_quad(pe, p, i, rhs, in_order("gm_lo", {1: 0}) if i == 0 else None, beside_g2(i))

            heads = head_groups()

            def beside_g0(i):
                def between(s):
                    if i == 0:
                        chunk_sum(s)
                    if (i, s) == (1, 0):
                        cb_products()
                    k = 4 * i + s
                    for h in heads[k - 1] if k else ():
                        y_head(h)
                    for h in heads[k]:
                        spread(h)
                return between
            p = ph["G0"]
            rhs = merge_rhs(conf_at)
            for i in range(p.quads):
                pe_quad(pe, p, i, rhs, in_order("cf_lo", {1: 0}) if i == 0 else None, beside_g0(i))
            for h in heads[-1]:
                y_head(h)
            pe.wait_ge(sem("a_exp"), HEADS)
            pe.wait_ge(sem("y_sum"), 8)
            turn_xb(NCH)
            for g in range(2):
                mm = pe.matmul(misc[0:SMP, 3, g * SMP:(g + 1) * SMP], xbc[:, 8 + g, SEQ:TOK], xbc[:, 10 + g, SEQ:TOK],
                               start=True, stop=True)
            mm.then_inc(sem("cb"), 1)
            pe.wait_ge(sem("xdt"), 2 * NCH + 2)
            pe.wait_ge(sem("bnat"), NCH + 1)
            pe.wait_ge(sem("cbm"), 3)
            for h in range(HEADS):
                mm = pe.matmul(misc[:, 0, h * SMP:(h + 1) * SMP], ident[0:HEADS, h:h + 1].to_broadcast([HEADS, P]),
                               a_rows[:, SEQ:TOK], start=True, stop=True)
            mm.then_inc(sem("s_spread"), 1)
            pe.wait_ge(sem("s_mix"), 1)
            for h in range(HEADS):
                rows = slice((h % 2) * HD, (h % 2 + 1) * HD)
                mm = pe.matmul(misc[rows, 1, (h // 2) * SMP:(h // 2 + 1) * SMP], xdt_s[:, h * HD:(h + 1) * HD],
                               temps[0:SMP, 4, h * SMP:(h + 1) * SMP], start=True, stop=True)
            mm.then_inc(sem("s_diag"), 1)
            pe.wait_ge(sem("xw"), NCH + 1)
            for b in range(NB):
                pe.wait_ge(sem(f"h0_landed{b % 2}"), 16 * (b // 2 + 1))
                for j in range(KD):
                    g = j // 4
                    mm = pe.matmul(misc[:, 2, j * SMP + TS * b:j * SMP + TS * b + TS], h0[:, b % 2, j * P:(j + 1) * P],
                                   xbc[:, 10 + g, SEQ + TS * b:SEQ + TS * b + TS], start=True, stop=True)
                mm.then_inc(sem("s_off"), 1)
                pe.wait_ge(sem("b_masked"), b + 1)
                for g in range(2):
                    pe.wait_ge(sem("s_exp"), 2)
                    bank = 0 if g == 0 else 3
                    if b:
                        pe.wait_ge(sem("h0_new"), 2 * (b - 1) + g + 1)
                    pe.matmul(misc[:, bank], bm_s[:, b % 2, g * STATE:(g + 1) * STATE], xw_s[:, g * 512:(g + 1) * 512],
                              start=True, stop=True).then_inc(sem("s_sum"), 1)

            pe_phase(pe, "Z", h_rhs)
            pe.wait_ge(sem("yz_sq"), 1)
            token_sum(T(5))
            spread_rms("ns")
            pe_phase(pe, "G1", merge_rhs(ssm_at), lo_ready("ssm", (1,)))
            pe_phase(pe, "WO", branch_rhs(mixed_at), in_order("mx_lo", {0: 0}))
            pe.wait_ge(sem("x2_sq"), 1)
            token_sum(T(5))
            spread_rms("n2")
            pe_phase(pe, "U1", h_rhs, lo_ready("n2"))
            pe_phase(pe, "D1", down_rhs(FFA // 2), in_order("f_lo", {0: 0, 1: FFA // 2}))
            pe_phase(pe, "U2", h_rhs)
            pe_phase(pe, "D2", down_rhs(FFB // 2), in_order("f_lo", {0: FFA, 1: FFA + FFB // 2}))
            pe.wait_ge(sem("x3_sq"), 1)
            token_sum(T(5))
            spread_rms("nf")

        @block.vector
        def _(dve):
            chained = [0]

            def link(ins_):
                chained[0] += 1
                ins_.then_inc(sem("dve_chain"), 1)
                dve.wait_ge(sem("dve_chain"), chained[0])

            def operand(name, n, produce, tmp, lo):
                for j in range(n + 1):
                    if j < n:
                        if j >= 2:
                            dve.wait_ge(sem(name + ("_lo", "_lo_odd")[j % 2]), j // 2)
                        produce(j).then_inc(sem(name + "_f32"), 1)
                    if j % 2:
                        i = j - 1
                        dve.wait_ge(sem(name + "_hi"), i + 1)
                        hi, dst = lo(i)
                        dve.tensor_tensor(dst, tmp(i), hi.bitcast(F32), ALU.subtract).then_inc(sem(name + "_lo"), 1)

            def inverse(name):
                dve.wait_ge(sem("rms_root"), nth(name))
                dve.reciprocal(rms[:, 1], rms[:, 0]).then_inc(sem("rms_inverse"), 1)

            def rstd(name):
                inverse(name)
                dve.wait_ge(sem("rms_spread"), nth(name))

            for j in range(1, KD):
                dve.wait_ge(sem("n1_sq"), j + 1)
                if j >= 2:
                    dve.wait_ge(sem("n1_added"), j - 1)
                dve.tensor_tensor(T(2), T(0) if j == 1 else T(2), T(j % 2), ALU.add).then_inc(sem("n1_added"), 1)
            rstd("n1")
            dve.wait_ge(sem("params_landed"), 16)

            def scaled(name):
                return lambda j: dve.scalar_tensor_tensor(out=halves(T(4 + j % 2)), in0=halves(xbc[:, j]),
                                                          scalar=param(name, j), in1=stat, op0=ALU.mult, op1=ALU.mult)
            operand("n1", KD, scaled("norm1_g"), lambda j: T(4 + j % 2), h_parts)
            dve.wait_ge(sem("small_landed"), 16 * 4)
            link(dve.tensor_copy(w_dt_split[:, 0], w_dt[:, :, :]))
            dve.tensor_tensor(w_dt_split[:, 1], w_dt[:, :, :], w_dt_split[:, 0].bitcast(F32), ALU.subtract)\
                .then_inc(sem("dt_w"), 1)
            dve.wait_ge(sem("hist_a_landed"), 64)
            for b in range(4):
                dve.wait_ge(acc_full[1], b + 1)
                dve.wait_ge(acc_free[0], b + 1)
                for src, sig, dst in zip(acc_pieces(1), [T(b % 2)[:, 0:HALF], T(b % 2)[:, HALF:SEQ],
                                                         T(b % 2)[:, SEQ:].rearrange("p (b t) -> p b t", b=NB)],
                                         line_pieces(line_a[:, b], CKW)):
                    ins_ = dve.tensor_tensor(dst, src, sig, ALU.mult)
                ins_.then_inc(acc_free[1], 1)

            dve.wait_ge(acc_free[1], 4)
            dve.wait_ge(sem("zeros_a"), 1)
            taps = [(b, t) for b in range(4) for t in range(CKW)]

            def conf_taps(n):
                for _ in range(min(n, len(taps))):
                    b, t = taps.pop(0)
                    w = param("conf_w", b * CKW + t)
                    pieces = [(samples(line_a[:, b], CKW - 1 + SEQ, CKW)[:, :, t:t + TS],
                               ca[:, b, SEQ:TOK].rearrange("p (b t) -> p b t", b=NB))]
                    if b != CONF_SHARED:
                        pieces.insert(0, (line_a[:, b, t:t + SEQ], ca[:, b, 0:SEQ]))
                    for src, dst in pieces:
                        if t == 0:
                            ins_ = dve.tensor_scalar(dst, src, w, param("conf_b", b), ALU.mult, ALU.add)
                        else:
                            ins_ = dve.scalar_tensor_tensor(out=dst, in0=src, scalar=w, in1=dst,
                                                            op0=ALU.mult, op1=ALU.add)
                    link(ins_)

            def x_conv(f):
                par, n = f % 2, line(SKW) - SKW + 1
                dve.wait_ge(sem("x_first"), f + 1)
                cv = T(2 + par, n)
                for t in range(1, SKW):
                    src, w = temps[:, par, t:t + n], param("ssm_w", f * SKW + t)
                    if t > 1:
                        dve.wait_ge(sem("x_conv"), f * (SKW - 1) + t - 1)
                    dve.scalar_tensor_tensor(out=cv, in0=src, scalar=w, in1=cv, op0=ALU.mult, op1=ALU.add)\
                        .then_inc(sem("x_conv"), 1)

            def four_sum(src, done):
                link(dve.tensor_tensor(T(4), src[:, 0], src[:, 1], ALU.add))
                link(dve.tensor_tensor(T(4), T(4), src[:, 2], ALU.add))
                dve.tensor_tensor(T(4), T(4), src[:, 3], ALU.add).then_inc(done, 1)

            def center(src, name):
                dve.wait_ge(sem(name + "_mean"), 1)
                for j in range(4):
                    ins_ = dve.scalar_tensor_tensor(out=halves(src[:, j]), in0=stat, scalar=-1.0 / CONF,
                                                    in1=halves(src[:, j]), op0=ALU.mult, op1=ALU.add)
                link(ins_)
                dve.tensor_tensor(T(4), src[:, 0], src[:, 0], ALU.mult)
                for j in range(1, 4):
                    link(dve.tensor_tensor(T(5), src[:, j], src[:, j], ALU.mult))
                    ins_ = dve.tensor_tensor(T(4), T(4), T(5), ALU.add)
                    if j < 3:
                        link(ins_)
                ins_.then_inc(sem(name + "_sq"), 1)

            def scale(src, name, gain, done):
                dve.wait_ge(sem("rms_spread"), nth(name))
                for j in range(4):
                    dve.scalar_tensor_tensor(out=halves(src[:, j]), in0=halves(src[:, j]), scalar=param(gain, j),
                                             in1=stat, op0=ALU.mult, op1=ALU.mult).then_inc(done, 1)

            dve.wait_ge(sem("gmlp_landed"), 16 * GMLP_LOADS)
            dve.tensor_tensor(ws_t, ws_t, tri.unsqueeze(1).to_broadcast([P, 4, CH]), ALU.mult)\
                .then_inc(sem("ws_masked"), 1)
            dve.tensor_tensor(ws_s, ws_s, mask_s[:, 0].unsqueeze(1).to_broadcast([SMP, 4, SMP]), ALU.mult)\
                .then_inc(sem("ws_masked"), 1)
            conf_taps(50)
            dve.wait_ge(acc_free[0], 6)
            dve.wait_ge(acc_free[1], 6)
            four_sum(v_sb, sem("gl_sum"))
            for f in range(12):
                x_conv(f)
                conf_taps(4)
                if f == 4:
                    center(v_sb, "gl")
                if f == 8:
                    inverse("gl")
                if f == 9:
                    scale(v_sb, "gl", "gmlp_ln_g", sem("vn_scaled"))
                    dve.wait_ge(sem("vn_scaled"), 4)
                    for j in range(4):
                        dve.tensor_scalar(v_sb[:, j], v_sb[:, j], param("gmlp_ln_b", j), None, ALU.add)\
                            .then_inc(sem("vn_done"), 1)

            def sm(q):
                return small[:, q]

            def by_head(ap):
                return ap.rearrange("p (c h) -> p c h", h=HEADS)
            dve.memset(small[:, X_DT], 0.0).then_inc(sem("dve_chain"), 1)
            chained[0] += 1
            dve.wait_ge(sem("dve_chain"), chained[0])
            dve.wait_ge(sem("dt_raw"), 1)
            n4 = NCH * HEADS
            dve.tensor_tensor(by_head(small[:, X_DT, 0:n4]), by_head(misc[:, 2, 0:n4]),
                              bias_rows[:, 0].unsqueeze(1).to_broadcast([P, NCH, HEADS]), ALU.add)
            dve.tensor_tensor(small[0:SMP, X_DT, n4:], misc[0:SMP, 2, n4:n4 + HEADS], bias_rows[0:SMP, 0], ALU.add)\
                .then_inc(sem("dt_read"), 1)
            dve.wait_ge(sem("dt_read"), 1)
            link(dve.tensor_scalar(sm(ABS), sm(X_DT), -1.0, None, ALU.mult))
            dve.tensor_tensor(sm(ABS), sm(ABS), sm(X_DT), ALU.max).then_inc(sem("dt_abs"), 1)
            dve.wait_ge(sem("dt_exp"), 1)
            link(dve.tensor_scalar(sm(RATIO), sm(EXPN), 2.0, None, ALU.add))
            link(dve.reciprocal(sm(RATIO2), sm(RATIO)))
            link(dve.tensor_tensor(sm(RATIO), sm(EXPN), sm(RATIO2), ALU.mult))
            link(dve.tensor_tensor(sm(RATIO2), sm(RATIO), sm(RATIO), ALU.mult))
            link(dve.tensor_scalar(sm(POLY), sm(RATIO2), 1.0 / 17, None, ALU.mult))
            for d in range(15, 1, -2):
                link(dve.scalar_tensor_tensor(out=sm(POLY), in0=sm(POLY), scalar=1.0 / d, in1=sm(RATIO2),
                                              op0=ALU.add, op1=ALU.mult))
            link(dve.scalar_tensor_tensor(out=sm(POLY), in0=sm(POLY), scalar=1.0, in1=sm(RATIO),
                                          op0=ALU.add, op1=ALU.mult))
            link(dve.tensor_scalar(sm(X_DT), sm(X_DT), 0.0, None, ALU.max))
            link(dve.scalar_tensor_tensor(out=sm(DT), in0=sm(POLY), scalar=2.0, in1=sm(X_DT), op0=ALU.mult,
                                          op1=ALU.add))
            dve.wait_ge(sem("dt_exp"), 2)
            dve.scalar_tensor_tensor(out=sm(ADT).rearrange("p (c h) -> p c h", h=HEADS),
                                     in0=sm(DT).rearrange("p (c h) -> p c h", h=HEADS), scalar=-1.0,
                                     in1=bias_rows[:, 1].unsqueeze(1).to_broadcast([P, NCH + 1, HEADS]),
                                     op0=ALU.mult, op1=ALU.mult).then_inc(sem("adt"), 1)

            for g in range(4):
                b0 = 2 * (g % 2)
                dve.wait_ge(sem("mix"), g + 1)
                wait(dve, sem("gm_f32"), g)
                dve.tensor_tensor(T(4, SEQ).rearrange("p (c t) -> p c t", c=NCH),
                                  misc[:, b0].rearrange("p (c t) -> p c t", c=NCH),
                                  bs[:, g].unsqueeze(1).to_broadcast([P, NCH, CH]), ALU.add)
                dve.tensor_tensor(temps[:, 4, SEQ:TOK].rearrange("p (b t) -> p b t", b=NB),
                                  misc[:, b0 + 1, 0:SMP].rearrange("p (b t) -> p b t", b=NB),
                                  bs[:, g, 0:TS].unsqueeze(1).to_broadcast([P, NB, TS]), ALU.add)\
                    .then_inc(sem("mix_read"), 1)
                dve.wait_ge(sem("mix_read"), g + 1)
                dve.tensor_tensor(u_sb[:, g], u_sb[:, g], T(4), ALU.mult).then_inc(sem("gm_f32"), 1)
            for g in range(4):
                dve.wait_ge(sem("gm_hi"), g + 1)
                dve.tensor_tensor(branch[:, gmlp_at(g)[1]], u_sb[:, g], branch[:, gmlp_at(g)[0]].bitcast(F32),
                                  ALU.subtract).then_inc(sem("gm_lo"), 1)

            dve.wait_ge(sem("cum"), 1)
            dve.tensor_copy(small[:, A_CUM, 0:n4], misc[:, 3, 0:n4])
            dve.tensor_copy(small[0:SMP, A_CUM, n4:], misc[0:SMP, 3, n4:n4 + HEADS])
            dve.tensor_copy(small[:, TOTAL, 0:n4], misc[:, 3, 80:80 + n4])
            link(dve.tensor_copy(small[0:SMP, TOTAL, n4:], misc[0:SMP, 3, 80 + n4:160]))
            dve.memset(small[:, TO_END, n4:], 0.0).then_inc(sem("dve_chain"), 1)
            chained[0] += 1
            dve.tensor_tensor(small[:, TO_END, 0:n4], small[:, TOTAL, 0:n4], small[:, A_CUM, 0:n4], ALU.subtract)\
                .then_inc(sem("to_end_arg"), 1)
            dve.wait_ge(sem("dve_chain"), chained[0])
            dve.tensor_tensor(small[0:SMP, TO_END, n4:], small[0:SMP, TOTAL, n4:], small[0:SMP, A_CUM, n4:],
                              ALU.subtract).then_inc(sem("to_end_arg"), 1)

            conf_taps(4 * CKW)
            dve.wait_ge(sem("tap_added"), CKW - 1)
            four_sum(ca, sem("cf_sum"))
            center(ca, "cf")
            inverse("cf")
            scale(ca, "cf", "conf_ln_g", sem("cf_scaled"))
            dve.wait_ge(sem("stored_a"), 16 * 8)
            for j in range(4):
                dve.wait_ge(sem("cf_hi"), j + 1)
                dve.tensor_tensor(branch[:, conf_at(j)[1]], ca[:, j], branch[:, conf_at(j)[0]].bitcast(F32),
                                  ALU.subtract).then_inc(sem("cf_lo"), 1)

            def x_times_dt(c):
                rows = P if c < NCH else SMP
                dve.wait_ge(sem("xb_turned"), c + 1)
                for r in range(2):
                    dst = (xdt[:, c] if c < NCH else xdt_s)[:, r * 512:(r + 1) * 512]
                    dve.tensor_tensor(dst.rearrange("p (h d) -> p h d", h=8),
                                      misc[0:rows, r].rearrange("p (h d) -> p h d", h=8),
                                      small[0:rows, DT, c * HEADS + 8 * r:c * HEADS + 8 * r + 8].unsqueeze(2)
                                      .to_broadcast([rows, 8, HD]), ALU.mult).then_inc(sem("xdt"), 1)

            def x_to_end(c):
                dve.wait_ge(sem("xdt"), 2 * (c + 1))
                if 2 <= c < NCH:
                    dve.wait_ge(sem("chunk_sum"), 2 * (c - 1))
                rows, dst, src = (P, xw[:, c % 2], xdt[:, c]) if c < NCH else (SMP, xw_s, xdt_s)
                dve.tensor_tensor(dst.rearrange("p (h d) -> p h d", h=HEADS), src.rearrange("p (h d) -> p h d", h=HEADS),
                                  small[0:rows, TO_END, c * HEADS:(c + 1) * HEADS].unsqueeze(2)
                                  .to_broadcast([rows, HEADS, HD]), ALU.mult).then_inc(sem("xw"), 1)

            def chunk_state(c):
                for g in range(2):
                    cols = slice(g * 512, (g + 1) * 512)
                    bank = misc[:, 2 * (c % 2) + g]
                    dve.wait_ge(sem("chunk_sum"), 2 * c + g + 1)
                    if c == 0:
                        dve.tensor_copy(h_chunk[:, 0, cols], bank).then_inc(sem("chunk_state"), 1)
                        continue
                    dve.wait_ge(sem("chunk_state"), 2 * c + g - 1)
                    dec = small[:, DECAY, c * HEADS + 8 * g:c * HEADS + 8 * g + 8]
                    link(dve.tensor_tensor(T(4 + g, 512).rearrange("p (h d) -> p h d", h=8),
                                           h_chunk[:, c - 1, cols].rearrange("p (h d) -> p h d", h=8),
                                           dec.unsqueeze(2).to_broadcast([P, 8, HD]), ALU.mult))
                    dve.tensor_tensor(h_chunk[:, c, cols], T(4 + g, 512), bank, ALU.add).then_inc(sem("chunk_state"), 1)
            dve.wait_ge(sem("dec_exp"), 2)
            for c in range(NCH):
                x_times_dt(c)
                if c < 2:
                    x_to_end(c)
            for c in range(NCH):
                chunk_state(c)
                if c < 2:
                    x_to_end(c + 2)
            for g in range(2):
                dve.wait_ge(sem("cb"), g + 1)
                dve.tensor_tensor(cbm[:, g].rearrange("p (c i) -> p c i", c=NCH),
                                  misc[:, g].rearrange("p (c i) -> p c i", c=NCH),
                                  tri.unsqueeze(1).to_broadcast([P, NCH, CH]), ALU.mult).then_inc(sem("cbm"), 1)
            dve.wait_ge(sem("cbm"), 2)

            def diffs(h):
                dve.wait_ge(sem("a_spread"), h + 1)
                if h >= 2:
                    dve.wait_ge(sem("y_head"), h - 1)
                for c in range(NCH):
                    cols = slice(c * CH, (c + 1) * CH)
                    ins_ = dve.tensor_scalar(T(4 + h % 2, SEQ)[:, cols], misc[:, h % 2, cols],
                                             small[:, A_CUM, c * HEADS + h:c * HEADS + h + 1], 0.0,
                                             ALU.subtract, ALU.min)
                ins_.then_inc(sem("diff"), 1)

            def y_sum(j):
                dve.wait_ge(sem("y_head"), 2 * j + 2)
                dve.scalar_tensor_tensor(out=xbc[:, j, 0:SEQ], in0=xbc[:, j, 0:SEQ], scalar=param("ssm_d", j),
                                         in1=misc[:, 2 + j % 2], op0=ALU.mult, op1=ALU.add)\
                    .then_inc(sem("y_sum"), 1)
            before = ()
            for group in [g for g in head_groups() if len(g)] + [()]:
                for h in before:
                    if h % 2:
                        y_sum(h // 2)
                for h in group:
                    diffs(h)
                for h in group:
                    dve.wait_ge(sem("pair_decay"), h + 1)
                    dve.tensor_tensor(T(4 + h % 2, SEQ), T(4 + h % 2, SEQ), cbm[:, h // 8], ALU.mult)\
                        .then_inc(sem("mix_head"), 1)
                    dve.wait_ge(sem("a_exp"), h + 1)
                    dve.tensor_tensor(c_dec[:, h % 2], c_dec[:, h % 2], xbc[:, 10 + h // 8, 0:SEQ], ALU.mult)\
                        .then_inc(sem("c_decayed"), 1)
                before = group
            x_times_dt(NCH)
            x_to_end(NCH)
            dve.wait_ge(sem("cb"), 3)
            dve.tensor_tensor(cbm_s, misc[0:SMP, 3, 0:2 * SMP].rearrange("p (g i) -> p g i", g=2),
                              mask_s[:, 0].unsqueeze(1).to_broadcast([SMP, 2, SMP]), ALU.mult).then_inc(sem("cbm"), 1)
            dve.wait_ge(sem("cbm"), 3)
            mixs = temps[0:SMP, 4, 0:512]
            dve.wait_ge(sem("s_spread"), 1)
            link(dve.tensor_tensor(mixs.rearrange("p (h i) -> p h i", h=HEADS),
                                   misc[0:SMP, 0].rearrange("p (h i) -> p h i", h=HEADS),
                                   small[0:SMP, A_CUM, n4:].unsqueeze(2).to_broadcast([SMP, HEADS, SMP]),
                                   ALU.subtract))
            dve.tensor_scalar(mixs, mixs, 0.0, None, ALU.min).then_inc(sem("s_diff"), 1)
            dve.wait_ge(sem("s_exp"), 1)
            for g in range(2):
                half = mixs[:, g * 256:(g + 1) * 256].rearrange("p (h i) -> p h i", h=8)
                ins_ = dve.tensor_tensor(half, half, cbm_s[:, g].unsqueeze(1).to_broadcast([SMP, 8, SMP]), ALU.mult)
            ins_.then_inc(sem("s_mix"), 1)
            dve.wait_ge(sem("bnat"), NCH + 1)

            def b_masked(b):
                dve.tensor_scalar(bm_s[:, b % 2], bnat_s, mask_s[:, 1, TS * b:TS * b + 1], None, ALU.mult)\
                    .then_inc(sem("b_masked"), 1)
            b_masked(0)
            for b in range(NB):
                if b + 1 < NB:
                    if b >= 1:
                        dve.wait_ge(sem("s_sum"), 2 * b)
                    b_masked(b + 1)
                for g in range(2):
                    dve.wait_ge(sem("s_sum"), 2 * b + g + 1)
                    dve.wait_ge(sem("h0_decayed"), 2 * b + g + 1)
                    hv = h0[:, b % 2, g * 512:(g + 1) * 512]
                    dve.tensor_tensor(hv, hv, misc[:, 0 if g == 0 else 3], ALU.add).then_inc(sem("h0_new"), 1)
            dve.wait_ge(sem("s_off"), NB)
            dve.wait_ge(sem("s_exp"), 2)
            dve.wait_ge(sem("s_diag"), 1)
            ys = T(4, KD * SMP)
            for r in range(2):
                rows = slice(r * HD, (r + 1) * HD)
                ins_ = dve.tensor_tensor(ys[rows].rearrange("p (j i) -> p j i", j=KD),
                                         misc[rows, 2, 0:KD * SMP].rearrange("p (j i) -> p j i", j=KD),
                                         temps[rows, 5, 0:512].rearrange("p (j r i) -> p j r i", j=KD, r=2)[:, :, r],
                                         ALU.mult)
            link(ins_)
            link(dve.tensor_tensor(ys, ys, misc[:, 1, 0:KD * SMP], ALU.add))
            for j in range(KD):
                ins_ = dve.scalar_tensor_tensor(out=xbc[:, j, SEQ:TOK], in0=xbc[:, j, SEQ:TOK],
                                                scalar=param("ssm_d", j), in1=ys[:, j * SMP:(j + 1) * SMP],
                                                op0=ALU.mult, op1=ALU.add)
            link(ins_)

            def sum_squares(j, last, done):
                dst = T(5) if j == 0 else T(4)
                link(dve.tensor_tensor(dst, xbc[:, j], xbc[:, j], ALU.mult))
                if j:
                    ins_ = dve.tensor_tensor(T(5), T(5), T(4), ALU.add)
                    if last:
                        ins_.then_inc(done, 1)
                    else:
                        link(ins_)

            for b in range(KD):
                dve.wait_ge(acc_free[b % 2], ph["Z"].pair0 + b // 2 + 1)
                dve.tensor_tensor(xbc[:, b], xbc[:, b], T(b % 2), ALU.mult).then_inc(sem("yz"), 1)
                dve.wait_ge(sem("yz"), b + 1)
                sum_squares(b, b == KD - 1, sem("yz_sq"))
            rstd("ns")

            dve.wait_ge(sem("stored_h"), 16)
            operand("ssm", KD, scaled("ssm_g"), lambda j: T(4 + j % 2), parts_of(ssm_at))

            for j in range(KD):
                dve.wait_ge(sem("mx_hi"), j + 1)
                dve.tensor_tensor(branch[:, mixed_at(j)[1]], mixed[:, j], branch[:, mixed_at(j)[0]].bitcast(F32),
                                  ALU.subtract).then_inc(sem("mx_lo"), 1)
            p = ph["WO"]
            for j in range(KD):
                a = j % 2
                dve.wait_ge(sem(f"x_landed{j}"), 32)
                dve.wait_ge(acc_full[a], p.pair0 + j // 2 + 1)
                dve.tensor_tensor(halves(xbc[:, j]), acc(a), halves(xbc[:, j]), ALU.add).then_inc(acc_free[a], 1)
                dve.wait_ge(acc_free[a], p.pair0 + j // 2 + 1)
                sum_squares(j, j == KD - 1, sem("x2_sq"))
            rstd("n2")
            operand("n2", KD, scaled("norm2_g"), lambda j: T(4 + j % 2), h_parts)

            n_out = SEQ + NB * (FKW - 1 + TS)

            def up(name, f0):
                p = ph[name]

                def quad(i):
                    for r in range(2):
                        f = i * 2 + (f0 + r)
                        pair = p.pair(i, 2 * r)
                        dve.wait_ge(acc_free[0], pair + 1)
                        dve.wait_ge(sem("f_hist"), f + 1)
                        cv = T(2 + r, n_out)
                        for t in range(FKW):
                            src, w = temps[:, r, t:t + n_out], param("ffn_w", i * (2 * FKW) + ((f0 + r) * FKW + t))
                            if t == 0:
                                dve.tensor_scalar(cv, src, w, None, ALU.mult).then_inc(sem("f_conv"), 1)
                            else:
                                dve.wait_ge(sem("f_conv"), i * (2 * FKW) + ((f0 + r) * FKW + t))
                                dve.scalar_tensor_tensor(out=cv, in0=src, scalar=w, in1=cv, op0=ALU.mult, op1=ALU.add)\
                                    .then_inc(sem("f_conv"), 1)
                        dve.wait_ge(sem("f_silu"), f + 1)
                        dve.wait_ge(acc_full[1], pair + 1)
                        prod = T(4 + r)
                        for src, sil, dst in zip(acc_pieces(1), conv_pieces(temps[:, 2 + r], FKW),
                                                 [prod[:, 0:HALF], prod[:, HALF:SEQ],
                                                  prod[:, SEQ:TOK].rearrange("p (b t) -> p b t", b=NB)]):
                            ins_ = dve.tensor_tensor(dst, src, sil, ALU.mult)
                        ins_.then_inc(acc_free[1], 1)
                        dve.wait_ge(sem("f_hi"), f + 1)
                        dve.tensor_tensor(pick(branch, i * 2 + (12 + r)), prod, pick(branch, i * 2 + r).bitcast(F32),
                                          ALU.subtract).then_inc(sem("f_lo"), 1)
                loop(dve, 0, p.quads, quad)

            def down(name, squares):
                p = ph[name]
                for j in range(KD):
                    a = j % 2
                    dve.wait_ge(acc_full[a], p.pair0 + j // 2 + 1)
                    dve.tensor_tensor(halves(xbc[:, j]), acc(a), halves(xbc[:, j]), ALU.add).then_inc(acc_free[a], 1)
                    if squares:
                        dve.wait_ge(acc_free[a], p.pair0 + j // 2 + 1)
                        sum_squares(j, j == KD - 1, sem("x3_sq"))
            dve.wait_ge(sem("zeros_f"), 1)
            up("U1", 0)
            down("D1", False)
            up("U2", FFA)
            down("D2", True)
            rstd("nf")
            for j in range(KD):
                dve.scalar_tensor_tensor(out=halves(xbc[:, j]), in0=halves(xbc[:, j]), scalar=param("final_g", j),
                                         in1=stat, op0=ALU.mult, op1=ALU.mult).then_inc(sem("y_done"), 1)
    return nc


def tiles(w, rows=None):
    k, n = w.shape
    return np.ascontiguousarray(w.reshape(k // P, P, n // P, P).transpose(2, 1, 0, 3).reshape(n // P, P, k))


def channels(a):
    lead = a.shape[:-1]
    v = a.reshape(*lead, a.shape[-1] // P, P)
    return np.ascontiguousarray(np.moveaxis(np.moveaxis(v, -1, 0), -1, 1))


def kernel(**inputs):
    import concourse.bacc as bacc
    from concourse.bass_utils import run_bass_kernel_spmd

    a = {k: np.asarray(v) for k, v in inputs.items()}
    o3, o4 = 2 * CONF + D, 2 * CONF + D + XBC
    o5 = o4 + HEADS
    win = a["w_in"][0]
    t_a1, t_a2 = tiles(win[:, 0:CONF]), tiles(win[:, CONF:2 * CONF])
    t_u, t_v = tiles(win[:, o5:o5 + CONF]), tiles(win[:, o5 + CONF:o5 + 2 * CONF])
    glu = np.stack([t_a2, t_a1], 1).reshape(8, P, D)
    up = tiles(a["ffn_w_up"][0])
    down = a["ffn_w_down"][0]

    def halves_of(w):
        t = tiles(w)
        return np.ascontiguousarray(t.reshape(KD, P, 2, w.shape[0] // 2).transpose(0, 2, 1, 3)
                                    .reshape(2 * KD, P, w.shape[0] // 2))
    cols = {
        "norm1_g": channels(a["norm1_g"][0]), "b_gate": channels(a["b_gate"][0]),
        "conf_w": channels(a["conf_conv_w"][0]), "conf_b": channels(a["conf_conv_b"][0]),
        "conf_ln_g": channels(a["conf_ln_g"][0]), "conf_ln_b": channels(a["conf_ln_b"][0]),
        "ssm_w": channels(a["ssm_conv_w"][0]), "ssm_b": channels(a["ssm_conv_b"][0]),
        "ssm_g": channels(a["ssm_norm_g"][0]), "ssm_d": channels(np.repeat(a["ssm_d"][0], HD)),
        "gmlp_ln_g": channels(a["gmlp_ln_g"][0]), "gmlp_ln_b": channels(a["gmlp_ln_b"][0]),
        "norm2_g": channels(a["norm2_g"][0]), "ffn_w": channels(a["ffn_conv_w"][0]),
        "ffn_b": channels(a["ffn_conv_b"][0]), "final_g": channels(a["final_norm_g"]),
    }
    i = np.arange(P)
    j = np.arange(SMP)
    same = (j[:, None] // TS) == (j[None, :] // TS)
    f32 = np.float32
    arrays = {
        "x": channels(np.concatenate([a["x_prompt"][0], a["x_sample"].reshape(SMP, D)], 0)),
        "consts": np.stack([np.eye(P), i[:, None] <= i[None, :], np.ones((P, P))], 1).astype(f32),
        "mask_s": np.stack([same & (j[:, None] <= j[None, :]), same], 1).astype(f32),
        "params": np.concatenate([cols[n].reshape(P, -1) for n, _ in PARAM_BLOCKS], 1),
        "w_in_main": np.concatenate([glu, t_v, t_u, tiles(win[:, o3:o4])], 0),
        "w_in_z": tiles(win[:, 2 * CONF:o3]),
        "w_dt": np.ascontiguousarray(win[:, o4:o5].reshape(KD, P, HEADS).transpose(1, 0, 2)),
        "ssm_dt_bias": a["ssm_dt_bias"][0], "ssm_a_log": a["ssm_a_log"][0],
        "w_gate": tiles(a["w_gate"][0]),
        "conf_w_out": tiles(a["conf_w_out"][0]), "ssm_w_out": tiles(a["ssm_w_out"][0]),
        "gmlp_w_out": tiles(a["gmlp_w_out"][0]), "w_o": tiles(a["w_o"][0]),
        "ffn_w_up": np.stack([up[0:NF], up[NF:]], 1).reshape(2 * NF, P, D),
        "ffn_w_down1": halves_of(down[0:FFA * P]), "ffn_w_down2": halves_of(down[FFA * P:]),
        "gmlp_w_s": np.ascontiguousarray(a["gmlp_w_s"][0].transpose(2, 0, 1)),
        "gmlp_b_s": a["gmlp_b_s"][0].reshape(-1),
        "state_conv_a": channels(a["state_conv_a"][0]),
        "state_conv_ssm": channels(a["state_conv_ssm"][0]),
        "state_conv_ffn": channels(a["state_conv_ffn"][0]),
        "state_ssm": np.ascontiguousarray(a["state_ssm"][0].transpose(0, 3, 1, 2).reshape(NB, STATE, D)),
    }
    arrays = {k: np.ascontiguousarray(v) for k, v in arrays.items()}
    shapes = {
        "y": (P, KD, TOK), "conv_a_p": (P, 4, CKW - 1), "conv_a_s": (P, 4, NB, CKW - 1),
        "conv_ssm": (P, 12, (NB + 1) * (SKW - 1)), "conv_ffn": (P, NF, (NB + 1) * (FKW - 1)),
        "ssm_p": (STATE, D), "ssm_s": (NB, STATE, D), "gmlp_v_s": (P, 4, SMP),
    }
    nc = bacc.Bacc("TRN2", target_bir_lowering=False, num_devices=1, dynamic_dma_scratch_size=1024)
    ins = {k: nc.dram_tensor(f"in_{k}", v.shape, F32, kind="ExternalInput").ap() for k, v in arrays.items()}
    outs = {k: nc.dram_tensor(f"out_{k}", v, F32, kind="ExternalOutput").ap() for k, v in shapes.items()}
    build(nc, ins, outs)
    r = run_bass_kernel_spmd(nc, [{f"in_{k}": v for k, v in arrays.items()}], core_ids=[0])
    got = {k: np.asarray(r.results[0][f"out_{k}"]) for k in shapes}

    def rows(t):
        v = np.moveaxis(np.moveaxis(t, 0, -1), 0, -2)
        return v.reshape(*v.shape[:-2], -1)

    y = rows(got["y"])
    n, m = SKW - 1, FKW - 1
    conv_ssm, conv_ffn = rows(got["conv_ssm"]), rows(got["conv_ffn"])

    def state(t):
        return t.reshape(*t.shape[:-2], STATE, HEADS, HD).transpose(0, 2, 3, 1)
    out = (
        y[0:SEQ][None], y[SEQ:].reshape(NB, TS, D), rows(got["conv_a_p"])[None, None],
        state(got["ssm_p"][None])[None], conv_ssm[0:n][None, None], conv_ffn[0:m][None, None],
        rows(got["conv_a_s"])[None], state(got["ssm_s"])[None],
        conv_ssm[n:].reshape(NB, n, XBC)[None], conv_ffn[m:].reshape(NB, m, FF)[None],
        rows(got["gmlp_v_s"]).reshape(NB, TS, CONF)[None],
    )
    return tuple(np.ascontiguousarray(o) for o in out)
```

```python
from contextlib import ExitStack

import numpy as np
import concourse.bass as bass
from concourse import mybir

F32 = mybir.dt.float32
F32R = mybir.dt.float32r
ACT = mybir.ActivationFunctionType
ALU = mybir.AluOpType

P = 128
D, SEQ, NB, TS = 1024, 512, 8, 4
SMP = NB * TS
TOK = SEQ + SMP
HALF = TOK // 2
KD = D // P
CONF, CKW = 512, 31
HEADS, HD, STATE, SKW, XBC = 16, 64, 128, 4, 1536
FF, FKW = 2816, 3
NF = FF // P
FFA = 12
FFB = NF - FFA
CH = 128
NCH = SEQ // CH
EPS = 1e-6
SLOTS = 4
CONF_TAPS = 2
X_TAPS = 1
WARM = (24, 2, 3, 8)
SAMPLES_AFTER = (0, 0, 0, 1, 1, 2, 2, 2)
H0_BUFS = 4
CONF_SHARED = 3
ACT_TAPS = (2, 2)
POOL_TAPS = (3, 4)
RING = 8
GMLP_LOADS = 2 + NB
HEADS_AFTER = (0, 0, 0, 0, 0, 1, 1, 2, 1, 2, 1, 2, 2, 1, 2, 1)
ELEM = KD * P

PHASES = [
    ("A", 2, (8, 8, 8, 8), 1),
    ("VU", 2, (8, 8, 8, 8), 1),
    ("X", 3, (8, 8, 8, 8), 1),
    ("G2", 4, (8, 4, 8, 4), 1),
    ("G0", 4, (8, 4, 8, 4), 1),
    ("Z", 2, (8, 8, 8, 8), 1),
    ("G1", 4, (8, 8, 8, 8), 1),
    ("WO", 2, (8, 8, 8, 8), 1),
    ("U1", 6, (8, 8, 8, 8), 1),
    ("D1", 4, (6, 6, 6, 6), 2),
    ("U2", 5, (8, 8, 8, 8), 1),
    ("D2", 4, (5, 5, 5, 5), 2),
]


class Phase:
    def __init__(self, name, quads, kb, per_block, quad0, pair0):
        self.name, self.quads, self.kb, self.per_block = name, quads, kb, per_block
        self.quad0, self.pair0 = quad0, pair0
        self.pairs_per_quad = 2 // per_block

    def pair(self, i, s):
        if self.per_block == 2:
            return i + self.pair0
        return i * 2 + (self.pair0 + s // 2)

    def acc(self, s):
        return s // 2 if self.per_block == 2 else s % 2


def phases():
    out, q, p = {}, 0, 0
    for name, quads, kb, per_block in PHASES:
        out[name] = Phase(name, quads, kb, per_block, q, p)
        q += quads
        p += quads * (2 // per_block)
    return out


PARAM_BLOCKS = [("norm1_g", KD), ("b_gate", 3 * KD), ("conf_w", 4 * CKW), ("conf_b", 4), ("conf_ln_g", 4),
                ("conf_ln_b", 4), ("ssm_w", 12 * SKW), ("ssm_b", 12), ("ssm_g", KD), ("ssm_d", KD),
                ("gmlp_ln_g", 4), ("gmlp_ln_b", 4), ("norm2_g", KD), ("ffn_w", NF * FKW), ("ffn_b", NF),
                ("final_g", KD)]
PARAM_AT, _n = {}, 0
for _name, _k in PARAM_BLOCKS:
    PARAM_AT[_name] = _n
    _n += _k
N_PARAM = _n


def line(k):
    return k - 1 + SEQ + NB * (k - 1 + TS)


def loop(e, lo, hi, body):
    if hi - lo == 1:
        body(lo)
    elif hi > lo:
        with e.Fori(lo, hi) as i:
            body(i)


def wait(e, sem, value):
    if isinstance(value, int) and value <= 0:
        return
    e.wait_ge(sem, value)


def pick(t, j):
    if isinstance(j, int):
        return t[:, j]
    v = t[:, bass.ds(j, 1)]
    names = "abcdef"[:len(v.shape) - 2]
    return v.rearrange(f"p o {' '.join(names)} -> p (o {names[0]}) {' '.join(names[1:])}")


def build(nc, ins, outs):
    ph = phases()
    order = [x[0] for x in PHASES]
    with ExitStack() as ctx:
        def sb(name, shape, dt=F32):
            return ctx.enter_context(nc.sbuf_tensor(name, shape, dt))

        sems = {}

        def sem(name):
            if name not in sems:
                sems[name] = ctx.enter_context(nc.semaphore(name))
            return sems[name]

        h_split = sb("h_split", [P, KD, 2, TOK], F32R)
        w_split = sb("w_split", [P, SLOTS, 2, ELEM], F32R)
        w_raw = sb("w_raw", [P, SLOTS, ELEM])
        params = sb("params", [P, N_PARAM])
        consts = sb("consts", [P, 3, P])
        mask_s = sb("mask_s", [SMP, 2, SMP])
        xbc = sb("xbc", [P, 12, TOK])
        u_sb = sb("u_sb", [P, 4, TOK])
        mixed = sb("mixed", [P, KD, TOK])
        ca = sb("ca", [P, 4, TOK])
        temps = sb("temps", [P, 6, 576])
        small = sb("small", [P, 12, 5 * HEADS])
        a_split = sb("a_split", [64, TOK], F32R)
        heads_f32 = sb("heads_f32", [64, HEADS])
        sample_of = sb("sample_of", [96, NB])
        head_of = sb("head_of", [64, HEADS], F32R)
        bias_rows = sb("bias_rows", [P, 2, HEADS])
        w_dt = sb("w_dt", [P, KD, HEADS])
        w_dt_split = sb("w_dt_split", [P, 2, KD, HEADS], F32R)
        eps = sb("eps", [P, 1])
        rms_scratch = sb("rms_scratch", [P, 1])
        rms = sb("rms", [P, 2, 6])
        hist_x = sb("hist_x", [P, 12, NB, SKW - 1])
        hist_f = sb("hist_f", [P, NF, NB, FKW - 1])
        tail_x = sb("tail_x", [P, 12, (NB + 1) * (SKW - 1)])
        tail_f = sb("tail_f", [P, NF, (NB + 1) * (FKW - 1)])
        with ExitStack() as early:
            part0, part1, part2 = (early.enter_context(nc.sbuf_tensor(f"part{n}", [P, 8 * TOK], F32))
                                   for n in range(3))
        branch = sb("branch", [P, 24, TOK], F32R)

        def carve(tensor, *shapes):
            out, o = [], 0
            for parts, *dims in shapes:
                n = int(np.prod(dims))
                v = tensor[0:parts, o:o + n]
                if len(dims) == 2:
                    v = v.rearrange("p (a b) -> p a b", a=dims[0])
                out.append(v)
                o += n
            assert o <= tensor.shape[1]
            return out

        u_flat = u_sb[:, :, :].rearrange("p j n -> p (j n)")
        ca_flat = ca[:, :, :].rearrange("p j n -> p (j n)")
        v_sb = mixed[:, 0:4]
        (tap_ring,) = carve(part0, (P, RING, SEQ))
        (line_a,) = carve(part1, (P, 4, line(CKW)))
        vnat, ws_t, bs, ws_s = carve(part2, (P, 5, CONF), (P, 4, CH), (P, 4, CH), (SMP, 4, SMP))
        (h_chunk,) = carve(part0, (P, NCH, D))
        (xdt,) = carve(part2, (P, NCH, D))
        bnat, cbm = carve(ca_flat, (P, NCH, 2 * STATE), (P, 2, SEQ))
        (c_dec,) = carve(ca_flat, (P, 2, SEQ))
        (xw,) = carve(u_flat, (P, 2, D))
        h0 = [half[:, r] for half in (carve(u_flat, (P, 2, D))[0], carve(ca_flat, (P, 2, D))[0])
              for r in range(2)]
        z_s = vnat[:, 0].rearrange("p (a n) -> p a n", n=SMP)[:, 0:KD]
        xdt_s, xw_s, cbm_s = carve(part1, (SMP, D), (SMP, D), (SMP, 2, SMP))
        b_stack, b_alone, xw_stack = carve(branch[:, 12:16].rearrange("p j n -> p (j n)"),
                                           (96, 2 * STATE), (96, 2, 2 * STATE), (96, D))
        ident, tri, ones = consts[:, 0], consts[:, 1], consts[:, 2]
        X_DT, ABS, EXPN, RATIO, RATIO2, POLY, TO_END, DT, ADT, A_CUM, TOTAL, DECAY = range(12)

        def param(name, j):
            if isinstance(j, int):
                return params[:, PARAM_AT[name] + j:PARAM_AT[name] + j + 1]
            return params[:, bass.ds(j + PARAM_AT[name], 1)]

        def T(r, n=TOK):
            return temps[:, r, 0:n]

        dt_rows = temps[0:HEADS, 5, 0:TOK]

        def norm_block(j):
            return T((4, 5, 2, 3)[j % 4])

        accs = ctx.enter_context(nc.psum_tensor("accs", [P, 2, 2, 512], F32))
        misc = ctx.enter_context(nc.psum_tensor("misc", [P, 4, 512], F32))
        stat = misc[:, 0:2, 0:HALF]

        def acc(a):
            return accs[:, a, :, 0:HALF]

        def halves(ap):
            return ap.rearrange("p (h n) -> p h n", h=2)

        def acc_pieces(a):
            return [accs[:, a, 0, 0:HALF], accs[:, a, 1, 0:SEQ - HALF],
                    accs[:, a, 1, SEQ - HALF:HALF].rearrange("p (b t) -> p b t", b=NB)]

        def samples(ln, start, k):
            return ln[:, start:start + NB * (k - 1 + TS)].rearrange("p (b t) -> p b t", b=NB)

        def line_pieces(ln, k):
            return [ln[:, k - 1:k - 1 + HALF], ln[:, k - 1 + HALF:k - 1 + SEQ],
                    samples(ln, k - 1 + SEQ, k)[:, :, k - 1:]]

        def conv_pieces(cv, k):
            return [cv[:, 0:HALF], cv[:, HALF:SEQ], samples(cv, SEQ, k)[:, :, k - 1:]]

        w_landed = [sem(f"w_landed{s}") for s in range(SLOTS)]
        w_hi = [sem(f"w_hi{s}") for s in range(SLOTS)]
        w_lo = [sem(f"w_lo{s}") for s in range(SLOTS)]
        acc_full = [sem(f"acc_full{a}") for a in range(2)]
        acc_free = [sem(f"acc_free{a}") for a in range(2)]

        block = ctx.enter_context(nc.Block())

        def w_src(name, i, s):
            if name in ("A", "VU", "X"):
                return ins["w_in_main"], i * 4 + ({"A": 0, "VU": 8, "X": 16}[name] + s)
            if name == "Z":
                return ins["w_in_z"], i * 4 + s
            if name in ("G0", "G1", "G2"):
                g = int(name[1])
                if s % 2 == 0:
                    return ins["w_gate"], i * 2 + (g * KD + s // 2)
                return ins[("conf_w_out", "ssm_w_out", "gmlp_w_out")[g]], i * 2 + s // 2
            if name == "WO":
                return ins["w_o"], i * 4 + s
            if name in ("U1", "U2"):
                return ins["ffn_w_up"], i * 4 + ((0 if name == "U1" else 2 * FFA) + s)
            return ins["ffn_w_down1" if name == "D1" else "ffn_w_down2"], i * 4 + s

        def load_quad(sp, p, i):
            for s in range(SLOTS):
                src, j = w_src(p.name, i, s)
                n = p.kb[s] * P
                wait(sp, w_lo[s], i + p.quad0)
                ap = src[j] if isinstance(j, int) else src[bass.ds(j, 1)].rearrange("o p n -> (o p) n")
                sp.dma_start(w_raw[:, s, 0:n], ap).then_inc(w_landed[s], 16)

        def load_phase(sp, name, first=0):
            p = ph[name]
            loop(sp, first, p.quads, lambda i: load_quad(sp, p, i))

        def split_hi(act, p, i, s):
            n = p.kb[s] * P
            act.wait_ge(w_landed[s], i * 16 + (p.quad0 + 1) * 16)
            act.activation(w_split[:, s, 0, 0:n], w_raw[:, s, 0:n], ACT.Copy).then_inc(w_hi[s], 1)

        def split_lo(pool, p, i, s):
            n = p.kb[s] * P
            pool.wait_ge(w_hi[s], i + (p.quad0 + 1))
            pool.tensor_tensor(w_split[:, s, 1, 0:n], w_raw[:, s, 0:n], w_split[:, s, 0, 0:n].bitcast(F32),
                               ALU.subtract).then_inc(w_lo[s], 1)

        def head_groups():
            out, h = [], 0
            for n in HEADS_AFTER:
                out.append(range(h, h + n))
                h += n
            assert h == HEADS
            return out

        def sample_groups():
            out, b = [], 0
            for n in SAMPLES_AFTER:
                out.append(range(b, b + n))
                b += n
            assert b == NB
            return out

        def act_quad(act, p, i, ahead, evac, between=None):
            for s in range(p.per_block - 1, SLOTS, p.per_block):
                a = p.acc(s)
                act.wait_ge(acc_full[a], p.pair(i, s) + 1)
                evac(i, s)
                if ahead is not None:
                    for r in range(s + 1 - p.per_block, s + 1):
                        split_hi(act, ahead[0], ahead[1], r)
                if between is not None:
                    between(i, s)

        def after(p):
            at = order.index(p.name)
            return (ph[order[at + 1]], 0) if at + 1 < len(order) else None

        def act_phase(act, name, evac, unroll=False, between=None):
            p = ph[name]
            if unroll:
                for i in range(p.quads - 1):
                    act_quad(act, p, i, (p, i + 1), evac, between)
            else:
                loop(act, 0, p.quads - 1, lambda i: act_quad(act, p, i, (p, i + 1), evac, between))
            act_quad(act, p, p.quads - 1, after(p), evac, between)

        def pe_quad(pe, p, i, rhs, ready=None, between=None):
            for s in range(SLOTS):
                a = p.acc(s)
                first, last = s % p.per_block == 0, s % p.per_block == p.per_block - 1
                pe.wait_ge(w_lo[s], i + (p.quad0 + 1))
                if first:
                    wait(pe, acc_free[a], p.pair(i, s))
                for k in range(p.kb[s]):
                    if ready is not None:
                        ready(s, k)
                    for n, (wp, xp) in enumerate(((0, 0), (0, 1), (1, 0))):
                        for half in range(2):
                            mm = pe.matmul(accs[:, a, half, 0:HALF], w_split[:, s, wp, k * P:(k + 1) * P],
                                           rhs(s, k, xp, half), start=(first and k == 0 and n == 0),
                                           stop=(last and k == p.kb[s] - 1 and n == 2))
                if last:
                    mm.then_inc(acc_full[a], 1)
                if between is not None:
                    between(s)

        def pe_phase(pe, name, rhs, ready=None):
            p = ph[name]
            if ready is not None:
                pe_quad(pe, p, 0, rhs, ready)
            loop(pe, 0 if ready is None else 1, p.quads, lambda i: pe_quad(pe, p, i, rhs))

        def tokens(half):
            return slice(half * HALF, (half + 1) * HALF)

        def h_rhs(s, k, part, half):
            return h_split[:, k, part, tokens(half)]

        def gmlp_at(k):
            return k, 4 + k

        def conf_at(k):
            return 8 + k, 12 + k

        def ssm_at(k):
            return 16 + k, k

        def mixed_at(k):
            return (8 + k, 12 + k) if k < 4 else (k - 4, k)

        def parts_of(at):
            return lambda j: (branch[:, at(j)[0]], branch[:, at(j)[1]])

        def h_parts(j):
            return h_split[:, j, 0], h_split[:, j, 1]

        def nth(name):
            return ("n1", "gl", "cf", "ns", "n2", "nf").index(name) + 1

        def branch_rhs(at):
            return lambda s, k, part, half: branch[:, at(k)[part], tokens(half)]

        def merge_rhs(at):
            return lambda s, k, part, half: (h_rhs if s % 2 == 0 else branch_rhs(at))(s, k, part, half)

        def down_rhs(kb):
            return lambda s, k, part, half: branch[:, 12 * part + kb * (s % 2) + k, tokens(half)]

        def sum_bank(b, g):
            return (0, 3, 1)[(2 * b + g) % 3]

        def decayed(e, b, g):
            hv = h0[b % H0_BUFS][:, g * 512:(g + 1) * 512].rearrange("p (h d) -> p h d", h=8)
            last = T(5, 512).rearrange("p (h i) -> p h i", h=HEADS)[:, g * 8:(g + 1) * 8, TS * b + TS - 1:TS * b + TS]
            return e.tensor_tensor(hv, hv, last.to_broadcast([P, 8, HD]), ALU.mult)

        @block.sync
        def _(sp):
            for j in range(KD):
                sp.dma_start(xbc[:, j], ins["x"][:, j]).then_inc(sem(f"x_landed{j}"), 16)
                if j == 3:
                    sp.dma_start(consts[:, :, :], ins["consts"]).then_inc(sem("consts_landed"), 16)
            sp.dma_start(params[:, :], ins["params"]).then_inc(sem("params_landed"), 16)
            load_quad(sp, ph["A"], 0)
            for j in range(4):
                sp.dma_start(samples(line_a[:, j], CKW - 1 + SEQ, CKW)[:, :, 0:CKW - 1],
                             ins["state_conv_a"][:, j]).then_inc(sem("hist_a_landed"), 16)
            sp.dma_start(hist_x[:, :, :, :], ins["state_conv_ssm"]).then_inc(sem("hist_landed"), 16)
            sp.dma_start(hist_f[:, :, :, :], ins["state_conv_ffn"]).then_inc(sem("hist_landed"), 16)
            sp.dma_start(mask_s[:, :, :], ins["mask_s"]).then_inc(sem("small_landed"), 16)
            sp.dma_start(w_dt[:, :, :], ins["w_dt"]).then_inc(sem("small_landed"), 16)
            sp.dma_start(sample_of[:, :], ins["sample_of"]).then_inc(sem("small_landed"), 16)
            sp.dma_start(heads_f32[:, :], ins["heads"]).then_inc(sem("small_landed"), 16)
            sp.dma_start(bias_rows[:, 0], ins["ssm_dt_bias"].partition_broadcast(P)).then_inc(sem("small_landed"), 16)
            sp.dma_start(bias_rows[:, 1], ins["ssm_a_log"].partition_broadcast(P)).then_inc(sem("small_landed"), 16)
            load_quad(sp, ph["A"], 1)
            sp.dma_start(ws_t, ins["gmlp_w_s"]).then_inc(sem("gmlp_landed"), 16)
            sp.dma_start(bs.rearrange("p g n -> p (g n)"), ins["gmlp_b_s"].partition_broadcast(P))\
                .then_inc(sem("gmlp_landed"), 16)
            for b in range(NB):
                sp.dma_start(ws_s[TS * b:TS * b + TS].rearrange("p g (b t) -> p g b t", b=NB),
                             ins["gmlp_w_s"][0:TS, :, 0:TS].unsqueeze(2).to_broadcast([TS, 4, NB, TS]))\
                    .then_inc(sem("gmlp_landed"), 16)
            load_phase(sp, "VU")
            load_phase(sp, "X")
            sp.wait_ge(acc_free[1], 4)
            for j in range(4):
                sp.dma_start(outs["conv_a_p"][:, j], line_a[:, j, SEQ:SEQ + CKW - 1]).then_inc(sem("stored_a"), 16)
                sp.dma_start(outs["conv_a_s"][:, j], samples(line_a[:, j], CKW - 1 + SEQ, CKW)[:, :, TS:])\
                    .then_inc(sem("stored_a"), 16)
            load_quad(sp, ph["G2"], 0)
            sp.wait_ge(sem("vn_done"), 4)
            sp.dma_start(outs["gmlp_v_s"], v_sb[:, :, SEQ:TOK]).then_inc(sem("stored_v"), 16)
            load_phase(sp, "G2", first=1)
            sp.wait_ge(sem("tail_x"), 24)
            sp.dma_start(outs["conv_ssm"], tail_x[:, :, :]).then_inc(sem("stored_tails"), 16)
            load_phase(sp, "G0")
            sp.wait_ge(sem("chunk_state"), 2 * NCH)
            sp.dma_start(outs["ssm_p"], h_chunk[:, NCH - 1]).then_inc(sem("stored_h"), 16)

            def load_h0(b):
                sp.dma_start(h0[b % H0_BUFS], ins["state_ssm"][b]).then_inc(sem(f"h0_landed{b % H0_BUFS}"), 16)
            sp.wait_ge(sem("chunk_sum"), 2 * NCH)
            load_h0(0)
            load_h0(1)
            load_phase(sp, "Z")
            sp.wait_ge(sem("y_head"), HEADS)
            load_h0(2)
            load_h0(3)
            load_quad(sp, ph["G1"], 0)
            for b in range(NB):
                r = b % H0_BUFS
                sp.wait_ge(sem("h0_new"), 2 * (b + 1))
                sp.dma_start(outs["ssm_s"][b], h0[r]).then_inc(sem(f"h0_stored{r}"), 16)
                if b + H0_BUFS < NB:
                    sp.wait_ge(sem(f"h0_stored{r}"), 16)
                    load_h0(b + H0_BUFS)
            load_phase(sp, "G1", first=1)
            for j in range(KD):
                sp.wait_ge(sem("ssm_f32"), j + 1)
                sp.dma_start(xbc[:, j], ins["x"][:, j]).then_inc(sem(f"x_landed{j}"), 16)
            for name in ("WO", "U1", "D1", "U2", "D2"):
                load_phase(sp, name)
            sp.wait_ge(sem("tail_f"), 2 * NF)
            sp.dma_start(outs["conv_ffn"], tail_f[:, :, :]).then_inc(sem("stored_tails"), 16)
            for j in range(KD):
                sp.wait_ge(sem("y_done"), j + 1)
                sp.dma_start(outs["y"][:, j], xbc[:, j]).then_inc(sem("stored_y"), 16)
            sp.wait_ge(sem("stored_a"), 16 * 8)
            sp.wait_ge(sem("stored_v"), 16)
            sp.wait_ge(sem("stored_tails"), 32)
            sp.wait_ge(sem("stored_h"), 16)
            for r in range(H0_BUFS):
                sp.wait_ge(sem(f"h0_stored{r}"), 16 * NB // H0_BUFS)
            sp.wait_ge(sem("stored_y"), 16 * KD)

        @block.gpsimd
        def _(pool):
            def pool_phase(name, work):
                p = ph[name]

                def quad(i, ahead):
                    for r in range(2):
                        work(i, r)
                        if ahead is not None:
                            split_lo(pool, ahead[0], ahead[1], 2 * r)
                            split_lo(pool, ahead[0], ahead[1], 2 * r + 1)
                loop(pool, 0, p.quads - 1, lambda i: quad(i, (p, i + 1)))
                quad(p.quads - 1, after(p))

            def nothing(i, r):
                pass

            def history(hist, f, par, k, conv, taps, done):
                wait(pool, conv, f * taps - taps)
                pool.tensor_copy(samples(temps[:, par], k - 1 + SEQ, k)[:, :, 0:k - 1], pick(hist, f)).then_inc(done, 1)

            def tails(tail, f, par, k, done):
                n = k - 1
                dst = pick(tail, f)
                pool.tensor_copy(dst[:, 0:n], temps[:, par, SEQ:SEQ + n]).then_inc(done, 1)
                pool.tensor_copy(dst[:, n:].rearrange("p (b t) -> p b t", b=NB),
                                 samples(temps[:, par], n + SEQ, k)[:, :, TS:]).then_inc(done, 1)

            pool.memset(eps[:, :], EPS).then_inc(sem("eps_set"), 1)
            pool.memset(temps[0:64, 5, 0:TOK], 0.0).then_inc(sem("rows_zero"), 1)
            pool.memset(line_a[:, :, 0:CKW - 1], 0.0).then_inc(sem("zeros_a"), 1)
            def lo_odd(name, dst):
                for j in range(1, KD, 2):
                    pool.wait_ge(sem(name + "_hi"), j + 1)
                    hi, lo = dst(j)
                    pool.tensor_tensor(lo, norm_block(j), hi.bitcast(F32), ALU.subtract).then_inc(sem(name + "_lo_odd"), 1)

            split_lo(pool, ph["A"], 0, 0)
            split_lo(pool, ph["A"], 0, 1)
            lo_odd("n1", h_parts)
            split_lo(pool, ph["A"], 0, 2)
            split_lo(pool, ph["A"], 0, 3)
            pool_phase("A", nothing)
            pool.wait_ge(acc_free[1], 4)
            pool.memset(temps[:, 0:2, 0:SKW - 1], 0.0).then_inc(sem("zeros_x"), 1)
            pool.wait_ge(sem("hist_landed"), 32)
            history(hist_x, 0, 0, SKW, sem("x_conv"), SKW - 1, sem("x_hist"))
            history(hist_x, 1, 1, SKW, sem("x_conv"), SKW - 1, sem("x_hist"))
            shared = iter(range(1, CKW))

            def add_taps(n):
                for _, t in zip(range(n), shared):
                    pool.wait_ge(sem("tap_product"), t + 1)
                    if t > 1:
                        pool.wait_ge(sem("tap_added"), t - 1)
                    pool.tensor_tensor(ca[:, CONF_SHARED, 0:SEQ], ca[:, CONF_SHARED, 0:SEQ], tap_ring[:, t % RING],
                                       ALU.add).then_inc(sem("tap_added"), 1)
            pool_phase("VU", lambda i, r: add_taps(POOL_TAPS[0]))

            def x_work(i, r):
                p = ph["X"]
                for par in range(2):
                    f = 4 * i + 2 * r + par
                    pool.wait_ge(acc_free[par], p.pair(i, 2 * r) + 1)
                    tails(tail_x, f, par, SKW, sem("tail_x"))
                    if f + 2 < 12:
                        history(hist_x, f + 2, par, SKW, sem("x_conv"), SKW - 1, sem("x_hist"))
            p = ph["X"]
            for i in range(p.quads):
                for r in range(2):
                    q, j = (p, i + 1) if i + 1 < p.quads else after(p)
                    split_lo(pool, q, j, 2 * r)
                    split_lo(pool, q, j, 2 * r + 1)
                    x_work(i, r)
                    add_taps(POOL_TAPS[1])

            def merge(name, n0):
                p = ph[name]

                def work(i, r):
                    j = i * 2 + r
                    pool.wait_ge(acc_free[0], p.pair(i, 2 * r) + 1)
                    pool.wait_ge(acc_free[1], p.pair(i, 2 * r) + 1)
                    if n0 == 0:
                        pool.tensor_tensor(pick(mixed, j), T(r), T(2), ALU.mult).then_inc(sem("merged"), 1)
                    else:
                        pool.tensor_tensor(T(2), T(r), T(2), ALU.mult).then_inc(sem("gated"), 1)
                        pool.wait_ge(sem("gated"), j + (n0 - 8 + 1))
                        pool.tensor_tensor(pick(mixed, j), pick(mixed, j), T(2), ALU.add).then_inc(sem("merged"), 1)
                pool_phase(name, work)

            pool.wait_ge(sem("v_turned"), 5)
            pool.wait_ge(sem("stored_v"), 16)
            add_taps(CKW)
            merge("G2", 0)
            merge("G0", 8)

            def decay_states(b):
                if b == 0:
                    pool.wait_ge(sem("s_exp"), 2)
                pool.wait_ge(sem("s_off"), b + 1)
                decayed(pool, b, 0).then_inc(sem("h0_decayed"), 1)
            p = ph["Z"]
            for i in range(p.quads):
                for s in range(SLOTS):
                    q, j = (p, i + 1) if i + 1 < p.quads else after(p)
                    split_lo(pool, q, j, s)
                    for b in sample_groups()[4 * i + s]:
                        decay_states(b)
            pool.wait_ge(sem("stored_h"), 16)
            lo_odd("ssm", parts_of(ssm_at))
            merge("G1", 16)
            pool_phase("WO", nothing)
            lo_odd("n2", h_parts)
            pool.memset(temps[:, 0:2, 0:FKW - 1], 0.0).then_inc(sem("zeros_f"), 1)
            history(hist_f, 0, 0, FKW, sem("f_conv"), FKW, sem("f_hist"))
            history(hist_f, 1, 1, FKW, sem("f_conv"), FKW, sem("f_hist"))

            def up(name, f0):
                p = ph[name]

                def work(i, r):
                    f = i * 2 + (f0 + r)
                    pool.wait_ge(acc_free[0], p.pair(i, 2 * r) + 1)
                    tails(tail_f, f, r, FKW, sem("tail_f"))
                    if not (isinstance(f, int) and f + 2 >= NF):
                        history(hist_f, i * 2 + (f0 + r + 2), r, FKW, sem("f_conv"), FKW, sem("f_hist"))
                pool_phase(name, work)
            up("U1", 0)
            pool_phase("D1", nothing)
            up("U2", FFA)
            pool_phase("D2", nothing)

        @block.scalar
        def _(act):
            def hi_blocks(name, n, src, dst):
                for j in range(n):
                    act.wait_ge(sem(name + "_f32"), j + 1)
                    act.activation(dst(j), src(j), ACT.Copy).then_inc(sem(name + "_hi"), 1)

            def sqrt_table():
                act.activation(rms_scratch[:, 0:1], eps[:, 0:1], ACT.Sqrt)

            def root(name, width):
                act.wait_ge(sem("rms_sum"), nth(name))
                act.activation(rms[:, 0], misc[:, 3, 0:6], ACT.Sqrt, bias=eps[:, 0:1], scale=1.0 / width)\
                    .then_inc(sem("rms_root"), 1)

            act.wait_ge(sem("eps_set"), 1)
            sqrt_table()
            for j in range(KD):
                act.wait_ge(sem(f"x_landed{j}"), 16)
                if j >= 2:
                    act.wait_ge(sem("n1_added"), max(j - 2, 1))
                act.activation(T(j % 2), xbc[:, j], ACT.Square).then_inc(sem("n1_sq"), 1)
            root("n1", D)
            split_hi(act, ph["A"], 0, 0)
            split_hi(act, ph["A"], 0, 1)
            hi_blocks("n1", KD, norm_block, lambda j: h_split[:, j, 0])
            split_hi(act, ph["A"], 0, 2)
            split_hi(act, ph["A"], 0, 3)

            def evac_a(i, s):
                if s % 2 == 0:
                    wait(act, acc_free[1], 2 * i + s // 2 - 1)
                    act.activation(halves(T(s // 2)), acc(0), ACT.Sigmoid).then_inc(acc_free[0], 1)
            act_phase(act, "A", evac_a, unroll=True)

            def evac_vu(i, s):
                a = s % 2
                act.activation(halves((v_sb if i == 0 else u_sb)[:, s]), acc(a), ACT.Gelu_apprx_tanh)\
                    .then_inc(acc_free[a], 1)
            shared = iter(range(CKW))

            def tap_products(n):
                for _, t in zip(range(n), shared):
                    src, w = line_a[:, CONF_SHARED, t:t + SEQ], param("conf_w", CONF_SHARED * CKW + t)
                    if t == 0:
                        act.wait_ge(acc_free[1], 4)
                        act.wait_ge(sem("zeros_a"), 1)
                        act.activation(ca[:, CONF_SHARED, 0:SEQ], src, ACT.Identity, bias=param("conf_b", CONF_SHARED),
                                       scale=w).then_inc(sem("tap_product"), 1)
                        continue
                    if t > RING:
                        act.wait_ge(sem("tap_added"), t - RING)
                    act.activation(tap_ring[:, t % RING], src, ACT.Copy, scale=w).then_inc(sem("tap_product"), 1)
            act_phase(act, "VU", evac_vu, unroll=True, between=lambda i, s: tap_products(ACT_TAPS[0]))

            def to_line(a, r, k):
                for n, (src, dst) in enumerate(zip(acc_pieces(a), line_pieces(temps[:, r], k))):
                    ins_ = act.activation(dst, src, ACT.Copy)
                ins_.then_inc(acc_free[a], 1)

            def silu_x(j):
                cv = temps[:, 2 + j % 2]
                act.wait_ge(sem("x_conv"), (SKW - 1) * (j + 1))
                act.activation(xbc[:, j, 0:SEQ], cv[:, 0:SEQ], ACT.Silu, bias=param("ssm_b", j))
                act.activation(xbc[:, j, SEQ:TOK].rearrange("p (b t) -> p b t", b=NB),
                               conv_pieces(cv, SKW)[2], ACT.Silu, bias=param("ssm_b", j)).then_inc(sem("xbc_done"), 1)

            def evac_x(i, s):
                b = 4 * i + s
                wait(act, sem("x_conv"), (SKW - 1) * (b - 1))
                wait(act, sem("tail_x"), 2 * (b - 1))
                if b < 2:
                    act.wait_ge(acc_free[1], 4)
                to_line(s % 2, s % 2, SKW)
                act.wait_ge(acc_free[s % 2], ph["X"].pair(i, s) + 1)
                act.wait_ge(sem("x_hist"), b + 1)
                if b < 2:
                    act.wait_ge(sem("zeros_x"), 1)
                n = line(SKW) - SKW + 1
                act.activation(T(2 + s % 2, n), temps[:, s % 2, 0:n], ACT.Copy, scale=param("ssm_w", b * SKW))\
                    .then_inc(sem("x_first"), 1)
                if b >= 1:
                    silu_x(b - 1)
            act_phase(act, "X", evac_x, unroll=True, between=lambda i, s: tap_products(ACT_TAPS[1]))
            tap_products(CKW)
            silu_x(11)

            root("gl", CONF)
            act.wait_ge(sem("dt_sum"), 1)
            act.activation(dt_rows[:, 0:SEQ], misc[0:HEADS, 2], ACT.Copy)
            act.activation(dt_rows[:, SEQ:TOK], misc[0:HEADS, 1, 0:SMP], ACT.Copy).then_inc(sem("dt_rows"), 1)
            act.wait_ge(sem("dt_abs"), 1)
            act.activation(small[:, EXPN], small[:, ABS], ACT.Exp, scale=-1.0).then_inc(sem("dt_exp"), 1)
            act.activation(bias_rows[:, 1], bias_rows[:, 1], ACT.Exp).then_inc(sem("dt_exp"), 1)
            for c in range(NCH + 1):
                act.wait_ge(sem("v_turned"), c + 1)
                if c < NCH:
                    act.activation(vnat[:, c], misc[:, c], ACT.Copy).then_inc(sem("vnat"), 1)
                else:
                    act.activation(vnat[0:SMP, c], misc[0:SMP, 0], ACT.Copy).then_inc(sem("vnat"), 1)
            act.wait_ge(sem("tap_added"), CKW - 1)
            hi_blocks("gm", 4, lambda j: u_sb[:, j], lambda j: branch[:, gmlp_at(j)[0]])

            def evac_branch(name, g, n0):
                def evac(i, s):
                    j = i * 2 + s // 2
                    if s % 2 == 0:
                        wait(act, sem("merged"), j + (n0 - 1))
                        act.activation(halves(T(s // 2)), acc(0), ACT.Sigmoid,
                                       bias=param("b_gate", i * 2 + (8 * g + s // 2))).then_inc(acc_free[0], 1)
                    else:
                        wait(act, sem("merged"), j + n0)
                        act.activation(halves(T(2)), acc(1), ACT.Copy).then_inc(acc_free[1], 1)
                return evac

            def beside_g2(i, s):
                if (i, s) == (0, 2):
                    act.wait_ge(sem("to_end_arg"), 2)
                    act.activation(small[:, TO_END], small[:, TO_END], ACT.Exp).then_inc(sem("dec_exp"), 1)
                    act.activation(small[:, DECAY, 0:NCH * HEADS], small[:, TOTAL, 0:NCH * HEADS], ACT.Exp)\
                        .then_inc(sem("dec_exp"), 1)
                if (i, s) == (0, 3):
                    act.wait_ge(sem("a_turned"), 1)
                    act.activation(a_split[0:HEADS, 0:SEQ], misc[0:HEADS, 2], ACT.Copy)
                    act.activation(a_split[0:HEADS, SEQ:TOK], misc[0:HEADS, 3, 256:256 + SMP], ACT.Copy)\
                        .then_inc(sem("a_hi"), 1)
                if (i, s) == (1, 2):
                    root("cf", CONF)
                if i == 2:
                    act.wait_ge(sem("cf_scaled"), s + 1)
                    act.wait_ge(sem("stored_a"), 16 * 8)
                    act.activation(ca[:, s], ca[:, s], ACT.Silu, bias=param("conf_ln_b", s))\
                        .then_inc(sem("cf_f32"), 1)
                    act.wait_ge(sem("cf_f32"), s + 1)
                    act.activation(branch[:, conf_at(s)[0]], ca[:, s], ACT.Copy).then_inc(sem("cf_hi"), 1)
                if i == 3:
                    act.wait_ge(sem("cf_lo"), 4)
                    act.wait_ge(sem("xb_turned"), s + 1)
                    act.activation(bnat[:, s], misc[:, 2, 0:2 * STATE], ACT.Copy).then_inc(sem("bnat"), 1)
            act.wait_ge(sem("xbc_done"), 12)
            act.wait_ge(sem("tail_x"), 24)
            p = ph["G2"]
            ev = evac_branch("G2", 2, 0)
            for i in range(p.quads):
                act_quad(act, p, i, (p, i + 1) if i + 1 < p.quads else after(p), ev, beside_g2)

            groups = head_groups()

            def beside_g0(i, s):
                for h in groups[4 * i + s]:
                    act.wait_ge(sem("diff"), h + 1)
                    act.activation(T(4 + h % 2, SEQ), T(4 + h % 2, SEQ), ACT.Exp).then_inc(sem("pair_decay"), 1)
                    if h >= 2:
                        act.wait_ge(sem("y_head"), h - 1)
                    act.activation(c_dec[:, h % 2], misc[:, h % 2], ACT.Exp).then_inc(sem("a_exp"), 1)
            ev = evac_branch("G0", 0, 8)
            p = ph["G0"]
            for i in range(p.quads):
                act_quad(act, p, i, (p, i + 1) if i + 1 < p.quads else after(p), ev, beside_g0)
            act.wait_ge(sem("merged"), 16)

            def evac_z(i, s):
                b = 4 * i + s
                wait(act, sem("yz"), b - 1)
                act.activation(halves(T(s % 2)), acc(s % 2), ACT.Silu).then_inc(acc_free[s % 2], 1)

            def beside_z(i, s):
                if (i, s) == (0, 1):
                    act.wait_ge(sem("xb_turned"), NCH + 1)
                    act.activation(b_stack[0:32], misc[0:SMP, 2, 0:2 * STATE], ACT.Copy)
                    act.activation(b_stack[32:64], misc[0:SMP, 2, 0:2 * STATE], ACT.Copy).then_inc(sem("bnat"), 1)
                if (i, s) == (0, 2):
                    act.wait_ge(sem("s_diff"), 1)
                    act.activation(temps[0:SMP, 4, 0:512], temps[0:SMP, 4, 0:512], ACT.Exp).then_inc(sem("s_exp"), 1)
                    act.activation(T(5, 512), misc[:, 0], ACT.Exp).then_inc(sem("s_exp"), 1)
                    act.wait_ge(sem("xw"), NCH + 1)
                    act.activation(xw_stack[0:32], xw_s, ACT.Copy)
                    act.activation(xw_stack[64:96], xw_s, ACT.Copy).then_inc(sem("xw_hi"), 1)
            act_phase(act, "Z", evac_z, unroll=True, between=beside_z)
            sqrt_table()
            root("ns", D)
            hi_blocks("ssm", KD, norm_block, lambda j: branch[:, ssm_at(j)[0]])
            ev = evac_branch("G1", 1, 16)
            p = ph["G1"]
            act_quad(act, p, 0, (p, 1), ev)
            loop(act, 1, 3, lambda i: act_quad(act, p, i, (p, i + 1), ev))
            def merged_hi(blocks):
                for j in blocks:
                    act.wait_ge(sem("merged"), 17 + j)
                    act.activation(branch[:, mixed_at(j)[0]], mixed[:, j], ACT.Copy).then_inc(sem("mx_hi"), 1)
            merged_hi(range(4))
            act_quad(act, p, 3, after(p), ev)
            merged_hi(range(4, KD))
            act_phase(act, "WO", lambda i, s: None, unroll=True)
            sqrt_table()
            root("n2", D)
            hi_blocks("n2", KD, norm_block, lambda j: h_split[:, j, 0])

            def up(name, f0):
                p = ph[name]


                def quad(i, ahead):
                    for r in range(2):
                        f = i * 2 + (f0 + r)
                        s = 2 * r
                        act.wait_ge(acc_full[0], p.pair(i, s) + 1)
                        wait(act, sem("f_conv"), i * (2 * FKW) + FKW * (f0 + r - 1))
                        wait(act, sem("tail_f"), i * 4 + 2 * (f0 + r - 1))
                        to_line(0, r, FKW)
                        split_hi(act, ahead[0], ahead[1], s)
                        act.wait_ge(sem("f_conv"), i * (2 * FKW) + FKW * (f0 + r + 1))
                        act.activation(T(2 + r, SEQ + NB * (FKW - 1 + TS)), T(2 + r, SEQ + NB * (FKW - 1 + TS)),
                                       ACT.Silu, bias=param("ffn_b", f)).then_inc(sem("f_silu"), 1)
                        act.wait_ge(acc_full[1], p.pair(i, s) + 1)
                        split_hi(act, ahead[0], ahead[1], s + 1)
                        act.wait_ge(acc_free[1], p.pair(i, s) + 1)
                        act.activation(pick(branch, i * 2 + r), T(4 + r), ACT.Copy).then_inc(sem("f_hi"), 1)
                if f0 == 0:
                    act.wait_ge(sem("zeros_f"), 1)
                    quad(0, (p, 1))
                    loop(act, 1, p.quads - 1, lambda i: quad(i, (p, i + 1)))
                else:
                    loop(act, 0, p.quads - 1, lambda i: quad(i, (p, i + 1)))
                quad(p.quads - 1, after(p))
            up("U1", 0)
            act_phase(act, "D1", lambda i, s: None)
            up("U2", FFA)
            act_phase(act, "D2", lambda i, s: None)
            sqrt_table()
            root("nf", D)

        @block.tensor
        def _(pe):
            def channel_sum(src, done):
                for half in range(2):
                    mm = pe.matmul(misc[:, half, 0:HALF], ones, src[:, tokens(half)], start=True, stop=True)
                mm.then_inc(done, 1)

            groups = [(h * HALF + o, n) for h in range(2) for o, n in ((0, P), (P, P), (HALF - P, HALF - 2 * P))]

            def token_sum(src):
                for c, (t0, _) in enumerate(groups):
                    mm = pe.matmul(misc[:, 3, c:c + 1], src[:, t0:t0 + P], ones[:, 0:1], start=True, stop=True)
                mm.then_inc(sem("rms_sum"), 1)

            def keep_warm(n):
                for _ in range(n):
                    pe.matmul(misc[:, 2, 0:P], ones, ident, start=True, stop=True)

            def spread_rms(name):
                pe.wait_ge(sem("rms_inverse"), nth(name))
                for c, (t0, n) in enumerate(groups):
                    at = t0 % HALF + P - n
                    mm = pe.matmul(misc[:, c // 3, at:at + n], rms[:, 1, c:c + 1].to_broadcast([P, P]),
                                   ident[:, P - n:P], start=True, stop=True)
                mm.then_inc(sem("rms_spread"), 1)

            def lo_ready(name, slots=(0,)):
                def ready(s, k):
                    if s == slots[0]:
                        pe.wait_ge(sem(name + ("_lo", "_lo_odd")[k % 2]), k // 2 + 1)
                return ready

            def in_order(name, slots):
                def ready(s, k):
                    if s in slots:
                        pe.wait_ge(sem(name), k + 1 + slots[s])
                return ready

            pe.wait_ge(sem("consts_landed"), 16)
            keep_warm(WARM[0])
            pe.wait_ge(sem("n1_added"), KD - 1)
            token_sum(T(2))
            keep_warm(WARM[1])
            spread_rms("n1")
            keep_warm(WARM[2])
            p = ph["A"]
            pe_quad(pe, p, 0, h_rhs, lo_ready("n1"))
            pe_quad(pe, p, 1, h_rhs)
            pe_phase(pe, "VU", h_rhs)
            p = ph["X"]
            pe_quad(pe, p, 0, h_rhs)
            pe.wait_ge(sem("gl_sum"), 1)
            channel_sum(T(4), sem("gl_mean"))
            pe_quad(pe, p, 1, h_rhs)
            pe_quad(pe, p, 2, h_rhs)
            pe.wait_ge(sem("gl_sq"), 1)
            token_sum(T(4))
            pe.wait_ge(sem("dt_w"), 1)
            for k in range(KD):
                for n, (wp, xp) in enumerate(((0, 0), (0, 1), (1, 0))):
                    for bank, cols in ((2, slice(0, SEQ)), (1, slice(SEQ, TOK))):
                        mm = pe.matmul(misc[0:HEADS, bank, 0:cols.stop - cols.start], w_dt_split[:, wp, k],
                                       h_split[:, k, xp, cols],
                                       start=(k == 0 and n == 0), stop=(k == KD - 1 and n == 2))
            mm.then_inc(sem("dt_sum"), 1)
            pe.wait_ge(sem("dt_rows"), 1)
            spread_rms("gl")

            def turn_dt():
                pe.wait_ge(sem("dt_rows"), 1)
                for c in range(NCH):
                    pe.transpose(misc[:, 2, c * HEADS:(c + 1) * HEADS], dt_rows[:, c * CH:(c + 1) * CH],
                                 ident[0:HEADS, 0:HEADS])
                pe.transpose(misc[0:SMP, 2, NCH * HEADS:(NCH + 1) * HEADS], dt_rows[:, SEQ:TOK],
                             ident[0:HEADS, 0:HEADS]).then_inc(sem("dt_raw"), 1)

            def turn_vn():
                pe.wait_ge(sem("vn_done"), 4)
                for c in range(NCH):
                    if c == 2:
                        pe.wait_ge(sem("dt_read"), 1)
                    for j in range(4):
                        mm = pe.transpose(misc[:, c, j * P:(j + 1) * P], v_sb[:, j, c * CH:(c + 1) * CH], ident)
                    mm.then_inc(sem("v_turned"), 1)
                pe.wait_ge(sem("vnat"), 1)
                for j in range(4):
                    mm = pe.transpose(misc[0:SMP, 0, j * P:(j + 1) * P], v_sb[:, j, SEQ:TOK], ident)
                mm.then_inc(sem("v_turned"), 1)

            def mix_tokens():
                pe.wait_ge(sem("vnat"), NCH + 1)
                pe.wait_ge(sem("ws_masked"), 2)
                for g in range(4):
                    b0 = 2 * (g % 2)
                    if g >= 2:
                        pe.wait_ge(sem("mix_read"), g - 1)
                    for c in range(NCH):
                        pe.matmul(misc[:, b0, c * CH:(c + 1) * CH], vnat[:, c, g * P:(g + 1) * P], ws_t[:, g],
                                  start=True, stop=True)
                    pe.matmul(misc[:, b0 + 1, 0:SMP], vnat[0:SMP, NCH, g * P:(g + 1) * P], ws_s[:, g],
                              start=True, stop=True).then_inc(sem("mix"), 1)

            n4 = NCH * HEADS

            def cumulate():
                pe.wait_ge(sem("adt"), 1)
                pe.matmul(misc[:, 3, 0:n4], tri, small[:, ADT, 0:n4], start=True, stop=True)
                pe.matmul(misc[0:SMP, 3, n4:n4 + HEADS], mask_s[:, 0], small[0:SMP, ADT, n4:n4 + HEADS],
                          start=True, stop=True)
                pe.matmul(misc[:, 3, 80:80 + n4], ones, small[:, ADT, 0:n4], start=True, stop=True)
                pe.matmul(misc[0:SMP, 3, 80 + n4:160], mask_s[:, 1], small[0:SMP, ADT, n4:n4 + HEADS],
                          start=True, stop=True).then_inc(sem("cum"), 1)

            def turn_rows():
                pe.wait_ge(sem("to_end_arg"), 2)
                for c in range(NCH):
                    pe.transpose(misc[0:HEADS, 2, c * CH:(c + 1) * CH], small[:, A_CUM, c * HEADS:(c + 1) * HEADS],
                                 ident)
                pe.transpose(misc[0:HEADS, 3, 256:256 + SMP], small[0:SMP, A_CUM, n4:n4 + HEADS],
                             ident[0:SMP, 0:SMP]).then_inc(sem("a_turned"), 1)

            def turn_xb(c):
                if c == 0:
                    pe.wait_ge(sem("cf_scaled"), 4)
                    pe.wait_ge(sem("a_rows"), 1)
                elif c < NCH:
                    pe.wait_ge(sem("xdt"), 2 * c)
                    pe.wait_ge(sem("bnat"), c)
                rows, cols = (P, slice(c * CH, (c + 1) * CH)) if c < NCH else (SMP, slice(SEQ, TOK))
                for j in range(KD):
                    pe.transpose(misc[0:rows, j // 4, (j % 4) * P:(j % 4 + 1) * P], xbc[:, j, cols], ident)
                for g in range(2):
                    mm = pe.transpose(misc[0:rows, 2, g * P:(g + 1) * P], xbc[:, 8 + g, cols], ident)
                mm.then_inc(sem("xb_turned"), 1)

            def chunk_sum(c):
                if c == 0:
                    pe.wait_ge(sem("xdt"), 2 * NCH)
                    pe.wait_ge(sem("bnat"), NCH)
                pe.wait_ge(sem("xw"), c + 1)
                for g in range(2):
                    b0 = 2 * (c % 2) + g
                    if c >= 2:
                        pe.wait_ge(sem("chunk_state"), 2 * (c - 2) + g + 1)
                    pe.matmul(misc[:, b0], bnat[:, c, g * STATE:(g + 1) * STATE], xw[:, c % 2, g * 512:(g + 1) * 512],
                              start=True, stop=True).then_inc(sem("chunk_sum"), 1)

            def cb_products():
                for g in range(2):
                    pe.wait_ge(sem("chunk_state"), 4 + 1 + g)
                    for c in range(NCH):
                        cols = slice(c * CH, (c + 1) * CH)
                        mm = pe.matmul(misc[:, g, cols], xbc[:, 8 + g, cols], xbc[:, 10 + g, cols],
                                       start=True, stop=True)
                    mm.then_inc(sem("cb"), 1)

            def spread(h):
                if h == 0:
                    pe.wait_ge(sem("cbm"), 2)
                if h >= 2:
                    pe.wait_ge(sem("a_exp"), h - 1)
                pe.matmul(misc[:, h % 2], head_of[0:48, h:h + 1].to_broadcast([48, P]), a_split[0:48, 0:SEQ],
                          start=True, stop=True).then_inc(sem("a_spread"), 1)

            def y_head(h):
                b0, rows = 2 + (h // 2) % 2, slice((h % 2) * HD, (h % 2 + 1) * HD)
                if h == 0:
                    pe.wait_ge(sem("chunk_state"), 2 * NCH)
                if h % 2 == 0 and h >= 4:
                    pe.wait_ge(sem("y_sum"), h // 2 - 1)
                pe.wait_ge(sem("mix_head"), h + 1)
                pe.wait_ge(sem("c_decayed"), h + 1)
                for c in range(NCH):
                    cols = slice(c * CH, (c + 1) * CH)
                    mm = pe.matmul(misc[rows, b0, cols], xdt[:, c, h * HD:(h + 1) * HD], T(4 + h % 2, SEQ)[:, cols],
                                   start=True, stop=(c == 0))
                    if c:
                        mm = pe.matmul(misc[rows, b0, cols], h_chunk[:, c - 1, h * HD:(h + 1) * HD],
                                       c_dec[:, h % 2, cols], start=False, stop=True)
                mm.then_inc(sem("y_head"), 1)

            def beside_g2(i):
                def between(s):
                    if (i, s) == (0, 0):
                        turn_dt()
                        turn_vn()
                        mix_tokens()
                    if (i, s) == (0, 1):
                        cumulate()
                    if (i, s) == (0, 2):
                        turn_rows()
                    if (i, s) == (1, 0):
                        pe.wait_ge(sem("cf_sum"), 1)
                        channel_sum(T(4), sem("cf_mean"))
                    if (i, s) == (1, 2):
                        pe.wait_ge(sem("a_rows"), 1)
                        pe.wait_ge(sem("cf_sq"), 1)
                        token_sum(T(4))
                    if (i, s) == (1, 3):
                        spread_rms("cf")
                    if i == 3:
                        turn_xb(s)
                return between
            p = ph["G2"]
            rhs = merge_rhs(gmlp_at)
            for i in range(p.quads):
                pe_quad(pe, p, i, rhs, in_order("gm_lo", {1: 0}) if i == 0 else None, beside_g2(i))

            heads = head_groups()

            def beside_g0(i):
                def between(s):
                    if i == 0:
                        chunk_sum(s)
                    if (i, s) == (1, 0):
                        cb_products()
                    k = 4 * i + s
                    for h in heads[k - 1] if k else ():
                        y_head(h)
                    for h in heads[k]:
                        spread(h)
                return between
            p = ph["G0"]
            rhs = merge_rhs(conf_at)
            for i in range(p.quads):
                pe_quad(pe, p, i, rhs, in_order("cf_lo", {1: 0}) if i == 0 else None, beside_g0(i))
            def turn_samples():
                pe.wait_ge(sem("a_exp"), HEADS)
                pe.wait_ge(sem("y_sum"), 8)
                turn_xb(NCH)
                for g in range(2):
                    mm = pe.matmul(misc[0:SMP, 3, g * SMP:(g + 1) * SMP], xbc[:, 8 + g, SEQ:TOK],
                                   xbc[:, 10 + g, SEQ:TOK], start=True, stop=True)
                mm.then_inc(sem("cb"), 1)

            def spread_samples():
                pe.wait_ge(sem("xdt"), 2 * NCH + 2)
                for h in range(HEADS):
                    mm = pe.matmul(misc[:, 0, h * SMP:(h + 1) * SMP], head_of[0:48, h:h + 1].to_broadcast([48, P]),
                                   a_split[0:48, SEQ:TOK], start=True, stop=True)
                mm.then_inc(sem("s_spread"), 1)

            def y_new_tokens():
                pe.wait_ge(sem("s_mix"), 1)
                pe.wait_ge(sem("b_masked"), 1)
                for h in range(HEADS):
                    rows = slice((h % 2) * HD, (h % 2 + 1) * HD)
                    mm = pe.matmul(misc[rows, 2, 256 + (h // 2) * SMP:256 + (h // 2 + 1) * SMP], xdt_s[:, h * HD:(h + 1) * HD],
                                   temps[0:SMP, 4, h * SMP:(h + 1) * SMP], start=True, stop=True)
                mm.then_inc(sem("s_diag"), 1)

            def sample_state(b):
                if b == 0:
                    pe.wait_ge(sem("cbm"), 3)
                    pe.wait_ge(sem("xw_split"), 1)
                pe.wait_ge(sem(f"h0_landed{b % H0_BUFS}"), 16 * (b // H0_BUFS + 1))
                for j in range(KD):
                    g = j // 4
                    mm = pe.matmul(misc[:, 2, j * SMP + TS * b:j * SMP + TS * b + TS],
                                   h0[b % H0_BUFS][:, j * P:(j + 1) * P],
                                   xbc[:, 10 + g, SEQ + TS * b:SEQ + TS * b + TS], start=True, stop=True)
                mm.then_inc(sem("s_off"), 1)
                pe.wait_ge(sem("b_masked"), b + 1)
                for g in range(2):
                    if 2 * b + g >= 3:
                        pe.wait_ge(sem("h0_new"), 2 * b + g - 2)
                    else:
                        pe.wait_ge(sem("s_exp"), 2)
                    pe.matmul(misc[:, sum_bank(b, g)], b_alone[:, b % 2, g * STATE:(g + 1) * STATE],
                              xw_stack[:, g * 512:(g + 1) * 512],
                              start=True, stop=True).then_inc(sem("s_sum"), 1)

            def beside_z(i):
                def between(s):
                    if (i, s) == (0, 0):
                        for h in heads[-1]:
                            y_head(h)
                    if (i, s) == (0, 1):
                        turn_samples()
                    if (i, s) == (0, 2):
                        spread_samples()
                    if (i, s) == (0, 3):
                        y_new_tokens()
                    for b in sample_groups()[4 * i + s]:
                        sample_state(b)
                return between
            for i in range(ph["Z"].quads):
                pe_quad(pe, ph["Z"], i, h_rhs, between=beside_z(i))
            def norm_ssm(s):
                if s == 0:
                    pe.wait_ge(sem("yz_sq"), 1)
                    token_sum(T(2))
                    keep_warm(WARM[1])
                    spread_rms("ns")
                    keep_warm(WARM[2])
            pe_quad(pe, ph["G1"], 0, merge_rhs(ssm_at), lo_ready("ssm", (1,)), norm_ssm)
            loop(pe, 1, ph["G1"].quads, lambda i: pe_quad(pe, ph["G1"], i, merge_rhs(ssm_at)))
            pe_phase(pe, "WO", branch_rhs(mixed_at), in_order("mx_lo", {0: 0}))
            keep_warm(WARM[3])
            pe.wait_ge(sem("x2_sq"), 1)
            token_sum(T(5))
            keep_warm(WARM[1])
            spread_rms("n2")
            keep_warm(WARM[2])
            pe_phase(pe, "U1", h_rhs, lo_ready("n2"))
            pe_phase(pe, "D1", down_rhs(FFA // 2), in_order("f_lo", {0: 0, 1: FFA // 2}))
            pe_phase(pe, "U2", h_rhs)
            pe_phase(pe, "D2", down_rhs(FFB // 2), in_order("f_lo", {0: FFA, 1: FFA + FFB // 2}))
            keep_warm(WARM[3])
            pe.wait_ge(sem("x3_sq"), 1)
            token_sum(T(5))
            keep_warm(WARM[1])
            spread_rms("nf")

        @block.vector
        def _(dve):
            chained = [0]

            def link(ins_):
                chained[0] += 1
                ins_.then_inc(sem("dve_chain"), 1)
                dve.wait_ge(sem("dve_chain"), chained[0])

            def operand(name, n, produce, tmp, lo):
                for j in range(n + 1):
                    if j < n:
                        if j >= 4:
                            dve.wait_ge(sem(name + ("_lo", "_lo_odd")[j % 2]), j // 2 - 1)
                        produce(j).then_inc(sem(name + "_f32"), 1)
                    if j % 2:
                        i = j - 1
                        dve.wait_ge(sem(name + "_hi"), i + 1)
                        hi, dst = lo(i)
                        dve.tensor_tensor(dst, tmp(i), hi.bitcast(F32), ALU.subtract).then_inc(sem(name + "_lo"), 1)

            def inverse(name):
                dve.wait_ge(sem("rms_root"), nth(name))
                dve.reciprocal(rms[:, 1], rms[:, 0]).then_inc(sem("rms_inverse"), 1)

            def rstd(name):
                inverse(name)
                dve.wait_ge(sem("rms_spread"), nth(name))

            dve.wait_ge(sem("rows_zero"), 1)
            link(dve.tensor_copy(a_split[:, :], temps[0:64, 5, 0:TOK]))
            for j in range(1, KD):
                dve.wait_ge(sem("n1_sq"), j + 1)
                if j >= 2:
                    dve.wait_ge(sem("n1_added"), j - 1)
                dve.tensor_tensor(T(2), T(0) if j == 1 else T(2), T(j % 2), ALU.add).then_inc(sem("n1_added"), 1)
            rstd("n1")
            dve.wait_ge(sem("params_landed"), 16)

            def scaled(name):
                return lambda j: dve.scalar_tensor_tensor(out=halves(norm_block(j)), in0=halves(xbc[:, j]),
                                                          scalar=param(name, j), in1=stat, op0=ALU.mult, op1=ALU.mult)
            operand("n1", KD, scaled("norm1_g"), norm_block, h_parts)
            dve.wait_ge(sem("small_landed"), 16 * 6)
            dve.tensor_copy(head_of[:, :], heads_f32[:, :])
            link(dve.tensor_copy(w_dt_split[:, 0], w_dt[:, :, :]))
            dve.tensor_tensor(w_dt_split[:, 1], w_dt[:, :, :], w_dt_split[:, 0].bitcast(F32), ALU.subtract)\
                .then_inc(sem("dt_w"), 1)
            dve.wait_ge(sem("hist_a_landed"), 64)
            for b in range(4):
                dve.wait_ge(acc_full[1], b + 1)
                dve.wait_ge(acc_free[0], b + 1)
                for src, sig, dst in zip(acc_pieces(1), [T(b % 2)[:, 0:HALF], T(b % 2)[:, HALF:SEQ],
                                                         T(b % 2)[:, SEQ:].rearrange("p (b t) -> p b t", b=NB)],
                                         line_pieces(line_a[:, b], CKW)):
                    ins_ = dve.tensor_tensor(dst, src, sig, ALU.mult)
                ins_.then_inc(acc_free[1], 1)

            dve.wait_ge(acc_free[1], 4)
            dve.wait_ge(sem("zeros_a"), 1)
            taps = [(b, t) for pair in (0, 2) for t in range(CKW) for b in (pair, pair + 1)]
            tap_at = {}

            def conf_taps(n):
                for _ in range(min(n, len(taps))):
                    b, t = taps.pop(0)
                    w = param("conf_w", b * CKW + t)
                    pieces = [(samples(line_a[:, b], CKW - 1 + SEQ, CKW)[:, :, t:t + TS],
                               ca[:, b, SEQ:TOK].rearrange("p (b t) -> p b t", b=NB))]
                    if b != CONF_SHARED:
                        pieces.insert(0, (line_a[:, b, t:t + SEQ], ca[:, b, 0:SEQ]))
                    if t:
                        dve.wait_ge(sem("dve_chain"), tap_at[b])
                    for src, dst in pieces:
                        if t == 0:
                            ins_ = dve.tensor_scalar(dst, src, w, param("conf_b", b), ALU.mult, ALU.add)
                        else:
                            ins_ = dve.scalar_tensor_tensor(out=dst, in0=src, scalar=w, in1=dst,
                                                            op0=ALU.mult, op1=ALU.add)
                    chained[0] += 1
                    tap_at[b] = chained[0]
                    ins_.then_inc(sem("dve_chain"), 1)

            def x_conv(f):
                par, n = f % 2, line(SKW) - SKW + 1
                dve.wait_ge(sem("x_first"), f + 1)
                cv = T(2 + par, n)
                for t in range(1, SKW):
                    src, w = temps[:, par, t:t + n], param("ssm_w", f * SKW + t)
                    if t > 1:
                        conf_taps(1)
                        dve.wait_ge(sem("x_conv"), f * (SKW - 1) + t - 1)
                    dve.scalar_tensor_tensor(out=cv, in0=src, scalar=w, in1=cv, op0=ALU.mult, op1=ALU.add)\
                        .then_inc(sem("x_conv"), 1)

            def four_sum(src, done):
                link(dve.tensor_tensor(T(4), src[:, 0], src[:, 1], ALU.add))
                link(dve.tensor_tensor(T(4), T(4), src[:, 2], ALU.add))
                dve.tensor_tensor(T(4), T(4), src[:, 3], ALU.add).then_inc(done, 1)

            def center(src, name):
                dve.wait_ge(sem(name + "_mean"), 1)
                for j in range(4):
                    ins_ = dve.scalar_tensor_tensor(out=halves(src[:, j]), in0=stat, scalar=-1.0 / CONF,
                                                    in1=halves(src[:, j]), op0=ALU.mult, op1=ALU.add)
                link(ins_)
                dve.tensor_tensor(T(4), src[:, 0], src[:, 0], ALU.mult)
                for j in range(1, 4):
                    link(dve.tensor_tensor(T(5), src[:, j], src[:, j], ALU.mult))
                    ins_ = dve.tensor_tensor(T(4), T(4), T(5), ALU.add)
                    if j < 3:
                        link(ins_)
                ins_.then_inc(sem(name + "_sq"), 1)

            def scale(src, name, gain, done):
                dve.wait_ge(sem("rms_spread"), nth(name))
                for j in range(4):
                    dve.scalar_tensor_tensor(out=halves(src[:, j]), in0=halves(src[:, j]), scalar=param(gain, j),
                                             in1=stat, op0=ALU.mult, op1=ALU.mult).then_inc(done, 1)

            dve.wait_ge(sem("gmlp_landed"), 16 * GMLP_LOADS)
            dve.tensor_tensor(ws_t, ws_t, tri.unsqueeze(1).to_broadcast([P, 4, CH]), ALU.mult)\
                .then_inc(sem("ws_masked"), 1)
            dve.tensor_tensor(ws_s, ws_s, mask_s[:, 0].unsqueeze(1).to_broadcast([SMP, 4, SMP]), ALU.mult)\
                .then_inc(sem("ws_masked"), 1)
            conf_taps(68)
            dve.wait_ge(acc_free[0], 6)
            dve.wait_ge(acc_free[1], 6)
            four_sum(v_sb, sem("gl_sum"))
            for f in range(12):
                x_conv(f)
                conf_taps(X_TAPS)
                if f == 3:
                    center(v_sb, "gl")
            inverse("gl")
            conf_taps(CONF_TAPS)
            scale(v_sb, "gl", "gmlp_ln_g", sem("vn_scaled"))
            dve.wait_ge(sem("vn_scaled"), 4)
            for j in range(4):
                dve.tensor_scalar(v_sb[:, j], v_sb[:, j], param("gmlp_ln_b", j), None, ALU.add)\
                    .then_inc(sem("vn_done"), 1)

            def sm(q):
                return small[:, q]

            def by_head(ap):
                return ap.rearrange("p (c h) -> p c h", h=HEADS)
            dve.memset(small[:, X_DT], 0.0).then_inc(sem("dve_chain"), 1)
            chained[0] += 1
            dve.wait_ge(sem("dve_chain"), chained[0])
            dve.wait_ge(sem("dt_raw"), 1)
            n4 = NCH * HEADS
            dve.tensor_tensor(by_head(small[:, X_DT, 0:n4]), by_head(misc[:, 2, 0:n4]),
                              bias_rows[:, 0].unsqueeze(1).to_broadcast([P, NCH, HEADS]), ALU.add)
            dve.tensor_tensor(small[0:SMP, X_DT, n4:], misc[0:SMP, 2, n4:n4 + HEADS], bias_rows[0:SMP, 0], ALU.add)\
                .then_inc(sem("dt_read"), 1)
            dve.wait_ge(sem("dt_read"), 1)
            link(dve.tensor_scalar(sm(ABS), sm(X_DT), -1.0, None, ALU.mult))
            dve.tensor_tensor(sm(ABS), sm(ABS), sm(X_DT), ALU.max).then_inc(sem("dt_abs"), 1)
            dve.wait_ge(sem("dt_exp"), 1)
            link(dve.tensor_scalar(sm(RATIO), sm(EXPN), 2.0, None, ALU.add))
            link(dve.reciprocal(sm(RATIO2), sm(RATIO)))
            link(dve.tensor_tensor(sm(RATIO), sm(EXPN), sm(RATIO2), ALU.mult))
            link(dve.tensor_tensor(sm(RATIO2), sm(RATIO), sm(RATIO), ALU.mult))
            link(dve.tensor_scalar(sm(POLY), sm(RATIO2), 1.0 / 17, None, ALU.mult))
            for d in range(15, 1, -2):
                link(dve.scalar_tensor_tensor(out=sm(POLY), in0=sm(POLY), scalar=1.0 / d, in1=sm(RATIO2),
                                              op0=ALU.add, op1=ALU.mult))
            link(dve.scalar_tensor_tensor(out=sm(POLY), in0=sm(POLY), scalar=1.0, in1=sm(RATIO),
                                          op0=ALU.add, op1=ALU.mult))
            link(dve.tensor_scalar(sm(X_DT), sm(X_DT), 0.0, None, ALU.max))
            link(dve.scalar_tensor_tensor(out=sm(DT), in0=sm(POLY), scalar=2.0, in1=sm(X_DT), op0=ALU.mult,
                                          op1=ALU.add))
            dve.wait_ge(sem("dt_exp"), 2)
            dve.scalar_tensor_tensor(out=sm(ADT).rearrange("p (c h) -> p c h", h=HEADS),
                                     in0=sm(DT).rearrange("p (c h) -> p c h", h=HEADS), scalar=-1.0,
                                     in1=bias_rows[:, 1].unsqueeze(1).to_broadcast([P, NCH + 1, HEADS]),
                                     op0=ALU.mult, op1=ALU.mult).then_inc(sem("adt"), 1)

            def gmlp_lo(g):
                dve.wait_ge(sem("gm_hi"), g + 1)
                dve.tensor_tensor(branch[:, gmlp_at(g)[1]], u_sb[:, g], branch[:, gmlp_at(g)[0]].bitcast(F32),
                                  ALU.subtract).then_inc(sem("gm_lo"), 1)

            for g in range(4):
                b0 = 2 * (g % 2)
                dve.wait_ge(sem("mix"), g + 1)
                wait(dve, sem("gm_f32"), g)
                dve.tensor_tensor(T(4, SEQ).rearrange("p (c t) -> p c t", c=NCH),
                                  misc[:, b0].rearrange("p (c t) -> p c t", c=NCH),
                                  bs[:, g].unsqueeze(1).to_broadcast([P, NCH, CH]), ALU.add)
                dve.tensor_tensor(temps[:, 4, SEQ:TOK].rearrange("p (b t) -> p b t", b=NB),
                                  misc[:, b0 + 1, 0:SMP].rearrange("p (b t) -> p b t", b=NB),
                                  bs[:, g, 0:TS].unsqueeze(1).to_broadcast([P, NB, TS]), ALU.add)\
                    .then_inc(sem("mix_read"), 1)
                dve.wait_ge(sem("mix_read"), g + 1)
                dve.tensor_tensor(u_sb[:, g], u_sb[:, g], T(4), ALU.mult).then_inc(sem("gm_f32"), 1)
                if g:
                    gmlp_lo(g - 1)
            gmlp_lo(3)

            dve.wait_ge(sem("cum"), 1)
            dve.tensor_copy(small[:, A_CUM, 0:n4], misc[:, 3, 0:n4])
            dve.tensor_copy(small[0:SMP, A_CUM, n4:], misc[0:SMP, 3, n4:n4 + HEADS])
            dve.tensor_copy(small[:, TOTAL, 0:n4], misc[:, 3, 80:80 + n4])
            link(dve.tensor_copy(small[0:SMP, TOTAL, n4:], misc[0:SMP, 3, 80 + n4:160]))
            dve.memset(small[:, TO_END, n4:], 0.0).then_inc(sem("dve_chain"), 1)
            chained[0] += 1
            dve.tensor_tensor(small[:, TO_END, 0:n4], small[:, TOTAL, 0:n4], small[:, A_CUM, 0:n4], ALU.subtract)\
                .then_inc(sem("to_end_arg"), 1)
            dve.wait_ge(sem("dve_chain"), chained[0])
            dve.tensor_tensor(small[0:SMP, TO_END, n4:], small[0:SMP, TOTAL, n4:], small[0:SMP, A_CUM, n4:],
                              ALU.subtract).then_inc(sem("to_end_arg"), 1)

            conf_taps(4 * CKW)
            dve.wait_ge(sem("dve_chain"), chained[0])
            dve.wait_ge(sem("tap_added"), CKW - 1)
            four_sum(ca, sem("cf_sum"))
            dve.wait_ge(sem("a_hi"), 1)
            dve.tensor_tensor(a_split[32:48, 0:SEQ], misc[0:HEADS, 2], a_split[0:HEADS, 0:SEQ].bitcast(F32),
                              ALU.subtract)
            dve.tensor_tensor(a_split[32:48, SEQ:TOK], misc[0:HEADS, 3, 256:256 + SMP],
                              a_split[0:HEADS, SEQ:TOK].bitcast(F32),
                              ALU.subtract).then_inc(sem("a_rows"), 1)
            center(ca, "cf")
            inverse("cf")
            scale(ca, "cf", "conf_ln_g", sem("cf_scaled"))
            dve.wait_ge(sem("stored_a"), 16 * 8)
            for j in range(4):
                dve.wait_ge(sem("cf_hi"), j + 1)
                dve.tensor_tensor(branch[:, conf_at(j)[1]], ca[:, j], branch[:, conf_at(j)[0]].bitcast(F32),
                                  ALU.subtract).then_inc(sem("cf_lo"), 1)

            def x_times_dt(c):
                rows = P if c < NCH else SMP
                dve.wait_ge(sem("xb_turned"), c + 1)
                for r in range(2):
                    dst = (xdt[:, c] if c < NCH else xdt_s)[:, r * 512:(r + 1) * 512]
                    dve.tensor_tensor(dst.rearrange("p (h d) -> p h d", h=8),
                                      misc[0:rows, r].rearrange("p (h d) -> p h d", h=8),
                                      small[0:rows, DT, c * HEADS + 8 * r:c * HEADS + 8 * r + 8].unsqueeze(2)
                                      .to_broadcast([rows, 8, HD]), ALU.mult).then_inc(sem("xdt"), 1)

            def x_to_end(c):
                dve.wait_ge(sem("xdt"), 2 * (c + 1))
                if 2 <= c < NCH:
                    dve.wait_ge(sem("chunk_sum"), 2 * (c - 1))
                rows, dst, src = (P, xw[:, c % 2], xdt[:, c]) if c < NCH else (SMP, xw_s, xdt_s)
                dve.tensor_tensor(dst.rearrange("p (h d) -> p h d", h=HEADS), src.rearrange("p (h d) -> p h d", h=HEADS),
                                  small[0:rows, TO_END, c * HEADS:(c + 1) * HEADS].unsqueeze(2)
                                  .to_broadcast([rows, HEADS, HD]), ALU.mult).then_inc(sem("xw"), 1)

            def chunk_state(c):
                for g in range(2):
                    cols = slice(g * 512, (g + 1) * 512)
                    bank = misc[:, 2 * (c % 2) + g]
                    dve.wait_ge(sem("chunk_sum"), 2 * c + g + 1)
                    if c == 0:
                        dve.tensor_copy(h_chunk[:, 0, cols], bank).then_inc(sem("chunk_state"), 1)
                        continue
                    dve.wait_ge(sem("chunk_state"), 2 * c + g - 1)
                    dec = small[:, DECAY, c * HEADS + 8 * g:c * HEADS + 8 * g + 8]
                    link(dve.tensor_tensor(T(4 + g, 512).rearrange("p (h d) -> p h d", h=8),
                                           h_chunk[:, c - 1, cols].rearrange("p (h d) -> p h d", h=8),
                                           dec.unsqueeze(2).to_broadcast([P, 8, HD]), ALU.mult))
                    dve.tensor_tensor(h_chunk[:, c, cols], T(4 + g, 512), bank, ALU.add).then_inc(sem("chunk_state"), 1)
            dve.wait_ge(sem("dec_exp"), 2)
            for c in range(NCH):
                x_times_dt(c)
                if c < 2:
                    x_to_end(c)
            for c in range(NCH):
                chunk_state(c)
                if c < 2:
                    x_to_end(c + 2)
            for g in range(2):
                dve.wait_ge(sem("cb"), g + 1)
                dve.tensor_tensor(cbm[:, g].rearrange("p (c i) -> p c i", c=NCH),
                                  misc[:, g].rearrange("p (c i) -> p c i", c=NCH),
                                  tri.unsqueeze(1).to_broadcast([P, NCH, CH]), ALU.mult).then_inc(sem("cbm"), 1)
            dve.wait_ge(sem("cbm"), 2)

            def diffs(h):
                dve.wait_ge(sem("a_spread"), h + 1)
                if h >= 2:
                    dve.wait_ge(sem("y_head"), h - 1)
                for c in range(NCH):
                    cols = slice(c * CH, (c + 1) * CH)
                    ins_ = dve.tensor_scalar(T(4 + h % 2, SEQ)[:, cols], misc[:, h % 2, cols],
                                             small[:, A_CUM, c * HEADS + h:c * HEADS + h + 1], 0.0,
                                             ALU.subtract, ALU.min)
                ins_.then_inc(sem("diff"), 1)

            def y_sum(j):
                dve.wait_ge(sem("y_head"), 2 * j + 2)
                dve.scalar_tensor_tensor(out=xbc[:, j, 0:SEQ], in0=xbc[:, j, 0:SEQ], scalar=param("ssm_d", j),
                                         in1=misc[:, 2 + j % 2], op0=ALU.mult, op1=ALU.add)\
                    .then_inc(sem("y_sum"), 1)
            before = ()
            for group in [g for g in head_groups() if len(g)] + [()]:
                for h in before:
                    if h % 2:
                        y_sum(h // 2)
                for h in group:
                    diffs(h)
                for h in group:
                    dve.wait_ge(sem("pair_decay"), h + 1)
                    dve.tensor_tensor(T(4 + h % 2, SEQ), T(4 + h % 2, SEQ), cbm[:, h // 8], ALU.mult)\
                        .then_inc(sem("mix_head"), 1)
                    dve.wait_ge(sem("a_exp"), h + 1)
                    dve.tensor_tensor(c_dec[:, h % 2], c_dec[:, h % 2], xbc[:, 10 + h // 8, 0:SEQ], ALU.mult)\
                        .then_inc(sem("c_decayed"), 1)
                before = group
            def y_times_z(b):
                y = xbc[:, b, 0:SEQ]
                dve.wait_ge(acc_free[b % 2], ph["Z"].pair0 + b // 2 + 1)
                link(dve.tensor_tensor(y, y, T(b % 2, SEQ), ALU.mult))
                dve.tensor_copy(z_s[:, b], temps[:, b % 2, SEQ:TOK]).then_inc(sem("yz"), 1)
                if b:
                    link(dve.tensor_tensor(T(3, SEQ), y, y, ALU.mult))
                    link(dve.tensor_tensor(T(2, SEQ), T(2, SEQ), T(3, SEQ), ALU.add))
                else:
                    link(dve.tensor_tensor(T(2, SEQ), y, y, ALU.mult))

            def b_masked(b):
                dve.tensor_scalar(b_alone[:, b % 2], b_stack[:, :].bitcast(F32), sample_of[:, b:b + 1], None, ALU.mult)\
                    .then_inc(sem("b_masked"), 1)

            def sample_decays():
                mixs = temps[0:SMP, 4, 0:512]
                dve.wait_ge(sem("s_spread"), 1)
                link(dve.tensor_tensor(mixs.rearrange("p (h i) -> p h i", h=HEADS),
                                       misc[0:SMP, 0].rearrange("p (h i) -> p h i", h=HEADS),
                                       small[0:SMP, A_CUM, n4:].unsqueeze(2).to_broadcast([SMP, HEADS, SMP]),
                                       ALU.subtract))
                dve.tensor_scalar(mixs, mixs, 0.0, None, ALU.min).then_inc(sem("s_diff"), 1)
                dve.wait_ge(sem("s_exp"), 1)
                for g in range(2):
                    half = mixs[:, g * 256:(g + 1) * 256].rearrange("p (h i) -> p h i", h=8)
                    ins_ = dve.tensor_tensor(half, half, cbm_s[:, g].unsqueeze(1).to_broadcast([SMP, 8, SMP]), ALU.mult)
                ins_.then_inc(sem("s_mix"), 1)

            def new_state(b):
                if b + 1 < NB:
                    if b >= 1:
                        dve.wait_ge(sem("s_sum"), 2 * b)
                    b_masked(b + 1)
                dve.wait_ge(sem("s_off"), b + 1)
                if b == 0:
                    dve.wait_ge(sem("s_exp"), 2)
                decayed(dve, b, 1).then_inc(sem("h0_decayed_1"), 1)
                for g in range(2):
                    dve.wait_ge(sem("s_sum"), 2 * b + g + 1)
                    dve.wait_ge(sem(("h0_decayed", "h0_decayed_1")[g]), b + 1)
                    hv = h0[b % H0_BUFS][:, g * 512:(g + 1) * 512]
                    dve.tensor_tensor(hv, hv, misc[:, sum_bank(b, g)], ALU.add).then_inc(sem("h0_new"), 1)
            for k in range(KD):
                y_times_z(k)
                if k == 1:
                    x_times_dt(NCH)
                    x_to_end(NCH)
                    dve.wait_ge(sem("cb"), 3)
                    dve.tensor_tensor(cbm_s, misc[0:SMP, 3, 0:2 * SMP].rearrange("p (g i) -> p g i", g=2),
                                      mask_s[:, 0].unsqueeze(1).to_broadcast([SMP, 2, SMP]), ALU.mult)\
                        .then_inc(sem("cbm"), 1)
                    dve.wait_ge(sem("cbm"), 3)
                    dve.wait_ge(sem("bnat"), NCH + 1)
                    link(dve.tensor_tensor(b_stack[64:96], misc[0:SMP, 2, 0:2 * STATE], b_stack[0:32].bitcast(F32),
                                           ALU.subtract))
                    b_masked(0)
                if k == 2:
                    sample_decays()
                    dve.wait_ge(sem("xw_hi"), 1)
                    dve.tensor_tensor(xw_stack[32:64], xw_s, xw_stack[0:32].bitcast(F32), ALU.subtract)\
                        .then_inc(sem("xw_split"), 1)
                for b in sample_groups()[k]:
                    new_state(b)
            dve.wait_ge(sem("s_off"), NB)
            dve.wait_ge(sem("s_exp"), 2)
            dve.wait_ge(sem("s_diag"), 1)
            ys = T(4, KD * SMP)
            for r in range(2):
                rows = slice(r * HD, (r + 1) * HD)
                ins_ = dve.tensor_tensor(ys[rows].rearrange("p (j i) -> p j i", j=KD),
                                         misc[rows, 2, 0:KD * SMP].rearrange("p (j i) -> p j i", j=KD),
                                         temps[rows, 5, 0:512].rearrange("p (j r i) -> p j r i", j=KD, r=2)[:, :, r],
                                         ALU.mult)
            link(ins_)
            link(dve.tensor_tensor(ys, ys, misc[:, 2, 256:256 + KD * SMP], ALU.add))
            for j in range(KD):
                ins_ = dve.scalar_tensor_tensor(out=xbc[:, j, SEQ:TOK], in0=xbc[:, j, SEQ:TOK],
                                                scalar=param("ssm_d", j), in1=ys[:, j * SMP:(j + 1) * SMP],
                                                op0=ALU.mult, op1=ALU.add)
            link(ins_)
            y_s = xbc[:, 0:KD, SEQ:TOK]
            link(dve.tensor_tensor(y_s, y_s, z_s, ALU.mult))
            link(dve.tensor_tensor(ys.rearrange("p (j i) -> p j i", j=KD), y_s, y_s, ALU.mult))
            for n in (4, 2, 1):
                dst = ys[:, 0:n * SMP] if n > 1 else temps[:, 2, SEQ:TOK]
                ins_ = dve.tensor_tensor(dst, ys[:, 0:n * SMP], ys[:, n * SMP:2 * n * SMP], ALU.add)
                if n > 1:
                    link(ins_)
            ins_.then_inc(sem("yz_sq"), 1)

            def sum_squares(j, last, done):
                dst = T(5) if j == 0 else T(4)
                link(dve.tensor_tensor(dst, xbc[:, j], xbc[:, j], ALU.mult))
                if j:
                    ins_ = dve.tensor_tensor(T(5), T(5), T(4), ALU.add)
                    if last:
                        ins_.then_inc(done, 1)
                    else:
                        link(ins_)
            rstd("ns")

            dve.wait_ge(sem("stored_h"), 16)
            operand("ssm", KD, scaled("ssm_g"), norm_block, parts_of(ssm_at))

            for j in range(KD):
                dve.wait_ge(sem("mx_hi"), j + 1)
                dve.tensor_tensor(branch[:, mixed_at(j)[1]], mixed[:, j], branch[:, mixed_at(j)[0]].bitcast(F32),
                                  ALU.subtract).then_inc(sem("mx_lo"), 1)
            p = ph["WO"]
            for j in range(KD):
                a = j % 2
                dve.wait_ge(sem(f"x_landed{j}"), 32)
                dve.wait_ge(acc_full[a], p.pair0 + j // 2 + 1)
                dve.tensor_tensor(halves(xbc[:, j]), acc(a), halves(xbc[:, j]), ALU.add).then_inc(acc_free[a], 1)
                dve.wait_ge(acc_free[a], p.pair0 + j // 2 + 1)
                sum_squares(j, j == KD - 1, sem("x2_sq"))
            rstd("n2")
            operand("n2", KD, scaled("norm2_g"), norm_block, h_parts)

            n_out = SEQ + NB * (FKW - 1 + TS)

            def up(name, f0):
                p = ph[name]

                def quad(i):
                    for r in range(2):
                        f = i * 2 + (f0 + r)
                        pair = p.pair(i, 2 * r)
                        dve.wait_ge(acc_free[0], pair + 1)
                        dve.wait_ge(sem("f_hist"), f + 1)
                        cv = T(2 + r, n_out)
                        for t in range(FKW):
                            src, w = temps[:, r, t:t + n_out], param("ffn_w", i * (2 * FKW) + ((f0 + r) * FKW + t))
                            if t == 0:
                                dve.tensor_scalar(cv, src, w, None, ALU.mult).then_inc(sem("f_conv"), 1)
                            else:
                                dve.wait_ge(sem("f_conv"), i * (2 * FKW) + ((f0 + r) * FKW + t))
                                dve.scalar_tensor_tensor(out=cv, in0=src, scalar=w, in1=cv, op0=ALU.mult, op1=ALU.add)\
                                    .then_inc(sem("f_conv"), 1)
                        dve.wait_ge(sem("f_silu"), f + 1)
                        dve.wait_ge(acc_full[1], pair + 1)
                        prod = T(4 + r)
                        for src, sil, dst in zip(acc_pieces(1), conv_pieces(temps[:, 2 + r], FKW),
                                                 [prod[:, 0:HALF], prod[:, HALF:SEQ],
                                                  prod[:, SEQ:TOK].rearrange("p (b t) -> p b t", b=NB)]):
                            ins_ = dve.tensor_tensor(dst, src, sil, ALU.mult)
                        ins_.then_inc(acc_free[1], 1)
                        dve.wait_ge(sem("f_hi"), f + 1)
                        dve.tensor_tensor(pick(branch, i * 2 + (12 + r)), prod, pick(branch, i * 2 + r).bitcast(F32),
                                          ALU.subtract).then_inc(sem("f_lo"), 1)
                loop(dve, 0, p.quads, quad)

            def down(name, squares):
                p = ph[name]
                for j in range(KD):
                    a = j % 2
                    dve.wait_ge(acc_full[a], p.pair0 + j // 2 + 1)
                    dve.tensor_tensor(halves(xbc[:, j]), acc(a), halves(xbc[:, j]), ALU.add).then_inc(acc_free[a], 1)
                    if squares:
                        dve.wait_ge(acc_free[a], p.pair0 + j // 2 + 1)
                        sum_squares(j, j == KD - 1, sem("x3_sq"))
            dve.wait_ge(sem("zeros_f"), 1)
            up("U1", 0)
            down("D1", False)
            up("U2", FFA)
            down("D2", True)
            rstd("nf")
            for j in range(KD):
                dve.scalar_tensor_tensor(out=halves(xbc[:, j]), in0=halves(xbc[:, j]), scalar=param("final_g", j),
                                         in1=stat, op0=ALU.mult, op1=ALU.mult).then_inc(sem("y_done"), 1)
    return nc


def tiles(w, rows=None):
    k, n = w.shape
    return np.ascontiguousarray(w.reshape(k // P, P, n // P, P).transpose(2, 1, 0, 3).reshape(n // P, P, k))


def channels(a):
    lead = a.shape[:-1]
    v = a.reshape(*lead, a.shape[-1] // P, P)
    return np.ascontiguousarray(np.moveaxis(np.moveaxis(v, -1, 0), -1, 1))


def kernel(**inputs):
    import concourse.bacc as bacc
    from concourse.bass_utils import run_bass_kernel_spmd

    a = {k: np.asarray(v) for k, v in inputs.items()}
    o3, o4 = 2 * CONF + D, 2 * CONF + D + XBC
    o5 = o4 + HEADS
    win = a["w_in"][0]
    t_a1, t_a2 = tiles(win[:, 0:CONF]), tiles(win[:, CONF:2 * CONF])
    t_u, t_v = tiles(win[:, o5:o5 + CONF]), tiles(win[:, o5 + CONF:o5 + 2 * CONF])
    glu = np.stack([t_a2, t_a1], 1).reshape(8, P, D)
    up = tiles(a["ffn_w_up"][0])
    down = a["ffn_w_down"][0]

    def halves_of(w):
        t = tiles(w)
        return np.ascontiguousarray(t.reshape(KD, P, 2, w.shape[0] // 2).transpose(0, 2, 1, 3)
                                    .reshape(2 * KD, P, w.shape[0] // 2))
    cols = {
        "norm1_g": channels(a["norm1_g"][0]), "b_gate": channels(a["b_gate"][0]),
        "conf_w": channels(a["conf_conv_w"][0]), "conf_b": channels(a["conf_conv_b"][0]),
        "conf_ln_g": channels(a["conf_ln_g"][0]), "conf_ln_b": channels(a["conf_ln_b"][0]),
        "ssm_w": channels(a["ssm_conv_w"][0]), "ssm_b": channels(a["ssm_conv_b"][0]),
        "ssm_g": channels(a["ssm_norm_g"][0]), "ssm_d": channels(np.repeat(a["ssm_d"][0], HD)),
        "gmlp_ln_g": channels(a["gmlp_ln_g"][0]), "gmlp_ln_b": channels(a["gmlp_ln_b"][0]),
        "norm2_g": channels(a["norm2_g"][0]), "ffn_w": channels(a["ffn_conv_w"][0]),
        "ffn_b": channels(a["ffn_conv_b"][0]), "final_g": channels(a["final_norm_g"]),
    }
    i = np.arange(P)
    j = np.arange(SMP)
    same = (j[:, None] // TS) == (j[None, :] // TS)
    f32 = np.float32
    arrays = {
        "x": channels(np.concatenate([a["x_prompt"][0], a["x_sample"].reshape(SMP, D)], 0)),
        "consts": np.stack([np.eye(P), i[:, None] <= i[None, :], np.ones((P, P))], 1).astype(f32),
        "sample_of": (np.arange(96)[:, None] % SMP // TS == np.arange(NB)[None, :]).astype(f32),
        "heads": (np.arange(64)[:, None] % 32 == np.arange(HEADS)[None, :]).astype(f32),
        "mask_s": np.stack([same & (j[:, None] <= j[None, :]), same], 1).astype(f32),
        "params": np.concatenate([cols[n].reshape(P, -1) for n, _ in PARAM_BLOCKS], 1),
        "w_in_main": np.concatenate([glu, t_v, t_u, tiles(win[:, o3:o4])], 0),
        "w_in_z": tiles(win[:, 2 * CONF:o3]),
        "w_dt": np.ascontiguousarray(win[:, o4:o5].reshape(KD, P, HEADS).transpose(1, 0, 2)),
        "ssm_dt_bias": a["ssm_dt_bias"][0], "ssm_a_log": a["ssm_a_log"][0],
        "w_gate": tiles(a["w_gate"][0]),
        "conf_w_out": tiles(a["conf_w_out"][0]), "ssm_w_out": tiles(a["ssm_w_out"][0]),
        "gmlp_w_out": tiles(a["gmlp_w_out"][0]), "w_o": tiles(a["w_o"][0]),
        "ffn_w_up": np.stack([up[0:NF], up[NF:]], 1).reshape(2 * NF, P, D),
        "ffn_w_down1": halves_of(down[0:FFA * P]), "ffn_w_down2": halves_of(down[FFA * P:]),
        "gmlp_w_s": np.ascontiguousarray(a["gmlp_w_s"][0].transpose(2, 0, 1)),
        "gmlp_b_s": a["gmlp_b_s"][0].reshape(-1),
        "state_conv_a": channels(a["state_conv_a"][0]),
        "state_conv_ssm": channels(a["state_conv_ssm"][0]),
        "state_conv_ffn": channels(a["state_conv_ffn"][0]),
        "state_ssm": np.ascontiguousarray(a["state_ssm"][0].transpose(0, 3, 1, 2).reshape(NB, STATE, D)),
    }
    arrays = {k: np.ascontiguousarray(v) for k, v in arrays.items()}
    shapes = {
        "y": (P, KD, TOK), "conv_a_p": (P, 4, CKW - 1), "conv_a_s": (P, 4, NB, CKW - 1),
        "conv_ssm": (P, 12, (NB + 1) * (SKW - 1)), "conv_ffn": (P, NF, (NB + 1) * (FKW - 1)),
        "ssm_p": (STATE, D), "ssm_s": (NB, STATE, D), "gmlp_v_s": (P, 4, SMP),
    }
    nc = bacc.Bacc("TRN2", target_bir_lowering=False, num_devices=1, dynamic_dma_scratch_size=1024)
    ins = {k: nc.dram_tensor(f"in_{k}", v.shape, F32, kind="ExternalInput").ap() for k, v in arrays.items()}
    outs = {k: nc.dram_tensor(f"out_{k}", v, F32, kind="ExternalOutput").ap() for k, v in shapes.items()}
    build(nc, ins, outs)
    r = run_bass_kernel_spmd(nc, [{f"in_{k}": v for k, v in arrays.items()}], core_ids=[0])
    got = {k: np.asarray(r.results[0][f"out_{k}"]) for k in shapes}

    def rows(t):
        v = np.moveaxis(np.moveaxis(t, 0, -1), 0, -2)
        return v.reshape(*v.shape[:-2], -1)

    y = rows(got["y"])
    n, m = SKW - 1, FKW - 1
    conv_ssm, conv_ffn = rows(got["conv_ssm"]), rows(got["conv_ffn"])

    def state(t):
        return t.reshape(*t.shape[:-2], STATE, HEADS, HD).transpose(0, 2, 3, 1)
    out = (
        y[0:SEQ][None], y[SEQ:].reshape(NB, TS, D), rows(got["conv_a_p"])[None, None],
        state(got["ssm_p"][None])[None], conv_ssm[0:n][None, None], conv_ffn[0:m][None, None],
        rows(got["conv_a_s"])[None], state(got["ssm_s"])[None],
        conv_ssm[n:].reshape(NB, n, XBC)[None], conv_ffn[m:].reshape(NB, m, FF)[None],
        rows(got["gmlp_v_s"]).reshape(NB, TS, CONF)[None],
    )
    return tuple(np.ascontiguousarray(o) for o in out)
```
